# Optimizing a Trainium2 kernel written in Bass

```python
import math
import jax
import jax.numpy as jnp
from jax import lax
import numpy as np
import jax, jax.numpy as jnp

D_MODEL = 1024
BATCH = 1
SEQ = 256
DEPTH = 2

GRID_W = 64
CTX_LEN = 256
HEAD_DIM = 64
Q_BLOCK = 128
D_FF = 2816
N_MOD = 9
ROPE_BASE = 10000.0
EPS = 1e-6
NEG = -1e30
A_HEADS = 8
A_KV_HEADS = 2
A_WINDOW = 128
B_HEADS = 4
B_V_DIM = 2 * HEAD_DIM
C_HEADS = 8
C_Q_RANK = 768
C_KV_RANK = 256
C_NOPE = 64
C_ROPE = 32
C_V = 64
D_HEADS = 8
D_WIN_ROWS = 8
D_WIN_COLS = 16
N_EVEN = (DEPTH + 1) // 2
N_ODD = DEPTH // 2
AB_SPLITS = (A_HEADS * HEAD_DIM, B_HEADS * 2 * HEAD_DIM, A_KV_HEADS * HEAD_DIM, A_KV_HEADS * HEAD_DIM, B_HEADS * 2 * HEAD_DIM, B_HEADS * B_V_DIM)
AB_Q_WIDTH = AB_SPLITS[0] + AB_SPLITS[1]
AB_IN = sum(AB_SPLITS)
AB_OUT = A_HEADS * HEAD_DIM + B_HEADS * B_V_DIM
CD_SPLITS = (C_Q_RANK, D_HEADS * HEAD_DIM, C_KV_RANK + C_ROPE, D_HEADS * HEAD_DIM, D_HEADS * HEAD_DIM)
CD_Q_WIDTH = CD_SPLITS[0] + CD_SPLITS[1]
CD_IN = sum(CD_SPLITS)
CD_OUT = C_HEADS * C_V + D_HEADS * HEAD_DIM


def split_cols(t, sizes):
    cuts = [int(v) for v in np.cumsum(sizes)[:-1]]
    return jnp.split(t, cuts, axis=-1)

def rms_norm(x, gain=None):
    xf = x.astype(jnp.float32)
    y = xf * lax.rsqrt(jnp.mean(xf * xf, axis=-1, keepdims=True) + EPS)
    if gain is not None:
        y = y * gain.astype(jnp.float32)
    return y.astype(x.dtype)

def modulate(h, shift, scale):
    return h * (1.0 + scale) + shift

def swiglu(h, w_gate, w_up, w_down):
    return (jax.nn.silu(h @ w_gate) * (h @ w_up)) @ w_down

def axial_rope_tables(n, rot_dim):
    nf = rot_dim // 4
    inv = ROPE_BASE ** (-jnp.arange(nf, dtype=jnp.float32) / nf)
    t = jnp.arange(n)
    row = (t // GRID_W).astype(jnp.float32)
    col = (t % GRID_W).astype(jnp.float32)
    ang = jnp.concatenate([row[:, None] * inv, col[:, None] * inv], axis=-1)
    return jnp.cos(ang), jnp.sin(ang)

def apply_rope2d(x, cos, sin):
    nf = x.shape[-1] // 4
    xf = x.astype(jnp.float32).reshape(x.shape[:-1] + (2, 2, nf))
    x1, x2 = xf[..., 0, :], xf[..., 1, :]
    c = cos.reshape(cos.shape[0], 1, 2, nf)
    s = sin.reshape(sin.shape[0], 1, 2, nf)
    out = jnp.stack([x1 * c - x2 * s, x2 * c + x1 * s], axis=-2)
    return out.reshape(x.shape).astype(x.dtype)

def joint_softmax(scores, sink=None):
    m = scores[0].max(axis=-1, keepdims=True)
    for s in scores[1:]:
        m = jnp.maximum(m, s.max(axis=-1, keepdims=True))
    if sink is not None:
        m = jnp.maximum(m, sink)
    es = [jnp.exp(s - m) for s in scores]
    denom = es[0].sum(axis=-1, keepdims=True)
    for e in es[1:]:
        denom = denom + e.sum(axis=-1, keepdims=True)
    if sink is not None:
        denom = denom + jnp.exp(sink - m)
    return [e / denom for e in es]

def sweep_blocks(fn, q, block):
    B, S = q.shape[0], q.shape[1]
    nb = S // block
    qb = jnp.moveaxis(q.reshape((B, nb, block) + q.shape[2:]), 1, 0)
    out = lax.map(lambda a: fn(a[0], a[1]), (qb, jnp.arange(nb)))
    return jnp.moveaxis(out, 0, 1).reshape((B, S) + out.shape[3:])

def gqa_attend(q, keyvals, sink=None):
    B, Q, H, d = q.shape
    kvh = keyvals[0][0].shape[2]
    g = H // kvh
    qg = q.reshape(B, Q, kvh, g, d)
    scores = []
    for k, _, mask in keyvals:
        s = jnp.einsum('bqhgd,bkhd->bhgqk', qg, k).astype(jnp.float32) * (d ** -0.5)
        if mask is not None:
            s = jnp.where(mask, s, NEG)
        scores.append(s)
    sink_b = None if sink is None else sink.astype(jnp.float32).reshape(kvh, g, 1, 1)
    probs = joint_softmax(scores, sink_b)
    out = None
    for p, (_, v, _) in zip(probs, keyvals):
        o = jnp.einsum('bhgqk,bkhd->bqhgd', p.astype(v.dtype), v)
        out = o if out is None else out + o
    return out.reshape(B, Q, H, d)

def windowed_sink_attention(q, k, v, k_ctx, v_ctx, sink):
    S = q.shape[1]
    span = Q_BLOCK + 2 * A_WINDOW
    pad = ((0, 0), (A_WINDOW, A_WINDOW), (0, 0), (0, 0))
    k_pad = jnp.pad(k, pad)
    v_pad = jnp.pad(v, pad)

    def block(q_blk, n):
        start = n * Q_BLOCK
        k_blk = lax.dynamic_slice_in_dim(k_pad, start, span, axis=1)
        v_blk = lax.dynamic_slice_in_dim(v_pad, start, span, axis=1)
        q_pos = start + jnp.arange(Q_BLOCK)
        k_pos = start - A_WINDOW + jnp.arange(span)
        mask = ((jnp.abs(q_pos[:, None] - k_pos[None, :]) <= A_WINDOW)
                & (k_pos >= 0)[None, :] & (k_pos < S)[None, :])
        return gqa_attend(q_blk, [(k_blk, v_blk, mask), (k_ctx, v_ctx, None)], sink)

    return sweep_blocks(block, q, Q_BLOCK)

def diff_lambda(lq1, lk1, lq2, lk2, lam_init):
    f = jnp.float32
    return (jnp.exp(jnp.sum(lq1.astype(f) * lk1.astype(f)))
            - jnp.exp(jnp.sum(lq2.astype(f) * lk2.astype(f))) + lam_init)

def diff_qk(t, gain, rope):
    B, n, _ = t.shape
    t = rms_norm(t.reshape(B, n, 2 * B_HEADS, HEAD_DIM), gain)
    if rope is not None:
        t = apply_rope2d(t, *rope)
    return t.reshape(B, n, B_HEADS, 2, HEAD_DIM)

def diff_attend(q, k, v, lam):
    s = jnp.einsum('bqhmd,bkhmd->bhmqk', q, k).astype(jnp.float32) * (HEAD_DIM ** -0.5)
    p = jax.nn.softmax(s, axis=-1)
    w = p[:, :, 0] - lam * p[:, :, 1]
    return jnp.einsum('bhqk,bkhe->bqhe', w.astype(v.dtype), v)

def mla_queries(dq, q_a_norm, w_uq, qn_nope, qn_rope, rope):
    B, n, _ = dq.shape
    q = (rms_norm(dq, q_a_norm) @ w_uq).reshape(B, n, C_HEADS, C_NOPE + C_ROPE)
    q_nope = rms_norm(q[..., :C_NOPE], qn_nope)
    q_rope = rms_norm(q[..., C_NOPE:], qn_rope)
    if rope is not None:
        q_rope = apply_rope2d(q_rope, *rope)
    return jnp.concatenate([q_nope, q_rope], axis=-1)

def mla_keys_values(dkv, kv_a_norm, w_ukv, kn_nope, kn_rope, rope):
    B, n, _ = dkv.shape
    c_kv, k_rope = dkv[..., :C_KV_RANK], dkv[..., C_KV_RANK:]
    kv = (rms_norm(c_kv, kv_a_norm) @ w_ukv).reshape(B, n, C_HEADS, C_NOPE + C_V)
    k_nope = rms_norm(kv[..., :C_NOPE], kn_nope)
    k_rope = rms_norm(k_rope, kn_rope)[:, :, None, :]
    if rope is not None:
        k_rope = apply_rope2d(k_rope, *rope)
    return k_nope, k_rope[:, :, 0, :], kv[..., C_NOPE:]

def mla_attend(q, k_nope, k_rope, v):
    q_nope, q_rope = q[..., :C_NOPE], q[..., C_NOPE:]
    s = (jnp.einsum('bqhd,bkhd->bhqk', q_nope, k_nope)
         + jnp.einsum('bqhr,bkr->bhqk', q_rope, k_rope)).astype(jnp.float32) * ((C_NOPE + C_ROPE) ** -0.5)
    p = jax.nn.softmax(s, axis=-1)
    return jnp.einsum('bhqk,bkhd->bqhd', p.astype(v.dtype), v)

def neighbourhood_attention(q, k, v, k_ctx, v_ctx, rpb):
    B, S, H, d = q.shape
    rows = S // GRID_W
    kh = min(D_WIN_ROWS, rows)
    kw = D_WIN_COLS
    k_grid = k.reshape(B, rows, GRID_W, H, d)
    v_grid = v.reshape(B, rows, GRID_W, H, d)
    cols = jnp.arange(GRID_W)
    col_start = jnp.clip(cols - kw // 2, 0, GRID_W - kw)
    col_mask = (cols[None, :] >= col_start[:, None]) & (cols[None, :] < col_start[:, None] + kw)
    dc_idx = jnp.clip(cols[None, :] - cols[:, None], -(kw - 1), kw - 1) + (D_WIN_COLS - 1)
    scale = d ** -0.5
    rpb_f = rpb.astype(jnp.float32)

    def row_block(q_row, r):
        row_start = jnp.clip(r - kh // 2, 0, rows - kh)
        k_band = lax.dynamic_slice_in_dim(k_grid, row_start, kh, axis=1)
        v_band = lax.dynamic_slice_in_dim(v_grid, row_start, kh, axis=1)
        dr_idx = row_start + jnp.arange(kh) - r + (D_WIN_ROWS - 1)
        bias = rpb_f[:, dr_idx[None, :, None], dc_idx[:, None, :]]
        s = jnp.einsum('bqhd,bjkhd->bhqjk', q_row, k_band).astype(jnp.float32) * scale + bias
        s = jnp.where(col_mask[:, None, :], s, NEG).reshape(B, H, GRID_W, kh * GRID_W)
        s_ctx = jnp.einsum('bqhd,bchd->bhqc', q_row, k_ctx).astype(jnp.float32) * scale
        p, p_ctx = joint_softmax([s, s_ctx])
        p = p.reshape(B, H, GRID_W, kh, GRID_W).astype(v.dtype)
        return (jnp.einsum('bhqjk,bjkhd->bqhd', p, v_band)
                + jnp.einsum('bhqc,bchd->bqhd', p_ctx.astype(v.dtype), v_ctx))

    return sweep_blocks(row_block, q, GRID_W)

def mix_window_diff(h, hc, w_in, w_out, a_q_norm, a_k_norm, a_sink, b_q_norm, b_k_norm,
                    b_lq1, b_lk1, b_lq2, b_lk2, b_sub_norm, lam_init, rope, need_ctx):
    B, S, _ = h.shape
    L = hc.shape[1]
    aq, bq, ak, av, bk, bv = split_cols(h @ w_in, AB_SPLITS)
    ak_c, av_c, bk_c, bv_c = split_cols(hc @ w_in[:, AB_Q_WIDTH:], AB_SPLITS[2:])
    aq = apply_rope2d(rms_norm(aq.reshape(B, S, A_HEADS, HEAD_DIM), a_q_norm), *rope)
    ak = apply_rope2d(rms_norm(ak.reshape(B, S, A_KV_HEADS, HEAD_DIM), a_k_norm), *rope)
    av = av.reshape(B, S, A_KV_HEADS, HEAD_DIM)
    ak_c = rms_norm(ak_c.reshape(B, L, A_KV_HEADS, HEAD_DIM), a_k_norm)
    av_c = av_c.reshape(B, L, A_KV_HEADS, HEAD_DIM)
    y_a = windowed_sink_attention(aq, ak, av, ak_c, av_c, a_sink)
    lam = diff_lambda(b_lq1, b_lk1, b_lq2, b_lk2, lam_init)
    bq = diff_qk(bq, b_q_norm, rope)
    bk = diff_qk(bk, b_k_norm, rope)
    bv = bv.reshape(B, S, B_HEADS, B_V_DIM)
    bk_c = diff_qk(bk_c, b_k_norm, None)
    bv_c = bv_c.reshape(B, L, B_HEADS, B_V_DIM)
    k_all = jnp.concatenate([bk_c, bk], axis=1)
    v_all = jnp.concatenate([bv_c, bv], axis=1)
    y_b = sweep_blocks(lambda q_blk, n: diff_attend(q_blk, k_all, v_all, lam), bq, Q_BLOCK)
    y_b = rms_norm(y_b, b_sub_norm) * (1.0 - lam_init)
    y = jnp.concatenate([y_a.reshape(B, S, -1), y_b.reshape(B, S, -1)], axis=-1) @ w_out
    if not need_ctx:
        return y, None
    aq_c, bq_c = split_cols(hc @ w_in[:, :AB_Q_WIDTH], AB_SPLITS[:2])
    aq_c = rms_norm(aq_c.reshape(B, L, A_HEADS, HEAD_DIM), a_q_norm)
    y_a_c = gqa_attend(aq_c, [(ak_c, av_c, None)], a_sink)
    y_b_c = rms_norm(diff_attend(diff_qk(bq_c, b_q_norm, None), bk_c, bv_c, lam), b_sub_norm) * (1.0 - lam_init)
    y_c = jnp.concatenate([y_a_c.reshape(B, L, -1), y_b_c.reshape(B, L, -1)], axis=-1) @ w_out
    return y, y_c

def mix_mla_neighbourhood(h, hc, w_in, w_out, c_q_a_norm, c_kv_a_norm, c_w_uq, c_w_ukv,
                          c_q_nope_norm, c_q_rope_norm, c_k_nope_norm, c_k_rope_norm,
                          d_q_norm, d_k_norm, d_rpb, rope, need_ctx):
    B, S, _ = h.shape
    L = hc.shape[1]
    cq, dq, ckv, dk, dv = split_cols(h @ w_in, CD_SPLITS)
    ckv_c, dk_c, dv_c = split_cols(hc @ w_in[:, CD_Q_WIDTH:], CD_SPLITS[2:])
    q = mla_queries(cq, c_q_a_norm, c_w_uq, c_q_nope_norm, c_q_rope_norm, rope)
    kn, kr, v = mla_keys_values(ckv, c_kv_a_norm, c_w_ukv, c_k_nope_norm, c_k_rope_norm, rope)
    kn_c, kr_c, v_c = mla_keys_values(ckv_c, c_kv_a_norm, c_w_ukv, c_k_nope_norm, c_k_rope_norm, None)
    kn_all = jnp.concatenate([kn_c, kn], axis=1)
    kr_all = jnp.concatenate([kr_c, kr], axis=1)
    v_all = jnp.concatenate([v_c, v], axis=1)
    y_mla = sweep_blocks(lambda q_blk, n: mla_attend(q_blk, kn_all, kr_all, v_all), q, Q_BLOCK)
    dq = rms_norm(dq.reshape(B, S, D_HEADS, HEAD_DIM), d_q_norm)
    dk = rms_norm(dk.reshape(B, S, D_HEADS, HEAD_DIM), d_k_norm)
    dv = dv.reshape(B, S, D_HEADS, HEAD_DIM)
    dk_c = rms_norm(dk_c.reshape(B, L, D_HEADS, HEAD_DIM), d_k_norm)
    dv_c = dv_c.reshape(B, L, D_HEADS, HEAD_DIM)
    y_nat = neighbourhood_attention(dq, dk, dv, dk_c, dv_c, d_rpb)
    y = jnp.concatenate([y_mla.reshape(B, S, -1), y_nat.reshape(B, S, -1)], axis=-1) @ w_out
    if not need_ctx:
        return y, None
    cq_c, dq_c = split_cols(hc @ w_in[:, :CD_Q_WIDTH], CD_SPLITS[:2])
    y_mla_c = mla_attend(mla_queries(cq_c, c_q_a_norm, c_w_uq, c_q_nope_norm, c_q_rope_norm, None), kn_c, kr_c, v_c)
    y_nat_c = gqa_attend(rms_norm(dq_c.reshape(B, L, D_HEADS, HEAD_DIM), d_q_norm), [(dk_c, dv_c, None)])
    y_c = jnp.concatenate([y_mla_c.reshape(B, L, -1), y_nat_c.reshape(B, L, -1)], axis=-1) @ w_out
    return y, y_c

def first_inputs(seed: int = 0) -> dict:
    key = jax.random.key(seed)
    ks = jax.random.split(key, 37)
    f32 = jnp.float32

    def nrm(i, shape, scale):
        return scale * jax.random.normal(ks[i], shape, f32)

    def gain(i, shape):
        return 1.0 + 0.05 * jax.random.normal(ks[i], shape, f32)

    D, F, NE, NO = D_MODEL, D_FF, N_EVEN, N_ODD
    return {
        "x": nrm(0, (BATCH, SEQ, D), 1.0),
        "c": nrm(1, (BATCH, D), 1.0),
        "ctx": nrm(2, (BATCH, CTX_LEN, D), 1.0),
        "c_ctx": nrm(3, (D,), 1.0),
        "w_mod": nrm(4, (DEPTH, D, N_MOD * D), 0.5 * D ** -0.5),
        "b_mod": nrm(5, (DEPTH, N_MOD * D), 0.02),
        "ffn1_w_gate": nrm(6, (DEPTH, D, F), D ** -0.5),
        "ffn1_w_up": nrm(7, (DEPTH, D, F), D ** -0.5),
        "ffn1_w_down": nrm(8, (DEPTH, F, D), F ** -0.5),
        "ffn2_w_gate": nrm(9, (DEPTH, D, F), D ** -0.5),
        "ffn2_w_up": nrm(10, (DEPTH, D, F), D ** -0.5),
        "ffn2_w_down": nrm(11, (DEPTH, F, D), F ** -0.5),
        "ab_w_in": nrm(12, (NE, D, AB_IN), D ** -0.5),
        "ab_w_out": nrm(13, (NE, AB_OUT, D), AB_OUT ** -0.5),
        "a_q_norm": gain(14, (NE, HEAD_DIM)),
        "a_k_norm": gain(15, (NE, HEAD_DIM)),
        "a_sink": nrm(16, (NE, A_HEADS), 0.5),
        "b_q_norm": gain(17, (NE, HEAD_DIM)),
        "b_k_norm": gain(18, (NE, HEAD_DIM)),
        "b_lambda_q1": nrm(19, (NE, HEAD_DIM), 0.1),
        "b_lambda_k1": nrm(20, (NE, HEAD_DIM), 0.1),
        "b_lambda_q2": nrm(21, (NE, HEAD_DIM), 0.1),
        "b_lambda_k2": nrm(22, (NE, HEAD_DIM), 0.1),
        "b_sub_norm": gain(23, (NE, B_V_DIM)),
        "cd_w_in": nrm(24, (NO, D, CD_IN), D ** -0.5),
        "cd_w_out": nrm(25, (NO, CD_OUT, D), CD_OUT ** -0.5),
        "c_q_a_norm": gain(26, (NO, C_Q_RANK)),
        "c_kv_a_norm": gain(27, (NO, C_KV_RANK)),
        "c_w_uq": nrm(28, (NO, C_Q_RANK, C_HEADS * (C_NOPE + C_ROPE)), C_Q_RANK ** -0.5),
        "c_w_ukv": nrm(29, (NO, C_KV_RANK, C_HEADS * (C_NOPE + C_V)), C_KV_RANK ** -0.5),
        "c_q_nope_norm": gain(30, (NO, C_NOPE)),
        "c_q_rope_norm": gain(31, (NO, C_ROPE)),
        "c_k_nope_norm": gain(32, (NO, C_NOPE)),
        "c_k_rope_norm": gain(33, (NO, C_ROPE)),
        "d_q_norm": gain(34, (NO, HEAD_DIM)),
        "d_k_norm": gain(35, (NO, HEAD_DIM)),
        "d_rpb": nrm(36, (NO, D_HEADS, 2 * D_WIN_ROWS - 1, 2 * D_WIN_COLS - 1), 0.5),
    }

def first_block(x, c, ctx, c_ctx, w_mod, b_mod,
              ffn1_w_gate, ffn1_w_up, ffn1_w_down, ffn2_w_gate, ffn2_w_up, ffn2_w_down,
              ab_w_in, ab_w_out, a_q_norm, a_k_norm, a_sink, b_q_norm, b_k_norm,
              b_lambda_q1, b_lambda_k1, b_lambda_q2, b_lambda_k2, b_sub_norm,
              cd_w_in, cd_w_out, c_q_a_norm, c_kv_a_norm, c_w_uq, c_w_ukv,
              c_q_nope_norm, c_q_rope_norm, c_k_nope_norm, c_k_rope_norm,
              d_q_norm, d_k_norm, d_rpb):
    S = x.shape[1]
    rope_head = axial_rope_tables(S, HEAD_DIM)
    rope_mla = axial_rope_tables(S, C_ROPE)
    c_act = jax.nn.silu(c)
    c_ctx_act = jax.nn.silu(c_ctx)
    xc = ctx
    for l in range(DEPTH):
        need_ctx = l < DEPTH - 1
        mx = jnp.split((c_act @ w_mod[l] + b_mod[l])[:, None, :], N_MOD, axis=-1)
        mc = jnp.split((c_ctx_act @ w_mod[l] + b_mod[l])[None, None, :], N_MOD, axis=-1)
        ffn1 = (ffn1_w_gate[l], ffn1_w_up[l], ffn1_w_down[l])
        ffn2 = (ffn2_w_gate[l], ffn2_w_up[l], ffn2_w_down[l])
        x = x + 0.5 * mx[2] * swiglu(modulate(rms_norm(x), mx[0], mx[1]), *ffn1)
        xc = xc + 0.5 * mc[2] * swiglu(modulate(rms_norm(xc), mc[0], mc[1]), *ffn1)
        h = modulate(rms_norm(x), mx[3], mx[4])
        hc = modulate(rms_norm(xc), mc[3], mc[4])
        i = l // 2
        if l % 2 == 0:
            lam_init = 0.8 - 0.6 * math.exp(-0.3 * l)
            y, y_c = mix_window_diff(h, hc, ab_w_in[i], ab_w_out[i], a_q_norm[i], a_k_norm[i], a_sink[i],
                                     b_q_norm[i], b_k_norm[i], b_lambda_q1[i], b_lambda_k1[i],
                                     b_lambda_q2[i], b_lambda_k2[i], b_sub_norm[i], lam_init,
                                     rope_head, need_ctx)
        else:
            y, y_c = mix_mla_neighbourhood(h, hc, cd_w_in[i], cd_w_out[i], c_q_a_norm[i], c_kv_a_norm[i],
                                           c_w_uq[i], c_w_ukv[i], c_q_nope_norm[i], c_q_rope_norm[i],
                                           c_k_nope_norm[i], c_k_rope_norm[i], d_q_norm[i], d_k_norm[i],
                                           d_rpb[i], rope_mla, need_ctx)
        x = x + mx[5] * y
        x = x + 0.5 * mx[8] * swiglu(modulate(rms_norm(x), mx[6], mx[7]), *ffn2)
        if need_ctx:
            xc = xc + mc[5] * y_c
            xc = xc + 0.5 * mc[8] * swiglu(modulate(rms_norm(xc), mc[6], mc[7]), *ffn2)
    return x


NORM_EPS = 1e-6
D_FF_2 = 2752
A_HEADS_2 = 6
A_WIDTH = 384
A_DECAY_LORA = 32
A_AAA_LORA = 32
A_GATE_LORA = 64
A_MV_LORA = 16
A_GN_EPS = 64e-5
A_SLAB = (384, 384, 384, 32, 32, 64)
A_IN = 1280
B_HEADS_2 = 6
B_WIDTH = 384
B_KV_LATENT = 128
B_IDX_HEADS = 8
B_IDX_DIM = 64
B_TOPK_MAX = 256
B_QUERY_BLOCK = 128
B_SLAB = (384, 128, 512, 64, 8)
B_IN = 1096
C_HEADS_2 = 4
C_WIDTH = 256
C_CHUNK = 128
C_ROPE_BASE = 10000.0
C_SLAB = (256, 256, 256, 256)
C_IN = 1024
D_MIX = 1024
N_IN = 3400


def _split(p, widths):
    out, start = [], 0
    for w in widths:
        out.append(p[..., start:start + w])
        start += w
    return out

def rmsnorm(x, g, eps=NORM_EPS):
    xf = x.astype(jnp.float32)
    y = xf * lax.rsqrt(jnp.mean(xf * xf, axis=-1, keepdims=True) + eps)
    return y.astype(x.dtype) * g

def swiglu_2(h, w_gate, w_up, w_down):
    return (jax.nn.silu(h @ w_gate) * (h @ w_up)) @ w_down

def shift_lerp(p, mu):
    prev = jnp.pad(p, ((0, 0), (1, 0), (0, 0)))[:, :-1]
    return p + (prev - p) * mu

def _head_layernorm(y, eps):
    mu = jnp.mean(y, axis=-1, keepdims=True)
    var = jnp.mean(jnp.square(y - mu), axis=-1, keepdims=True)
    return (y - mu) * lax.rsqrt(var + eps)

def _rwkv7_recurrence(r, decay, k, v, a, b):
    Bsz, T, H, N = r.shape

    def step(S, inp):
        r_t, w_t, k_t, v_t, a_t, b_t = inp
        sa = jnp.einsum('bhvk,bhk->bhv', S, a_t)
        S = S * w_t[:, :, None, :] + sa[..., None] * b_t[:, :, None, :] + v_t[..., None] * k_t[:, :, None, :]
        return S, jnp.einsum('bhvk,bhk->bhv', S, r_t)

    xs = tuple(jnp.moveaxis(z, 1, 0) for z in (r, decay, k, v, a, b))
    _, y = lax.scan(step, jnp.zeros((Bsz, H, N, N), jnp.float32), xs)
    return jnp.moveaxis(y, 0, 1)

def rwkv7_mixer(r, k, v, w_lo, a_lo, g_lo, w0, w2, a0, a2, g2, k_k, k_a, r_k, ln_w, ln_b):
    Bsz, T, _ = r.shape
    dt = r.dtype
    heads = lambda z: z.astype(jnp.float32).reshape(Bsz, T, A_HEADS_2, HEAD_DIM)
    w = -jax.nn.softplus(-(w0 + jnp.tanh(w_lo) @ w2)) - 0.5
    a = jax.nn.sigmoid(a0 + a_lo @ a2)
    g = jax.nn.sigmoid(g_lo) @ g2
    kk = heads(k * k_k)
    kk = kk / jnp.maximum(jnp.linalg.norm(kk, axis=-1, keepdims=True), 1e-12)
    k = k * (1.0 + (a - 1.0) * k_a)
    decay = jnp.exp(-jnp.exp(heads(w)))
    rh, kh, vh, ah = heads(r), heads(k), heads(v), heads(a)
    y = _rwkv7_recurrence(rh, decay, kh, vh, -kk, kk * ah)
    y = _head_layernorm(y, A_GN_EPS) * ln_w.reshape(A_HEADS_2, HEAD_DIM) + ln_b.reshape(A_HEADS_2, HEAD_DIM)
    y = y + jnp.sum(rh * kh * r_k, axis=-1, keepdims=True) * vh
    return y.reshape(Bsz, T, A_WIDTH).astype(dt) * g

def dsa_mixer(q, c_kv, iq, ik, iw, kv_norm, w_uk, w_uv):
    Bsz, T, _ = q.shape
    n_keys = T
    topk = min(B_TOPK_MAX, n_keys // 4)
    nb = T // B_QUERY_BLOCK
    c = rmsnorm(c_kv, kv_norm)
    qh = q.reshape(Bsz, T, B_HEADS_2, HEAD_DIM)
    q_lat = jnp.einsum('bthd,hdc->bthc', qh, w_uk) * HEAD_DIM ** -0.5
    iqh = iq.reshape(Bsz, T, B_IDX_HEADS, B_IDX_DIM) * B_IDX_DIM ** -0.5
    iwh = iw * B_IDX_HEADS ** -0.5
    key_pos = jnp.arange(n_keys)
    blocks = lambda z: jnp.moveaxis(z.reshape((Bsz, nb, B_QUERY_BLOCK) + z.shape[2:]), 1, 0)

    def one_block(args):
        q_lat_b, iq_b, iw_b, blk = args
        q_pos = blk * B_QUERY_BLOCK + jnp.arange(B_QUERY_BLOCK)
        rel = jax.nn.relu(jnp.einsum('bqhd,bsd->bqhs', iq_b, ik))
        score = jnp.einsum('bqh,bqhs->bqs', iw_b, rel).astype(jnp.float32)
        visible = key_pos[None, :] <= q_pos[:, None]
        score = jnp.where(visible[None], score, -jnp.inf)
        _, idx = lax.top_k(score, topk)
        valid = idx <= q_pos[None, :, None]
        c_sel = jax.vmap(lambda cb, ib: cb[ib])(c, idx)
        logits = jnp.einsum('bqhc,bqkc->bqhk', q_lat_b, c_sel).astype(jnp.float32)
        logits = jnp.where(valid[:, :, None, :], logits, -jnp.inf)
        prob = jax.nn.softmax(logits, axis=-1).astype(c.dtype)
        o_lat = jnp.einsum('bqhk,bqkc->bqhc', prob, c_sel)
        return jnp.einsum('bqhc,hcd->bqhd', o_lat, w_uv)

    out = lax.map(one_block, (blocks(q_lat), blocks(iqh), blocks(iwh), jnp.arange(nb)))
    return jnp.moveaxis(out, 0, 1).reshape(Bsz, T, B_WIDTH)

def _retnet_rotate(z):
    T = z.shape[1]
    half = HEAD_DIM // 2
    theta = C_ROPE_BASE ** (-jnp.linspace(0.0, 1.0, half, dtype=jnp.float32))
    ang = jnp.arange(T, dtype=jnp.float32)[:, None] * theta[None, :]
    cos, sin = jnp.cos(ang)[None, :, None, :], jnp.sin(ang)[None, :, None, :]
    z1, z2 = z[..., :half], z[..., half:]
    return jnp.concatenate([z1 * cos - z2 * sin, z1 * sin + z2 * cos], axis=-1)

def retention_mixer(q, k, v, g):
    Bsz, T, _ = q.shape
    nc = T // C_CHUNK
    dt = q.dtype
    f32 = jnp.float32
    heads = lambda z: z.astype(f32).reshape(Bsz, T, C_HEADS_2, HEAD_DIM)
    qh = _retnet_rotate(heads(q))
    kh = _retnet_rotate(heads(k)) * HEAD_DIM ** -0.5
    vh = heads(v)
    log_gamma = jnp.log(1.0 - 2.0 ** (-5.0 - jnp.arange(C_HEADS_2, dtype=f32)))
    n = jnp.arange(C_CHUNK, dtype=f32)
    diff = n[:, None] - n[None, :]
    intra = jnp.where(diff[None] >= 0, jnp.exp(jnp.maximum(diff, 0.0)[None] * log_gamma[:, None, None]), 0.0)
    q_decay = jnp.exp((n[:, None] + 1.0) * log_gamma[None, :])
    k_decay = jnp.exp((C_CHUNK - 1.0 - n)[:, None] * log_gamma[None, :])
    chunk_decay = jnp.exp(C_CHUNK * log_gamma)
    chunks = lambda z: jnp.moveaxis(z.reshape(Bsz, nc, C_CHUNK, C_HEADS_2, HEAD_DIM), 1, 0)

    def step(state, inp):
        qc, kc, vc = inp
        scores = jnp.einsum('bnhd,bmhd->bhnm', qc, kc) * intra[None]
        inner = jnp.einsum('bhnm,bmhe->bnhe', scores, vc)
        cross = jnp.einsum('bnhd,bhde->bnhe', qc, state) * q_decay[None, :, :, None]
        state = state * chunk_decay[None, :, None, None] + jnp.einsum('bmhd,bmhe->bhde', kc * k_decay[None, :, :, None], vc)
        return state, inner + cross

    state0 = jnp.zeros((Bsz, C_HEADS_2, HEAD_DIM, HEAD_DIM), f32)
    _, y = lax.scan(step, state0, (chunks(qh), chunks(kh), chunks(vh)))
    y = jnp.moveaxis(y, 0, 1).reshape(Bsz, T, C_HEADS_2, HEAD_DIM)
    y = y * lax.rsqrt(jnp.mean(y * y, axis=-1, keepdims=True) + NORM_EPS)
    return jax.nn.silu(g) * y.reshape(Bsz, T, C_WIDTH).astype(dt)

def second_inputs(seed: int = 0) -> dict:
    key = jax.random.key(seed)
    counter = [0]

    def nk():
        counter[0] += 1
        return jax.random.fold_in(key, counter[0])

    def nrm(shape, scale):
        return jax.random.normal(nk(), shape, jnp.float32) * scale

    def gain(shape):
        return 1.0 + nrm(shape, 0.02)

    L = DEPTH
    return {
        'x': nrm((BATCH, SEQ, D_MODEL), 1.0),
        'ffn1_norm': gain((L, D_MODEL)),
        'ffn1_w_gate': nrm((L, D_MODEL, D_FF_2), D_MODEL ** -0.5),
        'ffn1_w_up': nrm((L, D_MODEL, D_FF_2), D_MODEL ** -0.5),
        'ffn1_w_down': nrm((L, D_FF_2, D_MODEL), D_FF_2 ** -0.5),
        'mix_norm': gain((L, D_MODEL)),
        'w_in': nrm((L, D_MODEL, N_IN), D_MODEL ** -0.5),
        'w_out': nrm((L, D_MIX, D_MODEL), D_MIX ** -0.5),
        'rwkv_mu': jax.random.uniform(nk(), (L, A_IN), jnp.float32),
        'rwkv_w0': jnp.linspace(-6.0, -1.0, A_WIDTH, dtype=jnp.float32)[None, :] + nrm((L, A_WIDTH), 0.1),
        'rwkv_w2': nrm((L, A_DECAY_LORA, A_WIDTH), 0.1),
        'rwkv_a0': nrm((L, A_WIDTH), 0.1),
        'rwkv_a2': nrm((L, A_AAA_LORA, A_WIDTH), 0.1),
        'rwkv_g2': nrm((L, A_GATE_LORA, A_WIDTH), A_GATE_LORA ** -0.5),
        'rwkv_k_k': 0.85 + nrm((L, A_WIDTH), 0.02),
        'rwkv_k_a': 1.0 + nrm((L, A_WIDTH), 0.02),
        'rwkv_r_k': nrm((L, A_HEADS_2, HEAD_DIM), 0.1),
        'rwkv_ln_w': gain((L, A_WIDTH)),
        'rwkv_ln_b': nrm((L, A_WIDTH), 0.01),
        'rwkv_vres_w_in': nrm((L - 1, D_MODEL, A_MV_LORA), D_MODEL ** -0.5),
        'rwkv_vres_mu': jax.random.uniform(nk(), (L - 1, A_MV_LORA), jnp.float32),
        'rwkv_v0': 0.5 + nrm((L - 1, A_WIDTH), 0.1),
        'rwkv_v2': nrm((L - 1, A_MV_LORA, A_WIDTH), 0.1),
        'dsa_kv_norm': gain((L, B_KV_LATENT)),
        'dsa_w_uk': nrm((L, B_HEADS_2, HEAD_DIM, B_KV_LATENT), B_KV_LATENT ** -0.5),
        'dsa_w_uv': nrm((L, B_HEADS_2, B_KV_LATENT, HEAD_DIM), B_KV_LATENT ** -0.5),
        'ffn2_norm': gain((L, D_MODEL)),
        'ffn2_w_gate': nrm((L, D_MODEL, D_FF_2), D_MODEL ** -0.5),
        'ffn2_w_up': nrm((L, D_MODEL, D_FF_2), D_MODEL ** -0.5),
        'ffn2_w_down': nrm((L, D_FF_2, D_MODEL), D_FF_2 ** -0.5),
        'final_norm': gain((D_MODEL,)),
    }

def second_block(x, ffn1_norm, ffn1_w_gate, ffn1_w_up, ffn1_w_down, mix_norm, w_in, w_out,
              rwkv_mu, rwkv_w0, rwkv_w2, rwkv_a0, rwkv_a2, rwkv_g2, rwkv_k_k, rwkv_k_a, rwkv_r_k,
              rwkv_ln_w, rwkv_ln_b, rwkv_vres_w_in, rwkv_vres_mu, rwkv_v0, rwkv_v2,
              dsa_kv_norm, dsa_w_uk, dsa_w_uv,
              ffn2_norm, ffn2_w_gate, ffn2_w_up, ffn2_w_down, final_norm):
    v_first = None
    for l in range(DEPTH):
        x = x + 0.5 * swiglu_2(rmsnorm(x, ffn1_norm[l]), ffn1_w_gate[l], ffn1_w_up[l], ffn1_w_down[l])
        h = rmsnorm(x, mix_norm[l])
        if l == 0:
            p_a, p_b, p_c = _split(h @ w_in[l], (A_IN, B_IN, C_IN))
        else:
            w_comb = jnp.concatenate([w_in[l], rwkv_vres_w_in[l - 1]], axis=1)
            p_a, p_b, p_c, p_mv = _split(h @ w_comb, (A_IN, B_IN, C_IN, A_MV_LORA))
        r, k, v, w_lo, a_lo, g_lo = _split(shift_lerp(p_a, rwkv_mu[l]), A_SLAB)
        if l == 0:
            v_first = v
        else:
            mv = shift_lerp(p_mv, rwkv_vres_mu[l - 1])
            v = v + (v_first - v) * jax.nn.sigmoid(rwkv_v0[l - 1] + mv @ rwkv_v2[l - 1])
        o_a = rwkv7_mixer(r, k, v, w_lo, a_lo, g_lo, rwkv_w0[l], rwkv_w2[l], rwkv_a0[l], rwkv_a2[l],
                          rwkv_g2[l], rwkv_k_k[l], rwkv_k_a[l], rwkv_r_k[l], rwkv_ln_w[l], rwkv_ln_b[l])
        q_b, c_b, iq_b, ik_b, iw_b = _split(p_b, B_SLAB)
        o_b = dsa_mixer(q_b, c_b, iq_b, ik_b, iw_b, dsa_kv_norm[l], dsa_w_uk[l], dsa_w_uv[l])
        q_c, k_c, v_c, g_c = _split(p_c, C_SLAB)
        o_c = retention_mixer(q_c, k_c, v_c, g_c)
        x = x + jnp.concatenate([o_a, o_b, o_c], axis=-1) @ w_out[l]
        x = x + 0.5 * swiglu_2(rmsnorm(x, ffn2_norm[l]), ffn2_w_gate[l], ffn2_w_up[l], ffn2_w_down[l])
    return rmsnorm(x, final_norm)


def setup_inputs(seed=0):
    out = dict(first_inputs(seed))
    for name, value in second_inputs(seed + 1).items():
        if name != "x":
            out[name + "_2"] = value
    return out


def reference(
    x, c, ctx, c_ctx, w_mod, b_mod, ffn1_w_gate, ffn1_w_up, ffn1_w_down, ffn2_w_gate, ffn2_w_up,
    ffn2_w_down, ab_w_in, ab_w_out, a_q_norm, a_k_norm, a_sink, b_q_norm, b_k_norm, b_lambda_q1,
    b_lambda_k1, b_lambda_q2, b_lambda_k2, b_sub_norm, cd_w_in, cd_w_out, c_q_a_norm,
    c_kv_a_norm, c_w_uq, c_w_ukv, c_q_nope_norm, c_q_rope_norm, c_k_nope_norm, c_k_rope_norm,
    d_q_norm, d_k_norm, d_rpb, ffn1_norm_2, ffn1_w_gate_2, ffn1_w_up_2, ffn1_w_down_2,
    mix_norm_2, w_in_2, w_out_2, rwkv_mu_2, rwkv_w0_2, rwkv_w2_2, rwkv_a0_2, rwkv_a2_2,
    rwkv_g2_2, rwkv_k_k_2, rwkv_k_a_2, rwkv_r_k_2, rwkv_ln_w_2, rwkv_ln_b_2, rwkv_vres_w_in_2,
    rwkv_vres_mu_2, rwkv_v0_2, rwkv_v2_2, dsa_kv_norm_2, dsa_w_uk_2, dsa_w_uv_2, ffn2_norm_2,
    ffn2_w_gate_2, ffn2_w_up_2, ffn2_w_down_2, final_norm_2,
):
    x = first_block(
        x, c, ctx, c_ctx, w_mod, b_mod, ffn1_w_gate, ffn1_w_up, ffn1_w_down, ffn2_w_gate,
        ffn2_w_up, ffn2_w_down, ab_w_in, ab_w_out, a_q_norm, a_k_norm, a_sink, b_q_norm,
        b_k_norm, b_lambda_q1, b_lambda_k1, b_lambda_q2, b_lambda_k2, b_sub_norm, cd_w_in,
        cd_w_out, c_q_a_norm, c_kv_a_norm, c_w_uq, c_w_ukv, c_q_nope_norm, c_q_rope_norm,
        c_k_nope_norm, c_k_rope_norm, d_q_norm, d_k_norm, d_rpb,
    )
    return second_block(
        x, ffn1_norm_2, ffn1_w_gate_2, ffn1_w_up_2, ffn1_w_down_2, mix_norm_2, w_in_2, w_out_2,
        rwkv_mu_2, rwkv_w0_2, rwkv_w2_2, rwkv_a0_2, rwkv_a2_2, rwkv_g2_2, rwkv_k_k_2,
        rwkv_k_a_2, rwkv_r_k_2, rwkv_ln_w_2, rwkv_ln_b_2, rwkv_vres_w_in_2, rwkv_vres_mu_2,
        rwkv_v0_2, rwkv_v2_2, dsa_kv_norm_2, dsa_w_uk_2, dsa_w_uv_2, ffn2_norm_2, ffn2_w_gate_2,
        ffn2_w_up_2, ffn2_w_down_2, final_norm_2,
    )


_drawn_inputs = setup_inputs


def setup_inputs(seed=0):
    import zlib

    import numpy as np

    out = dict(_drawn_inputs(seed))
    spreads = {}
    factors = {'a_q_norm': 8.0,
     'a_k_norm': 8.0,
     'a_sink': 8.0,
     'b_q_norm': 4.565,
     'b_k_norm': 4.424,
     'b_lambda_q1': 6.615,
     'b_lambda_k1': 8.0,
     'b_lambda_q2': 5.075,
     'b_lambda_k2': 7.941,
     'c_q_a_norm': 8.0,
     'c_kv_a_norm': 5.801,
     'c_q_nope_norm': 8.0,
     'c_q_rope_norm': 8.0,
     'c_k_nope_norm': 8.0,
     'c_k_rope_norm': 8.0,
     'd_q_norm': 8.0,
     'd_k_norm': 8.0,
     'd_rpb': 3.79,
     'ffn1_norm_2': 2.958,
     'rwkv_k_k_2': 7.21,
     'rwkv_k_a_2': 4.365,
     'rwkv_ln_w_2': 5.464,
     'rwkv_ln_b_2': 8.0,
     'rwkv_vres_mu_2': 11.185,
     'rwkv_v0_2': 16.687,
     'dsa_kv_norm_2': 6.484,
     'ffn2_norm_2': 4.386,
     'final_norm_2': 7.886}
    for name, (base, spread) in spreads.items():
        noise = np.random.default_rng([zlib.crc32(name.encode()), seed]).standard_normal(out[name].shape)
        drawn = base * np.exp(spread * noise) if base else spread * noise
        out[name] = jnp.asarray(drawn.astype(out[name].dtype))
    for name, factor in factors.items():
        out[name] = (out[name] * factor).astype(out[name].dtype)
    return out
```

```python
from contextlib import ExitStack, contextmanager

import numpy as np
import concourse.bass as bass
from concourse import mybir

F32 = mybir.dt.float32
ALU = mybir.AluOpType
ACT = mybir.ActivationFunctionType
AX = mybir.AxisListType

P = 128
D = 1024
KD = D // P
T = 256
TC = 512
CH = 256
CHUNK = KD * CH
WEIGHT_SLOTS = 4
N_MOD = 9
F1, F2 = 2816, 2752
SEG = 1024
SEG_TURNS = 2
FR = mybir.dt.float32r
EPS = 1e-6
GN_EPS = 64e-5
NEG = -1e30
TAKEN = -3e38
TOPK = 64
LAM_INIT = 0.8 - 0.6
HEADS_R = 6
RC = 64
LEVELS = 6
DECAY = float(np.exp(-0.5))
LORA, MV = 9, 25

AQ, BQ, AK, BK = 0, 4, 8, 9
CQ, DQ, CKV, KR, DK = 0, 6, 10, 12, 13
RR, RK, RV, SQ, SC, SIQ, SIK, TQ, TK, TG = 0, 3, 6, 10, 13, 14, 18, 19, 21, 23


def param_layout():
    widths = [("c", 16), ("a_q", 1), ("a_k", 1), ("b_q", 1), ("b_k", 1), ("sub", 1), ("sink", 8), ("lam", 4),
              ("c_qa", 6), ("c_kva", 2), ("c_qn", 1), ("c_qr", 1), ("c_kn", 1), ("c_kr", 1), ("d_q", 1), ("d_k", 1),
              ("final", 8), ("one", 1), ("eps", 1), ("gn_eps", 1)]
    for l in range(2):
        widths += [(f"{n}{l}", w) for n, w in (
            ("n1_", 8), ("nm_", 8), ("n2_", 8), ("mu_", 10), ("w0_", 3), ("a0_", 3), ("kk_", 3), ("ka_", 3),
            ("rk_", 3), ("lnw_", 3), ("lnb_", 3), ("kv_", 1), ("vmu_", 1), ("v0_", 3),
            ("lora_", 384), ("v2_", 384), ("uk_", 384), ("uv_", 384))]
    out, at = {}, 0
    for n, w in widths:
        out[n] = (at, w)
        at += w
    return out, at


CONST = [("ident", 128), ("ones128", 128), ("ones64", 128), ("ones32", 128), ("rot32", 128), ("rot16", 128),
         ("rot8", 128), ("sel", 2)]
SHARED = [("amask", 512), ("cosh", TC), ("sinh", TC), ("cosm", TC), ("sinm", TC)]
SHARED2 = [("cosr", T), ("sinr", T), ("retm", 4 * 384), ("prodm", 512), ("levelm", LEVELS * 128), ("scanm", 768),
           ("causal", 2 * T)]


class Hand:

    def __init__(self, eng, plan):
        self.eng, self.plan = eng, plan
        self.wait_ge = eng.wait_ge
        self.seen, self.per = {}, {}
        self.turn, self.stages, self.per_turn = None, 0, {}
        self.job = {"A": 0, "V": 0, "chunk": 0, "split": 0}

    def next(self, sem, n=1):
        self.seen[sem] = self.seen.get(sem, 0) + n
        return self.seen[sem] if self.turn is None or not self.per.get(sem) else self.turn * self.per[sem] + self.seen[sem]

    @contextmanager
    def repeat(self, turns, jobs, per=None):
        per = per or {}
        before = dict(self.seen)
        with self.eng.Fori(0, turns) as i:
            self.turn, self.per, self.per_turn = i, per, jobs
            yield i
        for sem, n in self.seen.items():
            assert n - before.get(sem, 0) == per.get(sem, 0), (sem, n - before.get(sem, 0))
        self.turn = None
        for sem, n in per.items():
            self.seen[sem] += n * (turns - 1)
        for kind, n in jobs.items():
            self.job[kind] += n * (turns - 1)

    def take(self, pool):
        self.job[pool] += 1
        return self.job[pool] - 1

    def _turns(self, value, kind="A"):
        return value if self.turn is None else self.turn * (self.per_turn[kind] // 4) + value

    def opens(self, job):
        return self._turns(job // 4 + 1)

    def fills(self, job):
        return self._turns(job // 4 + 1)

    def frees(self, job):
        return self._turns(job // 4 + 2)

    def lands(self, chunk):
        value = 16 * (chunk // WEIGHT_SLOTS + 1)
        return value if self.turn is None else self.turn * (4 * self.per_turn["chunk"]) + value

    def splits(self, chunk):
        return self._turns(chunk // WEIGHT_SLOTS + 2, "chunk")

    def uses(self, split):
        return split if self.turn is None else self.turn * self.per_turn["split"] + split

    def stage(self):
        if self.plan["writer"] is self:
            self.plan[self.stages] = dict(self.job)
        else:
            self.job = dict(self.plan[self.stages])
        self.stages += 1


def build(nc, A, stop=None):
    PK, PW = param_layout()
    n_chunks = A["stream"].shape[0]
    ctx = ExitStack()
    with ctx:
        def sb(name, shape):
            return ctx.enter_context(nc.sbuf_tensor(name, shape, F32))

        def sem(name):
            return ctx.enter_context(nc.semaphore(name))

        xT = sb("xT", [P, KD, TC])
        ring = sb("ring", [P, WEIGHT_SLOTS, CHUNK])
        pk = sb("pk", [P, PW])
        mods = sb("mods", [P, 72, 2])
        bmod = sb("bmod", [P, 2, 144])
        cT = sb("cT", [P, KD, 32])
        const = sb("const", [P, sum(w for _, w in CONST)])
        shared = sb("shared", [P, sum(w for _, w in SHARED2)])
        vfirst = sb("vfirst", [P, 3, T])
        small = sb("small", [P, 64])
        ARENA = 25600
        hT_at = -(-nc.sbuf_base // 32) * 32
        hT = sb("hT", [P, KD, TC])
        arena_at = hT_at + 4 * KD * TC
        arena = sb("arena", [P, ARENA])

        def over(name, at, shape):
            return nc.alloc_sbuf_tensor_at(name, shape, FR, offset=at)

        h_hi = over("h_hi", hT_at, [P, KD, TC])
        h_lo = over("h_lo", arena_at, [P, KD, TC])
        hid_hi = over("hid_hi", arena_at + 4 * 4096, [P, SEG // P, TC])
        hid_lo = over("hid_lo", arena_at + 4 * 8192, [P, SEG // P, TC])
        w_hi = over("w_hi", arena_at + 4 * 12288, [P, 2, CHUNK])
        w_lo = over("w_lo", arena_at + 4 * 16384, [P, 2, CHUNK])

        banks = {p: [ctx.enter_context(nc.psum_tensor(f"bank{p}{b}", [P, 512], F32)) for b in range(4)] for p in "AV"}
        full = {p: [sem(f"full_{p}{b}") for b in range(4)] for p in "AV"}
        freed = {p: [sem(f"freed_{p}{b}") for b in range(4)] for p in "AV"}
        landed = [sem(f"chunk_landed{s}") for s in range(WEIGHT_SLOTS)]
        used = [sem(f"chunk_used{s}") for s in range(WEIGHT_SLOTS)]
        s_par, s_x, s_tab, s_tab2 = sem("params_in"), sem("x_in"), sem("tables1_in"), sem("tables2_in")
        s_bias, s_biasroom, s_room = sem("biases_in"), sem("biases_room"), sem("tables2_room")
        s_out, s_vdone = sem("out_stored"), sem("out_ready")
        v_self, a_self, pe_self = sem("vector_step"), sem("scalar_step"), sem("tensor_step")
        v_pe, a_pe = sem("vector_made_operand"), sem("scalar_made_operand")
        v_a, a_v = sem("vector_made_for_scalar"), sem("scalar_made_for_vector")
        v_g, g_pe = sem("vector_made_for_pool"), sem("pool_made_operand")
        mod_turn = sem("modulation_turn")
        split_used, hi_made = sem("split_used"), sem("leading_part_made")
        plan = {"writer": None}

        def par(name, i=0, n=1, rows=slice(0, P)):
            at = PK[name][0] + i
            return pk[rows, at:at + n]

        cat = {}
        for tensor, items in ((const, CONST), (shared, SHARED2)):
            at = 0
            for n, w in items:
                cat[n] = tensor[:, at:at + w]
                at += w
        at = 0
        for n, w in SHARED:
            cat[n] = shared[:, at:at + w]
            at += w
        ones = {128: cat["ones128"], 64: cat["ones64"], 32: cat["ones32"]}

        def room(at, *shape):
            n = int(np.prod(shape))
            assert at + n <= ARENA, (at, shape)
            v = arena[:, at:at + n]
            if len(shape) == 2:
                v = v.rearrange("p (a b) -> p a b", a=shape[0])
            if len(shape) == 3:
                v = v.rearrange("p (a b c) -> p a b c", a=shape[0], b=shape[1])
            return v, at + n

        squares, _ = room(4096, KD, TC)
        silb, _end = room(20480, 4, TC)
        hid32, _end = room(_end, 2, TC)
        rsum, _end = room(_end, TC)
        cond_rows, _ = room(0, 4, CH)

        def groups(n):
            return [(0, 0)] if n == T else [(0, 0), (1, T)]

        def pe_norm(pe, n):
            pe.stage()
            j = pe.take("V")
            pe.wait_ge(freed["V"][j % 4], pe.opens(j))
            bank = banks["V"][j % 4]
            stream.let_go()
            for k in range(KD):
                if k % 2 == 0:
                    pe.wait_ge(a_pe, pe.next(a_pe))
                ins = stream.mm(pe, bank[:, 0:n], ones[128], squares[:, k, 0:n], k == 0, k == KD - 1)
            ins.then_inc(full["V"][j % 4], 1)

        def act_norm(act, n, affine, split=False):
            act.stage()
            act.wait_ge(v_a, act.next(v_a))
            for k in range(0, KD, 2):
                act.eng.activation(squares[:, k:k + 2, 0:n], xT[:, k:k + 2, 0:n], ACT.Square).then_inc(a_pe, 1)
            if split:
                act_hi(act, 0)
            act_root(act, act.take("V"), rsum[:, 0:n], D, par("eps"))
            for k in range(KD if affine or split else 0):
                act.wait_ge(v_a, act.next(v_a))
                out = silb[:, k % 4, :] if split else hT[:, k, :]
                if affine:
                    for g, o in groups(n):
                        ins = act.eng.activation(out[:, o:o + T], out[:, o:o + T], ACT.Identity,
                                                 bias=mods[:, 8 * (affine - 1) + k, g:g + 1],
                                                 scale=mods[:, 8 * affine + k, g:g + 1])
                if split:
                    if affine:
                        ins.then_inc(a_self, 1)
                        act.wait_ge(a_self, act.next(a_self))
                    act.eng.activation(h_hi[:, k, 0:n], out[:, 0:n], ACT.Copy).then_inc(a_v, 1)
                elif k == KD - 1:
                    ins.then_inc(a_pe, 1)

        def act_hi(act, ahead):
            c, sp = act.job["chunk"] + ahead, act.job["split"] + ahead
            act.wait_ge(landed[c % WEIGHT_SLOTS], act.lands(c))
            if sp:
                act.wait_ge(split_used, act.uses(sp))
            act.eng.activation(w_hi[:, sp % 2, :], ring[:, c % WEIGHT_SLOTS, :], ACT.Copy).then_inc(hi_made, 1)

        def vec_lo(v, ahead):
            c, sp = v.job["chunk"] + ahead, v.job["split"] + ahead
            v.wait_ge(hi_made, v.next(hi_made))
            v.eng.tensor_tensor(w_lo[:, sp % 2, :], ring[:, c % WEIGHT_SLOTS, :], w_hi[:, sp % 2, :].bitcast(F32),
                                ALU.subtract).then_inc(used[c % WEIGHT_SLOTS], 1)

        def act_root(act, job, out, over, eps):
            act.wait_ge(full["V"][job % 4], act.fills(job))
            bank = banks["V"][job % 4]
            act.eng.activation(out, bank[:, 0:out.shape[1]], ACT.Sqrt, bias=eps, scale=1.0 / over).then_inc(freed["V"][job % 4], 1)

        def vec_norm(v, n, affine=None, gain=None, split=False):
            v.stage()
            v.eng.sem_inc(v_a, 1)
            if split:
                vec_lo(v, 0)
            j = v.take("V")
            v.wait_ge(freed["V"][j % 4], v.frees(j))
            v.eng.reciprocal(rsum[:, 0:n], rsum[:, 0:n]).then_inc(v_self, 1)
            v.wait_ge(v_self, v.next(v_self))
            for k in range(KD + 2 * split):
                if k < KD:
                    out = silb[:, k % 4, 0:n] if split else hT[:, k, 0:n]
                    if affine:
                        ins = v.eng.tensor_tensor(out, xT[:, k, 0:n], rsum[:, 0:n], ALU.mult)
                    else:
                        ins = v.eng.scalar_tensor_tensor(out, xT[:, k, 0:n], par(gain, k), rsum[:, 0:n], ALU.mult, ALU.mult)
                    if affine or split:
                        ins.then_inc(v_self, 1)
                        v.wait_ge(v_self, v.next(v_self))
                        v.eng.sem_inc(v_a, 1)
                if split and k >= 2:
                    v.wait_ge(a_v, v.next(a_v))
                    v.eng.tensor_tensor(h_lo[:, k - 2, 0:n], silb[:, (k - 2) % 4, 0:n], h_hi[:, k - 2, 0:n].bitcast(F32),
                                        ALU.subtract).then_inc(v_self, 1)
                    v.wait_ge(v_self, v.next(v_self))
            if split:
                v.eng.sem_inc(v_pe, 1)
            elif not affine:
                ins.then_inc(s_vdone if gain == "final" else v_pe, 1)

        class Stream:

            def __init__(self):
                self.pending, self.held = None, None

            def next(self, pe):
                c = pe.job["chunk"]
                pe.job["chunk"] += 1
                pe.wait_ge(landed[c % WEIGHT_SLOTS], pe.lands(c))
                self.pending, self.held = self.held, c % WEIGHT_SLOTS
                return ring[:, c % WEIGHT_SLOTS, :]

            def mm(self, pe, out, lhsT, rhs, start, stop):
                ins = pe.eng.matmul(out, lhsT, rhs, start=start, stop=stop)
                if self.pending is not None:
                    ins.then_inc(used[self.pending], 1)
                    self.pending = None
                return ins

            def let_go(self):
                self.pending, self.held = self.held, None

        stream = Stream()

        def by_k(chunk, kt=KD, w=CH):
            return chunk[:, 0:kt * w].rearrange("p (k c) -> p k c", k=kt)

        def segment(cols):
            out = []
            for c in range(0, cols, CH):
                tiles = [(q, min(P, cols - c - q)) for q in range(0, min(CH, cols - c), P)]
                out += [("gate", tiles), ("up", tiles)]
            return out + [("down", [(q, min(P, cols - c - q)) for q in range(0, min(CH, cols - c), P)])
                          for c in range(0, cols, CH)]

        PER_SEG = {"A": 12, "V": 12, "chunk": 12, "split": 12}

        def pe_ffn(pe, n, f):
            pe.stage()

            def products(out, w, wc, rhs, start, stop, first):
                hi, lo = w
                a, b = rhs
                pairs = ((lo, a), (hi, b), (hi, a))
                for q, (l, r) in enumerate(pairs):
                    ins = pe.eng.matmul(out, l[wc], r, start=start and q == 0, stop=stop and q == 2)
                    if first and q == 0:
                        ins.then_inc(split_used, 1)
                return ins

            def run(cols):
                hidden_at = 0
                jobs = None
                chunks = segment(cols)
                for i, (kind, tiles) in enumerate(chunks):
                    c, b = pe.job["chunk"], pe.job["split"] % 2
                    pe.job["chunk"] += 1
                    pe.job["split"] += 1
                    if kind == "down":
                        if jobs is None:
                            jobs = []
                            for p in "AAAAVVVV":
                                j = pe.take(p)
                                pe.wait_ge(freed[p][j % 4], pe.opens(j))
                                jobs.append((p, j))
                            hidden_at = 0
                        pe.wait_ge(v_pe, pe.next(v_pe))
                    pe.wait_ge(used[c % WEIGHT_SLOTS], pe.splits(c))
                    if kind == "down":
                        w = [m[:, b, :].rearrange("p (r c) -> p r c", r=2) for m in (w_hi, w_lo)]
                        for q, (_, rows) in enumerate(tiles):
                            r = slice(0, rows)
                            rhs = [m[r, hidden_at, 0:n] for m in (hid_hi, hid_lo)]
                            last = i == len(chunks) - 1 and q == len(tiles) - 1
                            for t, (p, j) in enumerate(jobs):
                                ins = products(banks[p][j % 4][:, 0:n], w, (r, q, slice(t * P, t * P + P)), rhs,
                                               hidden_at == 0, last, q == 0 and t == 0)
                                if last:
                                    ins.then_inc(full[p][j % 4], 1)
                            hidden_at += 1
                        continue
                    w = [m[:, b, :].rearrange("p (k c) -> p k c", k=KD) for m in (w_hi, w_lo)]
                    p = "A" if kind == "gate" else "V"
                    for q, (col, width) in enumerate(tiles):
                        j = pe.take(p)
                        pe.wait_ge(freed[p][j % 4], pe.opens(j))
                        for k in range(KD):
                            ins = products(banks[p][j % 4][0:width, 0:n], w, (slice(0, P), k, slice(col, col + width)),
                                           [m[:, k, 0:n] for m in (h_hi, h_lo)], k == 0, k == KD - 1, q == 0 and k == 0)
                        ins.then_inc(full[p][j % 4], 1)

            pe.wait_ge(v_pe, pe.next(v_pe))
            with pe.repeat(SEG_TURNS, PER_SEG, {v_pe: 4}):
                run(SEG)
            run(f - SEG_TURNS * SEG)

        def act_ffn(act, n, f):
            act.stage()

            def run(cols, end):
                at, chunks = 0, segment(cols)
                for i, (kind, tiles) in enumerate(chunks):
                    if not end or i < len(chunks) - 1:
                        act_hi(act, 1)
                    act.job["chunk"] += 1
                    act.job["split"] += 1
                    if kind == "gate":
                        for _, w in tiles:
                            j = act.take("A")
                            act.wait_ge(full["A"][j % 4], act.fills(j))
                            act.eng.activation(silb[0:w, j % 4, 0:n], banks["A"][j % 4][0:w, 0:n],
                                               ACT.Silu).then_inc(freed["A"][j % 4], 1)
                    if kind == "up":
                        for q, (_, w) in enumerate(tiles):
                            act.wait_ge(v_a, act.next(v_a))
                            act.eng.activation(hid_hi[0:w, at, 0:n], hid32[0:w, q, 0:n], ACT.Copy).then_inc(a_v, 1)
                            at += 1
                act.job["A"] += 4

            with act.repeat(SEG_TURNS, PER_SEG, {v_a: 8}):
                run(SEG, False)
            run(f - SEG_TURNS * SEG, True)

        def vec_ffn(v, n, f, m):
            v.stage()

            def run(cols, end):
                at, chunks = 0, segment(cols)
                a0 = v.job["A"]
                for i, (kind, tiles) in enumerate(chunks):
                    if not end or i < len(chunks) - 1:
                        vec_lo(v, 1)
                    v.job["chunk"] += 1
                    v.job["split"] += 1
                    if kind != "up":
                        continue
                    for q, (_, w) in enumerate(tiles):
                        jv, ja = v.take("V"), v.take("A")
                        v.wait_ge(freed["A"][ja % 4], v.frees(ja))
                        v.wait_ge(full["V"][jv % 4], v.fills(jv))
                        v.eng.tensor_tensor(hid32[0:w, q, 0:n], silb[0:w, ja % 4, 0:n], banks["V"][jv % 4][0:w, 0:n],
                                            ALU.mult).then_inc(freed["V"][jv % 4], 1)
                        v.wait_ge(freed["V"][jv % 4], v.frees(jv))
                        v.eng.sem_inc(v_a, 1)
                    for q, (_, w) in enumerate(tiles):
                        v.wait_ge(a_v, v.next(a_v))
                        v.eng.tensor_tensor(hid_lo[0:w, at, 0:n], hid32[0:w, q, 0:n], hid_hi[0:w, at, 0:n].bitcast(F32),
                                            ALU.subtract).then_inc(v_self, 1)
                        v.wait_ge(v_self, v.next(v_self))
                        at += 1
                    v.eng.sem_inc(v_pe, 1)
                add_to_x(v, [("A", v.take("A")) for _ in range(4)] + [("V", v.take("V")) for _ in range(4)], n, m)

            with v.repeat(SEG_TURNS, PER_SEG, {hi_made: 12, a_v: 8, v_self: 8}):
                run(SEG, False)
            run(f - SEG_TURNS * SEG, True)

        def add_to_x(v, jobs, n, m):
            for c, (p, j) in enumerate(jobs):
                v.wait_ge(full[p][j % 4], v.fills(j))
                bank = banks[p][j % 4]
                for g, o in groups(n):
                    s = 0.5 if m is None else 1.0 if m == "one" else mods[:, 8 * m + c, g:g + 1]
                    ins = v.eng.scalar_tensor_tensor(xT[:, c, o:o + T], bank[:, o:o + T], s, xT[:, c, o:o + T],
                                                     ALU.mult, ALU.add)
                ins.then_inc(freed[p][j % 4], 1)
                v.wait_ge(freed[p][j % 4], v.frees(j))

        def pe_tiles(pe, chunk, kt, plan_, rhs_of):
            for c, w, n in plan_:
                j = pe.take("A")
                pe.wait_ge(freed["A"][j % 4], pe.opens(j))
                bank = banks["A"][j % 4]
                for k in range(kt):
                    ins = stream.mm(pe, bank[0:w, 0:n], chunk[:, k, c:c + w], rhs_of(k, n), k == 0, k == kt - 1)
                ins.then_inc(full["A"][j % 4], 1)

        def pe_rows(pe, chunk, kt, c, w, n, lhs_of):
            for tt in range(n // P):
                j = pe.take("A")
                pe.wait_ge(freed["A"][j % 4], pe.opens(j))
                bank = banks["A"][j % 4]
                for k in range(kt):
                    ins = stream.mm(pe, bank[:, 0:w], lhs_of(k, tt), chunk[:, k, c:c + w], k == 0, k == kt - 1)
                ins.then_inc(full["A"][j % 4], 1)

        def act_out(act, dst, rows=slice(0, P), width=None, func=ACT.Copy, bias=None, scale=1.0):
            j = act.take("A")
            act.wait_ge(full["A"][j % 4], act.fills(j))
            bank = banks["A"][j % 4]
            src = bank[rows, 0:width]
            if len(dst.shape) == 3:
                src = src.rearrange("p (a b) -> p a b", a=dst.shape[1])
            if bias is None:
                ins = act.eng.activation(dst, src, func, scale=scale)
            else:
                ins = act.eng.activation(dst, src, func, bias=bias, scale=scale)
            ins.then_inc(freed["A"][j % 4], 1)
            return j

        def pe_heads(pe, items, sq):
            pe.stage()
            jobs = []
            for i in range(len(items) + 1):
                if i < len(items):
                    it = items[i]
                    if it["size"]:
                        j = pe.take("V")
                        pe.wait_ge(freed["V"][j % 4], pe.opens(j))
                        bank = banks["V"][j % 4]
                        pe.wait_ge(a_pe, pe.next(a_pe))
                        for q in range(len(it["tiles"])):
                            ins = pe.eng.matmul(bank[:, 0:it["n"]], ones[it["size"]], sq[i % 2][:, q * it["n"]:(q + 1) * it["n"]],
                                                start=q == 0, stop=q == len(it["tiles"]) - 1)
                        ins.then_inc(full["V"][j % 4], 1)
                if i and items[i - 1]["rot"]:
                    it = items[i - 1]
                    for tile in it["tiles"]:
                        j = pe.take("V")
                        pe.wait_ge(freed["V"][j % 4], pe.opens(j))
                        bank = banks["V"][j % 4]
                        pe.wait_ge(v_pe, pe.next(v_pe))
                        pe.eng.matmul(bank[:, 0:it["n"]], cat[it["rot"][0]], tile, start=True, stop=True).then_inc(full["V"][j % 4], 1)
            pe.wait_ge(v_pe, pe.next(v_pe))

        def heads_jobs(items, base):
            norm, rot = {}, {}
            for i in range(len(items) + 1):
                if i < len(items) and items[i]["size"]:
                    norm[i] = base
                    base += 1
                if i and items[i - 1]["rot"]:
                    rot[i - 1] = [base + q for q in range(len(items[i - 1]["tiles"]))]
                    base += len(items[i - 1]["tiles"])
            return norm, rot, base

        def act_heads(act, items, sq, rt):
            act.stage()
            norm, _, end = heads_jobs(items, act.job["V"])
            for i in range(len(items) + 1):
                if i in norm:
                    n = items[i]["n"]
                    if i - 2 in norm:
                        act.wait_ge(full["V"][(norm[i - 2]) % 4], act.fills(norm[i - 2]))
                    for q, tile in enumerate(items[i]["tiles"]):
                        ins = act.eng.activation(sq[i % 2][:, q * n:(q + 1) * n], tile, ACT.Square)
                    ins.then_inc(a_self, 1)
                    act.wait_ge(a_self, act.next(a_self))
                    act.eng.sem_inc(a_pe, 1)
                if i - 1 in norm:
                    it = items[i - 1]
                    if i - 3 in norm:
                        act.wait_ge(v_a, act.next(v_a))
                    act_root(act, norm[i - 1], rt[(i - 1) % 2][:, 0:it["n"]], it["over"], par("eps"))
            act.wait_ge(v_a, act.next(v_a, min(2, len(norm))))

        def vec_heads(v, items, rt, inv_t, rot_t):
            v.stage()
            norm, rot, end = heads_jobs(items, v.job["V"])

            def scale(i):
                it = items[i]
                n = it["n"]
                if it["size"]:
                    v.wait_ge(freed["V"][norm[i] % 4], v.frees(norm[i]))
                    v.eng.reciprocal(inv_t[:, 0:n], rt[i % 2][:, 0:n]).then_inc(v_self, 1)
                    v.wait_ge(v_self, v.next(v_self))
                    v.eng.sem_inc(v_a, 1)
                    for q, tile in enumerate(it["tiles"]):
                        ins = v.eng.scalar_tensor_tensor(tile, tile, it["gains"][q], inv_t[:, 0:n], ALU.mult, ALU.mult)
                        if it["rot"]:
                            ins.then_inc(v_self, 1)
                            v.wait_ge(v_self, v.next(v_self))
                            v.eng.sem_inc(v_pe, 1)
                        elif q == len(it["tiles"]) - 1:
                            ins.then_inc(v_self, 1)
                            v.wait_ge(v_self, v.next(v_self))
                elif it["rot"]:
                    for _ in it["tiles"]:
                        v.eng.sem_inc(v_pe, 1)

            def rotate(i):
                it = items[i]
                n = it["n"]
                for q, tile in enumerate(it["tiles"]):
                    v.wait_ge(full["V"][rot[i][q] % 4], v.fills(rot[i][q]))
                    bank = banks["V"][rot[i][q] % 4]
                    _, cos, sin = it["rot"]
                    v.eng.tensor_tensor(rot_t[:, 0:n], bank[:, 0:n], cat[sin][:, 0:n], ALU.mult).then_inc(freed["V"][rot[i][q] % 4], 1)
                    v.wait_ge(freed["V"][rot[i][q] % 4], v.frees(rot[i][q]))
                    v.eng.tensor_tensor(tile, tile, cat[cos][:, 0:n], ALU.mult).then_inc(v_self, 1)
                    v.wait_ge(v_self, v.next(v_self))
                    v.eng.tensor_tensor(tile, tile, rot_t[:, 0:n], ALU.add).then_inc(v_self, 1)
                    v.wait_ge(v_self, v.next(v_self))

            for i in range(len(items) + 1):
                if i < len(items):
                    scale(i)
                if i and items[i - 1]["rot"]:
                    rotate(i - 1)
            v.eng.sem_inc(v_pe, 1)
            v.job["V"] = end

        def item(tiles, n, size, over=None, gains=None, rot=None):
            return {"tiles": tiles, "n": n, "size": size, "over": over or size, "gains": gains, "rot": rot}

        def att_jobs(gs, base):
            jt, jav, a = {}, {}, base
            u = 0
            for g, grp in enumerate(gs):
                for _ in grp["units"]:
                    jt[u] = a
                    a += 1
                    u += 1
                jav[g] = a
                a += 1
            return jt, jav, a

        def flat(gs):
            return [(g, qi, un) for g, grp in enumerate(gs) for qi, un in enumerate(grp["units"])]

        def pe_att(pe, gs, W):
            pe.stage()
            us = flat(gs)
            a0 = pe.job["A"]
            for u in range(len(us) + 1):
                if u < len(us):
                    for parts in us[u][2]["maps"]:
                        j = pe.take("V")
                        pe.wait_ge(freed["V"][j % 4], pe.opens(j))
                        bank = banks["V"][j % 4]
                        for i, (q, k) in enumerate(parts):
                            ins = pe.eng.matmul(bank[:, 0:us[u][2]["nk"]], q, k, start=i == 0, stop=i == len(parts) - 1)
                        ins.then_inc(full["V"][j % 4], 1)
                if u:
                    g, qi, un = us[u - 1]
                    j = pe.take("A")
                    pe.wait_ge(freed["A"][j % 4], pe.opens(j))
                    bank = banks["A"][j % 4]
                    pe.wait_ge(v_pe, pe.next(v_pe))
                    for c in range(un["nk"] // P):
                        ins = pe.eng.transpose(bank[:, c * P:(c + 1) * P], W["pn"][:, (u - 1) % 2, c * P:(c + 1) * P], cat["ident"])
                    ins.then_inc(full["A"][j % 4], 1)
                    if qi == len(gs[g]["units"]) - 1:
                        pe.wait_ge(freed["A"][j % 4], pe.frees(j))
                        jo = pe.take("A")
                        pe.wait_ge(freed["A"][jo % 4], pe.opens(jo))
                        bank = banks["A"][jo % 4]
                        n = P * len(gs[g]["units"])
                        r = gs[g]["rows"]
                        for c, val in enumerate(gs[g]["vals"]):
                            ins = pe.eng.matmul(bank[r, 0:n], val, W["pT"][:, g % 2, c, 0:n], start=c == 0,
                                                stop=c == len(gs[g]["vals"]) - 1)
                        ins.then_inc(full["A"][jo % 4], 1)

        def act_att(act, gs, W):
            act.stage()
            us = flat(gs)
            jt, jav, end = att_jobs(gs, act.job["A"])
            for u in range(len(us) + 1):
                if u < len(us):
                    un = us[u][2]
                    for m in range(len(un["maps"])):
                        act.wait_ge(v_a, act.next(v_a))
                        s = W["s"][:, u % 2, m, 0:un["nk"]]
                        nm = W["st"][:, u % 2, m:m + 1]
                        if un["sink"] is not None:
                            act.eng.activation(W["st"][:, u % 2, 4:5], un["sink"], ACT.Exp, bias=nm)
                        act.eng.activation(s, s, ACT.Exp, bias=nm, accum_out=W["st"][:, u % 2, 2 + m:3 + m]).then_inc(a_self, 1)
                        act.wait_ge(a_self, act.next(a_self))
                        act.eng.sem_inc(a_v, 1)
                if u:
                    g, qi, un = us[u - 1]
                    nc_ = un["nk"] // P
                    act.wait_ge(full["A"][(jt[u - 1]) % 4], act.fills(jt[u - 1]))
                    bank = banks["A"][(jt[u - 1]) % 4]
                    act.eng.activation(W["pT"][:, g % 2, 0:nc_, qi * P:(qi + 1) * P],
                                                   bank[:, 0:nc_ * P].rearrange("p (c q) -> p c q", c=nc_), ACT.Copy).then_inc(freed["A"][(jt[u - 1]) % 4], 1)
                    if qi == len(gs[g]["units"]) - 1:
                        act.wait_ge(full["A"][jav[g] % 4], act.fills(jav[g]))
                        bank = banks["A"][jav[g] % 4]
                        act.eng.activation(gs[g]["dst"], bank[gs[g]["rows"], 0:P * len(gs[g]["units"])], ACT.Copy).then_inc(freed["A"][jav[g] % 4], 1)
            act.job["A"] = end

        def vec_att(v, gs, W):
            v.stage()
            us = flat(gs)
            jt, jav, end = att_jobs(gs, v.job["A"])
            for u in range(len(us) + 1):
                if u < len(us):
                    un = us[u][2]
                    nk = un["nk"]
                    for m in range(len(un["maps"])):
                        j = v.take("V")
                        v.wait_ge(full["V"][j % 4], v.fills(j))
                        bank = banks["V"][j % 4]
                        s = W["s"][:, u % 2, m, :]
                        if un["mask"] is not None:
                            if nk > T:
                                v.eng.tensor_scalar(s[:, T:nk], bank[:, T:nk], un["scale"], None, ALU.mult)
                            ins = v.eng.scalar_tensor_tensor(s[:, 0:T], bank[:, 0:T], un["scale"], un["mask"], ALU.mult, ALU.add)
                        else:
                            ins = v.eng.tensor_scalar(s[:, 0:nk], bank[:, 0:nk], un["scale"], None, ALU.mult)
                        ins.then_inc(freed["V"][j % 4], 1)
                        v.wait_ge(freed["V"][j % 4], v.frees(j))
                        nm = W["st"][:, u % 2, m:m + 1]
                        if un["sink"] is not None:
                            v.eng.tensor_reduce(nm, s[:, 0:nk], AX.X, ALU.max, negate=True).then_inc(v_self, 1)
                            v.wait_ge(v_self, v.next(v_self))
                            v.eng.scalar_tensor_tensor(nm, un["sink"], -1.0, nm, ALU.mult, ALU.min).then_inc(v_self, 1)
                            v.wait_ge(v_self, v.next(v_self))
                            v.eng.sem_inc(v_a, 1)
                        else:
                            v.eng.tensor_reduce(nm, s[:, 0:nk], AX.X, ALU.max, negate=True).then_inc(v_self, 1)
                            v.wait_ge(v_self, v.next(v_self))
                            v.eng.sem_inc(v_a, 1)
                if u:
                    g, qi, un = us[u - 1]
                    b = (u - 1) % 2
                    nk = un["nk"]
                    nm_ = len(un["maps"])
                    v.wait_ge(a_v, v.next(a_v, nm_))
                    st = W["st"]
                    if un["sink"] is not None:
                        v.eng.tensor_tensor(st[:, b, 2:3], st[:, b, 2:3], st[:, b, 4:5], ALU.add).then_inc(v_self, 1)
                        v.wait_ge(v_self, v.next(v_self))
                    v.eng.reciprocal(st[:, b, 5:5 + nm_], st[:, b, 2:2 + nm_]).then_inc(v_self, 1)
                    v.wait_ge(v_self, v.next(v_self))
                    if u >= 3:
                        v.wait_ge(full["A"][(jt[u - 3]) % 4], v.fills(jt[u - 3]))
                    pn = W["pn"][:, b, 0:nk]
                    if nm_ == 1:
                        v.eng.tensor_scalar(pn, W["s"][:, b, 0, 0:nk], st[:, b, 5:6], None, ALU.mult).then_inc(v_self, 1)
                        v.wait_ge(v_self, v.next(v_self))
                        v.eng.sem_inc(v_pe, 1)
                    else:
                        v.eng.tensor_scalar(pn, W["s"][:, b, 0, 0:nk], st[:, b, 5:6], None, ALU.mult)
                        v.eng.tensor_tensor(st[:, b, 6:7], st[:, b, 6:7], small[:, 1:2], ALU.mult).then_inc(v_self, 1)
                        v.wait_ge(v_self, v.next(v_self))
                        v.eng.scalar_tensor_tensor(pn, W["s"][:, b, 1, 0:nk], st[:, b, 6:7], pn, ALU.mult, ALU.add).then_inc(v_self, 1)
                        v.wait_ge(v_self, v.next(v_self))
                        v.eng.sem_inc(v_pe, 1)
            v.job["A"] = end

        fm0, e0 = room(0, 13, TC)
        vt0, e0 = room(e0, 4, 640)
        sq0a, e1 = room(e0, TC)
        sq0b, e1 = room(e1, TC)
        rt0, e1 = room(e1, 2, TC)
        in0, e1 = room(e1, TC)
        ro0, e1 = room(e1, TC)
        W0 = {}
        W0["s"], e1 = room(e0, 2, 2, TC)
        W0["pn"], e1 = room(e1, 2, TC)
        W0["pT"], e1 = room(e1, 2, 4 * T)
        W0["pT"] = W0["pT"].rearrange("p g (c q) -> p g c q", c=4)
        W0["st"], e1 = room(e1, 2, 8)
        sqy, e2 = room(e0, 2, TC)
        rty, e2 = room(e2, 2, TC)
        iny, e2 = room(e2, TC)
        yT = hT

        def rope_items0():
            rope = ("rot16", "cosh", "sinh")
            its = []
            for t in range(13):
                g = "a_q" if t < BQ else "b_q" if t < AK else "a_k" if t < BK else "b_k"
                its.append(item([fm0[:, t, :]], TC, 64, gains=[par(g)], rot=rope))
            return its

        def att0():
            gs = []
            for side in range(2):
                nk, k0 = (TC, 0) if side == 0 else (T, T)
                kts = range(4) if side == 0 else range(2, 4)
                for h in range(8):
                    r = slice(64 * (h // 4), 64 * (h // 4) + 64)
                    units = []
                    for qt in range(2):
                        q0 = T * side + P * qt
                        units.append({"maps": [[(fm0[r, AQ + h % 4, q0:q0 + P], fm0[r, AK, k0:k0 + nk])]], "nk": nk,
                                      "scale": 0.125, "sink": par("sink", h),
                                      "mask": cat["amask"][:, qt * T:(qt + 1) * T] if side == 0 else None})
                    o = slice(64 * (h % 2), 64 * (h % 2) + 64)
                    gs.append({"units": units, "rows": o, "dst": yT[o, h // 2, T * side:T * side + T],
                               "vals": [vt0[:, kt, 64 * (h // 4):64 * (h // 4) + 64] for kt in kts]})
                for h in range(4):
                    units = []
                    for qt in range(2):
                        q0 = T * side + P * qt
                        maps = [[(fm0[64 * m:64 * m + 64, BQ + h, q0:q0 + P], fm0[64 * m:64 * m + 64, BK + h, k0:k0 + nk])]
                                for m in range(2)]
                        units.append({"maps": maps, "nk": nk, "scale": 0.125, "sink": None, "mask": None})
                    gs.append({"units": units, "rows": slice(0, P), "dst": yT[:, 4 + h, T * side:T * side + T],
                               "vals": [vt0[:, kt, 128 + 128 * h:256 + 128 * h] for kt in kts]})
            return gs

        def sub_items():
            return [item([yT[:, 4 + h, :]], TC, 128, gains=[small[:, 4:5]]) for h in range(4)]

        fm1, f0 = room(0, 17, TC)
        vt1, f0 = room(f0, 4, 512)
        bias1, _ = room(16000, 16, T)
        sq1, f1_ = room(f0, 2, 3 * TC)
        rt1, f1_ = room(f1_, 2, TC)
        in1, f1_ = room(f1_, TC)
        ro1, f1_ = room(f1_, TC)
        W1 = {}
        W1["s"], g0 = room(f0, 2, 2 * TC)
        W1["s"] = W1["s"].rearrange("p u (m k) -> p u m k", m=2)
        W1["pn"], g0 = room(g0, 2, TC)
        W1["pT"], g0 = room(g0, 2, 4 * T)
        W1["pT"] = W1["pT"].rearrange("p g (c q) -> p g c q", c=4)
        W1["st"], g0 = room(g0, 2, 8)

        qn1 = hT[:, 0:2, :].rearrange("p a (b t) -> p (a b) t", b=2)
        qr1 = hT[:, 2, :].rearrange("p (b t) -> p b t", b=2)
        kn1 = hT[:, 3:7, :]
        vm1 = fm1[:, CQ:CQ + 4, :]
        ym1 = xT[:, :, T:TC]

        def items1a():
            its = [item([fm1[:, CQ + t, 0:T] for t in range(6)], T, 128, 768, [par("c_qa", t) for t in range(6)]),
                   item([fm1[:, CKV + t, :] for t in range(2)], TC, 128, 256, [par("c_kva", t) for t in range(2)]),
                   item([fm1[:, KR, :]], TC, 32, gains=[par("c_kr")], rot=("rot8", "cosm", "sinm"))]
            its += [item([fm1[:, DQ + t, 0:T]], T, 64, gains=[par("d_q")]) for t in range(4)]
            its += [item([fm1[:, DK + t, :]], TC, 64, gains=[par("d_k")]) for t in range(4)]
            return its

        def items1b():
            its = [item([qn1[:, t, :]], T, 64, gains=[par("c_qn")]) for t in range(4)]
            its += [item([qr1[:, t, :]], T, 32, gains=[par("c_qr")], rot=("rot8", "cosm", "sinm")) for t in range(2)]
            its += [item([kn1[:, t, :]], TC, 64, gains=[par("c_kn")]) for t in range(4)]
            return its

        def att1(which):
            gs = []
            for h in range(8):
                o = slice(64 * (h % 2), 64 * (h % 2) + 64)
                units = []
                for qt in range(2):
                    q = slice(P * qt, P * qt + P)
                    if which == 0:
                        ro = slice(32 * (h % 4), 32 * (h % 4) + 32)
                        units.append({"maps": [[(qn1[o, h // 2, q], kn1[o, h // 2, :]), (qr1[ro, h // 4, q], fm1[ro, KR, :])]],
                                      "nk": TC, "scale": 96 ** -0.5, "sink": None, "mask": None})
                    else:
                        units.append({"maps": [[(fm1[o, DQ + h // 2, q], fm1[o, DK + h // 2, :])]], "nk": TC,
                                      "scale": 0.125, "sink": None, "mask": bias1[:, 2 * h + qt, :]})
                vals = [(vm1 if which == 0 else vt1)[:, kt, 64 * h:64 * h + 64] for kt in range(4)]
                gs.append({"units": units, "rows": o, "dst": ym1[o, 4 * which + h // 2, :], "vals": vals})
            return gs

        fs, s0 = room(0, 26, T)
        vtr, s0 = room(s0, 2, T)
        iw, s0 = room(s0, 2, 8)
        diff, _d = room(s0, 11, T)
        AR, s1 = room(s0, 3, 4 * P)
        AR = AR.rearrange("p a (b c t) -> p a b c t", b=2, c=2)
        Bf, s1 = room(s1, 3, T)
        Kf, s1 = room(s1, 3, T)
        gate, s1 = room(s1, 3, T)
        yr, s1 = room(s1, 3, T)
        ec, s1 = room(s1, 3, T)
        lo, s2 = room(s1, T)
        sgw, s2 = room(s2, 3, T)
        sa, s2 = room(s2, 3, T)
        sv, s2 = room(s2, 3, T)
        kk, s2 = room(s2, 3, T)
        w1, s2 = room(s2, 3, T)
        w2, s2 = room(s2, 3, T)
        tok, s3 = room(s1, 6, 384)
        prod, s3 = room(s3, 12, 512)
        NM, s3 = room(s3, 12, P)
        Y, s3 = room(s3, 12, P)
        U, _ = room(s3 - 2 * 12 * P, 384)
        SA, _ = room(s3 - 2 * 12 * P + 384, 384)
        S, _ = room(s3 - 2 * 12 * P + 768, 2, 192)
        Xh, XTh = xT[:, 0:6, T:TC], hT[:, 0:6, T:TC]

        def at(m, i, r=slice(0, P), c=slice(0, P)):
            return m[r, i // 2, 128 * (i % 2) + c.start:128 * (i % 2) + c.stop]

        ctok, d0 = room(s0, 2, P)
        qlat, d0 = room(d0, 6, T)
        olat, d0 = room(d0, 6, T)
        acc, d0 = room(d0, 2, T)
        tmp, d0 = room(d0, T)
        madd, d0 = room(d0, 2, T)
        top8, d0 = room(d0, 8)
        W2 = {}
        sS, d0 = room(d0, 2, T)
        W2["s"] = sS.rearrange("p u (m k) -> p u m k", m=1)
        W2["pn"], d0 = room(d0, 2, T)
        W2["pT"], d0 = room(d0, 2, 2 * T)
        W2["pT"] = W2["pT"].rearrange("p g (c q) -> p g c q", c=2)
        W2["st"], d0 = room(d0, 2, 8)
        sT, r0 = room(d0, 4, 384)
        sg, r0 = room(r0, 2, T)
        sqr, r0 = room(r0, 2, T)
        rtr, r0 = room(r0, 2, T)
        inr, r0 = room(r0, T)
        ror, r0 = room(r0, T)

        def two(t):
            return t[:, 0, :], t[:, 1, :]

        def half(h):
            return slice(64 * (h % 2), 64 * (h % 2) + 64)

        def pe_mod(pe):
            pe.stage()
            stream.let_go()
            pe.wait_ge(a_pe, pe.next(a_pe))
            jm = pe.take("V")
            pe.wait_ge(freed["V"][jm % 4], pe.opens(jm))
            if stream.pending is not None:
                stream.mm(pe, banks["V"][jm % 4][0:32, 0:32], cT[:, 0, :], cT[:, 0, :], True, True)
            with pe.repeat(9, {"A": 4, "chunk": 4}) as i:
                jobs = []
                for c in range(4):
                    w = by_k(stream.next(pe))
                    j = pe.take("A")
                    pe.wait_ge(freed["A"][j % 4], pe.opens(j))
                    for k in range(KD):
                        g = slice(32 * (k % 4), 32 * (k % 4) + 32)
                        ins = stream.mm(pe, banks["A"][j % 4][g, 0:CH], cT[:, k, :], w[:, k, :], k < 4, k >= 4)
                    ins.then_inc(full["A"][j % 4], 1)
                    jobs.append(j)
                stream.let_go()
                for c, j in enumerate(jobs):
                    pe.wait_ge(freed["A"][j % 4], pe.frees(j))
                    for t in range(2):
                        ins = stream.mm(pe, banks["V"][jm % 4][:, bass.ds(i * 16 + 4 * c + 2 * t, 2)],
                                        cond_rows[:, c, t * P:(t + 1) * P], cat["sel"], True, True)
                ins.then_inc(mod_turn, 1)
            pe.eng.sem_inc(full["V"][jm % 4], 1)

        def act_mod(act):
            act.stage()
            with act.repeat(9, {"A": 4, "chunk": 4}):
                for c in range(4):
                    j = act.take("A")
                    act.job["chunk"] += 1
                    act.wait_ge(full["A"][j % 4], act.fills(j))
                    act.eng.activation(cond_rows[:, c, :], banks["A"][j % 4][:, 0:CH], ACT.Copy).then_inc(freed["A"][j % 4], 1)

        def vec_mod(v, l):
            v.stage()
            j = v.take("V")
            v.wait_ge(mod_turn, v.next(mod_turn, 9))
            bank = banks["V"][j % 4]
            m2 = mods[:, :, :].rearrange("p a b -> p (a b)")
            v.eng.tensor_tensor(m2, bank[:, 0:144], bmod[:, l, :], ALU.add).then_inc(v_self, 1)
            v.wait_ge(v_self, v.next(v_self))
            for m, add, mul in ((1, 1.0, 1.0), (4, 1.0, 1.0), (7, 1.0, 1.0), (2, 0.0, 0.5), (8, 0.0, 0.5)):
                seg = m2[:, 16 * m:16 * m + 16]
                ins = v.eng.tensor_scalar(seg, seg, add, mul, ALU.add, ALU.mult)
            ins.then_inc(freed["V"][j % 4], 1)
            v.wait_ge(freed["V"][j % 4], v.frees(j))

        def pe_out(pe, n, rhs_of):
            pe.stage()
            for c in range(KD):
                if c % 2 == 0:
                    w = by_k(stream.next(pe))
                p = "A" if c < 4 else "V"
                j = pe.take(p)
                pe.wait_ge(freed[p][j % 4], pe.opens(j))
                bank = banks[p][j % 4]
                for k in range(KD):
                    ins = stream.mm(pe, bank[:, 0:n], w[:, k, (c % 2) * P:(c % 2 + 1) * P], rhs_of(k), k == 0, k == KD - 1)
                ins.then_inc(full[p][j % 4], 1)

        def vec_out(v, n, m):
            v.stage()
            add_to_x(v, [("A", v.take("A")) for _ in range(4)] + [("V", v.take("V")) for _ in range(4)], n, m)

        def pe_mix0(pe):
            def h_rhs(k, n):
                return hT[:, k, 0:n]

            def h_lhs(k, tt):
                return hT[:, k, tt * P:(tt + 1) * P]

            pe.wait_ge(a_pe, pe.next(a_pe))
            for c in range(7):
                w = by_k(stream.next(pe))
                pe_tiles(pe, w, KD, [(0, P, TC)] if c == 6 else [(0, P, TC), (P, P, TC)], h_rhs)
            pe_rows(pe, w, KD, P, P, TC, h_lhs)
            for c in range(2):
                pe_rows(pe, by_k(stream.next(pe)), KD, 0, CH, TC, h_lhs)
            pe_heads(pe, rope_items0(), (sq0a, sq0b))
            pe_att(pe, att0(), W0)
            pe_heads(pe, sub_items(), two(sqy))
            pe_out(pe, TC, lambda k: yT[:, k, :])

        def act_mix0(act):
            for t in range(13):
                act_out(act, fm0[:, t, :], width=TC)
            for tt in range(4):
                act_out(act, vt0[:, tt, 0:P], width=P)
            for c in range(2):
                for tt in range(4):
                    j = act_out(act, vt0[:, tt, P + CH * c:P + CH * c + CH], width=CH)
            act.wait_ge(freed["A"][j % 4], act.frees(j))
            act_heads(act, rope_items0(), (sq0a, sq0b), two(rt0))
            act_att(act, att0(), W0)
            act.wait_ge(freed["A"][(act.job["A"] - 1) % 4], act.frees(act.job["A"] - 1))
            act_heads(act, sub_items(), two(sqy), two(rty))

        def vec_mix0(v):
            v.job["A"] += 13 + 12
            vec_heads(v, rope_items0(), two(rt0), in0, ro0)
            vec_att(v, att0(), W0)
            vec_heads(v, sub_items(), two(rty), iny, None)
            vec_out(v, TC, 5)

        def pe_mix1(pe):
            def h_lhs(k, tt):
                return hT[:, k, tt * P:(tt + 1) * P]

            pe.wait_ge(a_pe, pe.next(a_pe))
            for c in range(9):
                w = by_k(stream.next(pe))
                plan_ = [(P * q, P, T if 2 * c + q < CKV else TC) for q in range(2) if 2 * c + q < 17]
                pe_tiles(pe, w, KD, plan_, lambda k, n: hT[:, k, 0:n])
            for c in range(2):
                pe_rows(pe, by_k(stream.next(pe)), KD, 0, CH, TC, h_lhs)
            pe_heads(pe, items1a(), two(sq1))
            for c in range(3):
                pe_tiles(pe, by_k(stream.next(pe), 6), 6, [(0, P, T), (P, P, T)], lambda k, n: fm1[:, CQ + k, 0:n])
            w = by_k(stream.next(pe), 2, D)
            pe_tiles(pe, w, 2, [(P * t, P, TC) for t in range(4)], lambda k, n: fm1[:, CKV + k, 0:n])
            pe_rows(pe, w, 2, 512, 512, TC, lambda k, tt: fm1[:, CKV + k, tt * P:(tt + 1) * P])
            pe_heads(pe, items1b(), two(sq1))
            pe_att(pe, att1(0), W1)
            pe_att(pe, att1(1), W1)
            pe.wait_ge(freed["A"][(pe.job["A"] - 1) % 4], pe.frees(pe.job["A"] - 1))
            pe_out(pe, T, lambda k: ym1[:, k, :])

        def act_mix1(act):
            for t in range(17):
                n = T if t < CKV else TC
                act_out(act, fm1[:, t, 0:n], width=n)
            for c in range(2):
                for tt in range(4):
                    j = act_out(act, vt1[:, tt, CH * c:CH * c + CH], width=CH)
            act.wait_ge(freed["A"][j % 4], act.frees(j))
            act_heads(act, items1a(), two(sq1), two(rt1))
            for t in range(4):
                act_out(act, qn1[:, t, :], width=T)
            for t in range(2):
                act_out(act, qr1[:, t, :], width=T)
            for t in range(4):
                act_out(act, kn1[:, t, :], width=TC)
            for tt in range(4):
                j = act_out(act, vm1[:, tt, :], width=TC)
            act.wait_ge(freed["A"][j % 4], act.frees(j))
            act_heads(act, items1b(), two(sq1), two(rt1))
            act_att(act, att1(0), W1)
            act_att(act, att1(1), W1)

        def vec_mix1(v):
            v.job["A"] += 17 + 8
            vec_heads(v, items1a(), two(rt1), in1, ro1)
            v.job["A"] += 14
            vec_heads(v, items1b(), two(rt1), in1, ro1)
            vec_att(v, att1(0), W1)
            v.eng.wait_ge(s_bias, 16)
            vec_att(v, att1(1), W1)
            vec_out(v, T, 5)

        def c_items(l):
            return [item([fs[:, SC, :]], T, 128, gains=[par(f"kv_{l}")])]

        def ret_items():
            return [item([fs[:, t, :]], T, 0, rot=("rot32", "cosr", "sinr")) for t in (TQ, TQ + 1, TK, TK + 1)]

        def ret_norms():
            return [item([yT[:, 6 + t, 0:T]], T, 64, gains=[par("one")]) for t in range(2)]

        def att2():
            gs = []
            for h in range(6):
                units = [{"maps": [[(qlat[:, h, P * qt:P * qt + P], fs[:, SC, :])]], "nk": T, "scale": 1.0, "sink": None,
                          "mask": madd[:, qt, :]} for qt in range(2)]
                gs.append({"units": units, "rows": slice(0, P), "dst": olat[:, h, :], "vals": [ctok[:, kt, :] for kt in range(2)]})
            return gs

        SIXES = [(h, tt) for h in range(HEADS_R) for tt in range(2)]

        def pe_sums(pe, src):
            for t in range(3):
                j = pe.take("V")
                pe.wait_ge(freed["V"][j % 4], pe.opens(j))
                bank = banks["V"][j % 4]
                pe.eng.matmul(bank[:, 0:T], ones[64], src[:, t, :], start=True, stop=True).then_inc(full["V"][j % 4], 1)

        def pe_mix2(pe, l):
            def h_lhs(k, tt):
                return hT[:, k, tt * P:(tt + 1) * P]

            pe.wait_ge(v_pe, pe.next(v_pe))
            for c in range(13):
                w = by_k(stream.next(pe))
                pe_tiles(pe, w, KD, [(0, P, T), (P, P if c < 12 else 24, T)], lambda k, n: hT[:, k, 0:n])
            pe_rows(pe, w, KD, P + 16, 8, T, h_lhs)
            pe_rows(pe, by_k(stream.next(pe)), KD, 0, CH, T, h_lhs)
            pe.wait_ge(a_pe, pe.next(a_pe))
            lora = par(f"lora_{l}", 0, 384)
            for r in (slice(0, 32), slice(32, 64), slice(64, P)):
                for t in range(3):
                    j = pe.take("A")
                    pe.wait_ge(freed["A"][j % 4], pe.opens(j))
                    bank = banks["A"][j % 4]
                    pe.eng.matmul(bank[:, 0:T], lora[r, t * P:(t + 1) * P], lo[r, :], start=True, stop=True).then_inc(full["A"][j % 4], 1)
            if l:
                for t in range(3):
                    j = pe.take("A")
                    pe.wait_ge(freed["A"][j % 4], pe.opens(j))
                    bank = banks["A"][j % 4]
                    pe.eng.matmul(bank[:, 0:T], par(f"v2_{l}", 0, 384)[0:16, t * P:(t + 1) * P], fs[0:16, MV, :],
                                          start=True, stop=True).then_inc(full["A"][j % 4], 1)
            pe.wait_ge(v_pe, pe.next(v_pe))
            pe_sums(pe, w1)
            pe.wait_ge(v_pe, pe.next(v_pe))
            pe_sums(pe, w1)
            for h, tt in SIXES:
                j = pe.take("V")
                pe.wait_ge(freed["V"][j % 4], pe.opens(j))
                bank = banks["V"][j % 4]
                ts = slice(P * tt, P * tt + P)
                rhs = AR[half(h), h // 2, tt, :, :].rearrange("p c t -> p (c t)")
                pe.eng.matmul(bank[:, 0:T], Bf[half(h), h // 2, ts], rhs, start=True, stop=True)
                pe.eng.matmul(bank[:, T:TC], Kf[half(h), h // 2, ts], rhs, start=True, stop=True).then_inc(full["V"][j % 4], 1)
            for src in (Bf, Kf, fs[:, RV:RV + 3, :]):
                for tt in range(2):
                    j = pe.take("A")
                    pe.wait_ge(freed["A"][j % 4], pe.opens(j))
                    bank = banks["A"][j % 4]
                    for t in range(3):
                        ins = pe.eng.transpose(bank[:, t * P:(t + 1) * P], src[:, t, P * tt:P * tt + P], cat["ident"])
                    ins.then_inc(full["A"][j % 4], 1)
            pe.wait_ge(v_pe, pe.next(v_pe))
            for lev in range(LEVELS):
                pe.wait_ge(g_pe, pe.next(g_pe))
                if lev:
                    pe.wait_ge(v_pe, pe.next(v_pe))
                for q in range(3):
                    j = pe.take("A")
                    pe.wait_ge(freed["A"][j % 4], pe.opens(j))
                    bank = banks["A"][j % 4]
                    for i in range(4 * q, 4 * q + 4):
                        ins = pe.eng.matmul(bank[:, (i % 4) * P:(i % 4 + 1) * P], NM[:, i, :], at(Xh, i), start=True, stop=True)
                    ins.then_inc(full["A"][j % 4], 1)
                pe.wait_ge(freed["A"][j % 4], pe.frees(j))
                if lev:
                    pe.wait_ge(v_pe, pe.next(v_pe))
                if lev < LEVELS - 1:
                    for q in range(3):
                        j = pe.take("V")
                        pe.wait_ge(freed["V"][j % 4], pe.opens(j))
                        bank = banks["V"][j % 4]
                        for i in range(4 * q, 4 * q + 4):
                            ins = pe.eng.matmul(bank[:, (i % 4) * P:(i % 4 + 1) * P], at(XTh, i), Y[:, i, :], start=True, stop=True)
                        ins.then_inc(full["V"][j % 4], 1)
                for q in range(3):
                    j = pe.take("V")
                    pe.wait_ge(freed["V"][j % 4], pe.opens(j))
                    bank = banks["V"][j % 4]
                    for i in range(4 * q, 4 * q + 4):
                        ins = pe.eng.matmul(bank[:, (i % 4) * P:(i % 4 + 1) * P], Y[:, i, :], at(XTh, i), start=True, stop=True)
                    ins.then_inc(full["V"][j % 4], 1)
            pe.wait_ge(v_pe, pe.next(v_pe))
            for ci in range(T // RC):
                tt, o = ci // 2, slice(64 * (ci % 2), 64 * (ci % 2) + 64)
                S0 = S[:, ci % 2, :]
                same = [h for h in range(HEADS_R) if half(h) == o]
                other = [h for h in range(HEADS_R) if half(h) != o]

                def col(h):
                    return slice(64 * h, 64 * h + 64)

                def duo(h):
                    return slice(64 * (h // 2), 64 * (h // 2) + 64)

                jU = pe.take("V")
                pe.wait_ge(freed["V"][jU % 4], pe.opens(jU))
                bank = banks["V"][jU % 4]
                for h in other + same:
                    pe.eng.matmul(bank[o, col(h)], prod[o, 2 * h + tt, T + o.start:T + o.stop], tok[o, 4 + tt, col(h)],
                                  start=h == other[0], stop=False)
                    if ci and h == other[-1]:
                        pe.wait_ge(v_pe, pe.next(v_pe))
                    if h in same:
                        ins = pe.eng.matmul(bank[o, col(h)], AR[half(h), h // 2, tt, 0, o], S0[half(h), duo(h)],
                                            start=False, stop=False)
                ins.then_inc(pe_self, 1)
                pe.wait_ge(pe_self, pe.next(pe_self))
                for h in other:
                    ins = pe.eng.matmul(bank[o, col(h)], AR[half(h), h // 2, tt, 0, o], S0[half(h), duo(h)],
                                        start=False, stop=h == other[-1])
                ins.then_inc(full["V"][jU % 4], 1)
                jSA = pe.take("V")
                pe.wait_ge(freed["V"][jSA % 4], pe.opens(jSA))
                bank = banks["V"][jSA % 4]
                pe.wait_ge(freed["V"][jU % 4], pe.frees(jU))
                for h in range(HEADS_R):
                    c = slice(64 * h, 64 * h + 64)
                    ins = pe.eng.matmul(bank[o, c], at(XTh, 2 * h + tt, o, o), U[o, c], start=True, stop=True)
                ins.then_inc(full["V"][jSA % 4], 1)
                pe.wait_ge(freed["V"][jSA % 4], pe.frees(jSA))
                if ci < T // RC - 1:
                    j = pe.take("V")
                    pe.wait_ge(freed["V"][j % 4], pe.opens(j))
                    bank = banks["V"][j % 4]
                    for h in range(HEADS_R):
                        c, hs = slice(64 * h, 64 * h + 64), slice(64 * (h // 2), 64 * (h // 2) + 64)
                        pe.eng.matmul(bank[half(h), hs], tok[o, tt, c], SA[o, c], start=True, stop=False)
                        ins = pe.eng.matmul(bank[half(h), hs], tok[o, 2 + tt, c], tok[o, 4 + tt, c], start=False, stop=True)
                    ins.then_inc(full["V"][j % 4], 1)
                j = pe.take("A")
                pe.wait_ge(freed["A"][j % 4], pe.opens(j))
                bank = banks["A"][j % 4]
                for h in other + same:
                    i, out = 2 * h + tt, bank[half(h), duo(h)]
                    pe.eng.matmul(out, SA[o, col(h)], prod[o, i, P + o.start:P + o.stop], start=h in (other[0], same[0]), stop=False)
                    ins = pe.eng.matmul(out, tok[o, 4 + tt, col(h)], prod[o, i, 384 + o.start:384 + o.stop],
                                        start=False, stop=False)
                    if h in same:
                        ins = pe.eng.matmul(out, S0[half(h), duo(h)], AR[half(h), h // 2, tt, 1, o], start=False, stop=h == same[-1])
                ins.then_inc(pe_self, 1)
                pe.wait_ge(pe_self, pe.next(pe_self))
                for h in other:
                    ins = pe.eng.matmul(bank[half(h), duo(h)], S0[half(h), duo(h)], AR[half(h), h // 2, tt, 1, o],
                                        start=False, stop=h == other[-1])
                ins.then_inc(full["A"][j % 4], 1)
            pe.wait_ge(freed["A"][j % 4], pe.frees(j))
            pe_sums(pe, yr)
            pe.wait_ge(v_pe, pe.next(v_pe))
            plan[f"variance{l}"] = pe.job["V"]
            pe_sums(pe, Kf)
            pe_heads(pe, c_items(l), two(sqr))
            j = pe.take("A")
            pe.wait_ge(freed["A"][j % 4], pe.opens(j))
            bank = banks["A"][j % 4]
            for tt in range(2):
                ins = pe.eng.transpose(bank[:, P * tt:P * tt + P], fs[:, SC, P * tt:P * tt + P], cat["ident"])
            ins.then_inc(full["A"][j % 4], 1)
            uk, uv = par(f"uk_{l}", 0, 384), par(f"uv_{l}", 0, 384)
            for h in range(6):
                j = pe.take("A")
                pe.wait_ge(freed["A"][j % 4], pe.opens(j))
                bank = banks["A"][j % 4]
                pe.eng.matmul(bank[:, 0:T], uk[half(h), P * (h // 2):P * (h // 2) + P], fs[half(h), SQ + h // 2, :],
                                      start=True, stop=True).then_inc(full["A"][j % 4], 1)
            for tt in range(2):
                for h in range(8):
                    jj = pe.take("V")
                    pe.wait_ge(freed["V"][jj % 4], pe.opens(jj))
                    bank = banks["V"][jj % 4]
                    pe.eng.matmul(bank[:, 0:T], fs[half(h), SIQ + h // 2, P * tt:P * tt + P], fs[half(h), SIK, :],
                                          start=True, stop=True).then_inc(full["V"][jj % 4], 1)
            pe.wait_ge(freed["A"][j % 4], pe.frees(j))
            pe_att(pe, att2(), W2)
            pe.wait_ge(freed["A"][(pe.job["A"] - 1) % 4], pe.frees(pe.job["A"] - 1))
            for t in range(3):
                j = pe.take("A")
                pe.wait_ge(freed["A"][j % 4], pe.opens(j))
                bank = banks["A"][j % 4]
                for h in (2 * t, 2 * t + 1):
                    ins = pe.eng.matmul(bank[half(h), 0:T], uv[:, 64 * h:64 * h + 64], olat[:, h, :], start=True, stop=True)
                ins.then_inc(full["A"][j % 4], 1)
            pe_heads(pe, ret_items(), None)
            for h in range(4):
                j = pe.take("V")
                pe.wait_ge(freed["V"][j % 4], pe.opens(j))
                bank = banks["V"][j % 4]
                q, k = fs[half(h), TQ + h // 2, :], fs[half(h), TK + h // 2, :]
                pe.eng.matmul(bank[:, 0:T], k[:, 0:P], q, start=True, stop=True)
                pe.eng.matmul(bank[:, T:T + P], k[:, P:T], q[:, P:T], start=True, stop=True).then_inc(full["V"][j % 4], 1)
            pe.wait_ge(freed["V"][j % 4], pe.frees(j))
            for t in range(2):
                j = pe.take("A")
                pe.wait_ge(freed["A"][j % 4], pe.opens(j))
                bank = banks["A"][j % 4]
                for h in (2 * t, 2 * t + 1):
                    c = slice(64 * h, 64 * h + 64)
                    pe.eng.matmul(bank[half(h), 0:P], vtr[:, 0, c], sT[:, h, 0:P], start=True, stop=True)
                    pe.eng.matmul(bank[half(h), P:T], vtr[:, 0, c], sT[:, h, P:T], start=True, stop=False)
                    ins = pe.eng.matmul(bank[half(h), P:T], vtr[:, 1, c], sT[:, h, T:T + P], start=False, stop=True)
                ins.then_inc(full["A"][j % 4], 1)
            pe_heads(pe, ret_norms(), two(sqr))
            pe.wait_ge(v_pe, pe.next(v_pe))
            pe_out(pe, T, lambda k: yT[:, k, 0:T])

        def act_mix2(act, l):
            for t in range(26):
                r = slice(0, 24 if t == MV else P)
                act_out(act, fs[r, t, :], rows=r, width=T)
            for tt in range(2):
                act_out(act, iw[:, tt, :], width=8, scale=8 ** -0.5 * 0.125)
            for tt in range(2):
                act_out(act, vtr[:, tt, :], width=T)
            act.wait_ge(v_a, act.next(v_a))
            act.eng.activation(lo[0:32, :], fs[0:32, LORA, :], ACT.Tanh)
            act.eng.activation(lo[32:64, :], fs[32:64, LORA, :], ACT.Copy)
            act.eng.activation(lo[64:P, :], fs[64:P, LORA, :], ACT.Sigmoid).then_inc(a_self, 1)
            act.wait_ge(a_self, act.next(a_self))
            act.eng.sem_inc(a_pe, 1)
            for dst, name in ((sgw, "w0_"), (sa, "a0_"), (gate, None), (sv, "v0_")):
                if dst is sv and not l:
                    continue
                for t in range(3):
                    if name:
                        act_out(act, dst[:, t, :], width=T, func=ACT.Sigmoid, bias=par(f"{name}{l}", t))
                    else:
                        act_out(act, dst[:, t, :], width=T)
            act.wait_ge(v_a, act.next(v_a))
            act.eng.activation(w2[:, :, :], w2[:, :, :], ACT.Sqrt).then_inc(a_self, 1)
            act.wait_ge(a_self, act.next(a_self))
            act.eng.sem_inc(a_v, 1)
            act.wait_ge(v_a, act.next(v_a))
            act.eng.activation(ec[:, :, :], w1[:, :, :], ACT.Exp)
            act.wait_ge(v_a, act.next(v_a))
            act.eng.activation(sgw[:, :, :], w1[:, :, :], ACT.Exp, scale=-1.0)
            act.eng.activation(sv[:, :, :], w2[:, :, :], ACT.Exp).then_inc(a_self, 1)
            act.wait_ge(a_self, act.next(a_self))
            act.eng.sem_inc(a_v, 1)
            for q in range(6):
                act_out(act, tok[:, q, :], width=384)
            for lev in range(LEVELS):
                for q in range(3):
                    act_out(act, Y[:, 4 * q:4 * q + 4, :], width=TC)
            for ci in range(T // RC):
                act_out(act, yr[:, :, RC * ci:RC * ci + RC], width=192)
            for t in range(3):
                act_root(act, plan[f"variance{l}"] + t, Bf[:, t, :], 64, par("gn_eps"))
            act.wait_ge(v_a, act.next(v_a))
            act_heads(act, c_items(l), two(sqr), two(rtr))
            act_out(act, ctok[:, :, :], width=T)
            for h in range(6):
                act_out(act, qlat[:, h, :], width=T, scale=0.125)
            act_att(act, att2(), W2)
            for t in range(3):
                act_out(act, yT[:, 3 + t, 0:T], width=T)
            act_heads(act, ret_items(), None, None)
            for t in range(2):
                j = act_out(act, yT[:, 6 + t, 0:T], width=T)
            act.wait_ge(freed["A"][j % 4], act.frees(j))
            act_heads(act, ret_norms(), two(sqr), two(rtr))
            act.eng.activation(sg[:, :, :], fs[:, TG:TG + 2, :], ACT.Silu).then_inc(a_self, 1)
            act.wait_ge(a_self, act.next(a_self))
            act.eng.sem_inc(a_v, 1)

        def vec_mix2(v, l):
            E = v.eng
            a0 = v.job["A"]
            v.wait_ge(freed["A"][(a0 + 29) % 4], v.frees(a0 + 29))
            v.job["A"] += 30
            spans = [(0, 10, "mu_")] + ([(MV, 1, "vmu_")] if l else [])
            for t0, nt, _ in spans:
                d = diff[:, min(t0, 10):min(t0, 10) + nt, :]
                E.tensor_tensor(d[:, :, 1:T], fs[:, t0:t0 + nt, 0:T - 1], fs[:, t0:t0 + nt, 1:T], ALU.subtract) if t0 == 0 else \
                    E.tensor_tensor(d[0:16, :, 1:T], fs[0:16, t0:t0 + nt, 0:T - 1], fs[0:16, t0:t0 + nt, 1:T], ALU.subtract)
                r = slice(0, P if t0 == 0 else 16)
                E.tensor_scalar(d[r, :, 0:1], fs[r, t0:t0 + nt, 0:1], -1.0, None, ALU.mult).then_inc(v_self, 1)
                v.wait_ge(v_self, v.next(v_self))
            for t0, nt, name in spans:
                r = slice(0, P if t0 == 0 else 16)
                for t in range(nt):
                    x_ = fs[r, t0 + t, :]
                    ins = E.scalar_tensor_tensor(x_, diff[r, min(t0, 10) + t, :], par(f"{name}{l}", t, rows=r), x_, ALU.mult, ALU.add)
            ins.then_inc(v_self, 1)
            v.wait_ge(v_self, v.next(v_self))
            E.sem_inc(v_a, 1)
            k_, r_, v_ = fs[:, RK:RK + 3, :], fs[:, RR:RR + 3, :], fs[:, RV:RV + 3, :]
            for t in range(3):
                ins = E.tensor_scalar(kk[:, t, :], k_[:, t, :], par(f"kk_{l}", t), None, ALU.mult)
            ins.then_inc(v_self, 1)
            v.wait_ge(v_self, v.next(v_self))
            E.tensor_tensor(w1[:, :, :], kk[:, :, :], kk[:, :, :], ALU.mult).then_inc(v_self, 1)
            v.wait_ge(v_self, v.next(v_self))
            v.eng.sem_inc(v_pe, 1)
            for t in range(3):
                j = v.take("V")
                v.wait_ge(full["V"][j % 4], v.fills(j))
                bank = banks["V"][j % 4]
                E.tensor_scalar(w2[:, t, :], bank[:, 0:T], 1e-24, None, ALU.max).then_inc(freed["V"][j % 4], 1)
                v.wait_ge(freed["V"][j % 4], v.frees(j))
            E.sem_inc(v_a, 1)
            v.wait_ge(a_v, v.next(a_v))
            E.reciprocal(w2[:, :, :], w2[:, :, :]).then_inc(v_self, 1)
            v.wait_ge(v_self, v.next(v_self))
            E.tensor_tensor(kk[:, :, :], kk[:, :, :], w2[:, :, :], ALU.mult).then_inc(v_self, 1)
            v.wait_ge(v_self, v.next(v_self))
            n_lo = 12 if l else 9
            v.wait_ge(freed["A"][(v.job["A"] + n_lo - 1) % 4], v.frees(v.job["A"] + n_lo - 1))
            v.job["A"] += n_lo
            for t in range(3):
                ins = E.tensor_scalar(w1[:, t, :], sa[:, t, :], 1.0, par(f"ka_{l}", t), ALU.subtract, ALU.mult)
            ins.then_inc(v_self, 1)
            v.wait_ge(v_self, v.next(v_self))
            E.scalar_tensor_tensor(k_, w1[:, :, :], 1.0, k_, ALU.add, ALU.mult).then_inc(v_self, 1)
            v.wait_ge(v_self, v.next(v_self))
            if l:
                E.tensor_tensor(w2[:, :, :], vfirst[:, :, :], v_, ALU.subtract).then_inc(v_self, 1)
                v.wait_ge(v_self, v.next(v_self))
                E.tensor_tensor(w2[:, :, :], w2[:, :, :], sv[:, :, :], ALU.mult).then_inc(v_self, 1)
                v.wait_ge(v_self, v.next(v_self))
                E.tensor_tensor(v_, v_, w2[:, :, :], ALU.add).then_inc(v_self, 1)
                v.wait_ge(v_self, v.next(v_self))
            else:
                E.tensor_copy(vfirst[:, :, :], v_).then_inc(v_self, 1)
                v.wait_ge(v_self, v.next(v_self))
            E.tensor_scalar(w2[:, :, :], sgw[:, :, :], -DECAY, None, ALU.mult).then_inc(v_self, 1)
            v.wait_ge(v_self, v.next(v_self))
            f2 = "p a b -> p (a b)"
            E.tensor_tensor_scan(w1[:, :, :].rearrange(f2), cat["scanm"], w2[:, :, :].rearrange(f2), 0.0, ALU.mult, ALU.add).then_inc(v_self, 1)
            v.wait_ge(v_self, v.next(v_self))
            E.sem_inc(v_a, 1)
            E.tensor_tensor(w2[:, :, :], w1[:, :, :], w2[:, :, :], ALU.subtract).then_inc(v_self, 1)
            v.wait_ge(v_self, v.next(v_self))
            E.sem_inc(v_a, 1)
            E.tensor_tensor(Bf[:, :, :], kk[:, :, :], sa[:, :, :], ALU.mult).then_inc(v_self, 1)
            v.wait_ge(v_self, v.next(v_self))
            v.wait_ge(a_v, v.next(a_v))
            E.tensor_tensor(Bf[:, :, :], Bf[:, :, :], sgw[:, :, :], ALU.mult)
            E.tensor_tensor(Kf[:, :, :], k_, sgw[:, :, :], ALU.mult)
            by2 = "p (b t) -> p b t"
            for t in range(3):
                E.scalar_tensor_tensor(AR[:, t, :, 0, :], kk[:, t, :].rearrange(by2, b=2), -1.0, sv[:, t, :].rearrange(by2, b=2),
                                       ALU.mult, ALU.mult)
                E.tensor_tensor(AR[:, t, :, 1, :], r_[:, t, :].rearrange(by2, b=2), ec[:, t, :].rearrange(by2, b=2), ALU.mult)
            for t in range(3):
                ins = E.scalar_tensor_tensor(w1[:, t, :], r_[:, t, :], par(f"rk_{l}", t), k_[:, t, :], ALU.mult, ALU.mult)
            ins.then_inc(v_self, 1)
            v.wait_ge(v_self, v.next(v_self))
            v.eng.sem_inc(v_pe, 1)
            for t in range(3):
                j = v.take("V")
                v.wait_ge(full["V"][j % 4], v.fills(j))
                bank = banks["V"][j % 4]
                E.tensor_tensor(k_[:, t, :], bank[:, 0:T], v_[:, t, :], ALU.mult).then_inc(freed["V"][j % 4], 1)
                v.wait_ge(freed["V"][j % 4], v.frees(j))
            for i in range(12):
                j = v.take("V")
                v.wait_ge(full["V"][j % 4], v.fills(j))
                bank = banks["V"][j % 4]
                E.tensor_tensor(prod[:, i, :], bank[:, :], cat["prodm"], ALU.mult).then_inc(freed["V"][j % 4], 1)
                v.wait_ge(freed["V"][j % 4], v.frees(j))
            v.wait_ge(freed["V"][j % 4], v.frees(j))
            E.sem_inc(v_g, 1)
            for m in (Xh, XTh):
                for i in range(12):
                    ins = E.tensor_copy(at(m, i), cat["ident"])
            ins.then_inc(v_self, 1)
            v.wait_ge(v_self, v.next(v_self))
            v.eng.sem_inc(v_pe, 1)
            v.job["A"] += 6 + 3 * LEVELS
            for lev in range(LEVELS):
                for m in ([Xh, XTh] if lev < LEVELS - 1 else [XTh]):
                    for q in range(3):
                        j = v.take("V")
                        v.wait_ge(full["V"][j % 4], v.fills(j))
                        bank = banks["V"][j % 4]
                        dst = m[:, 2 * q:2 * q + 2, :]
                        E.tensor_tensor(dst, dst, bank[:, :].rearrange("p (a b) -> p a b", a=2), ALU.add).then_inc(freed["V"][j % 4], 1)
                        v.wait_ge(freed["V"][j % 4], v.frees(j))
                    if lev < LEVELS - 1:
                        v.wait_ge(freed["V"][j % 4], v.frees(j))
                        E.sem_inc(v_pe, 1)
            v.wait_ge(freed["V"][j % 4], v.frees(j))
            E.memset(S[:, 0, :], 0.0).then_inc(v_self, 1)
            v.wait_ge(v_self, v.next(v_self))
            v.eng.sem_inc(v_pe, 1)
            for ci in range(T // RC):
                o = slice(64 * (ci % 2), 64 * (ci % 2) + 64)
                for dst in (U, SA):
                    j = v.take("V")
                    v.wait_ge(full["V"][j % 4], v.fills(j))
                    bank = banks["V"][j % 4]
                    E.tensor_copy(dst[o, :], bank[o, 0:384]).then_inc(freed["V"][j % 4], 1)
                    v.wait_ge(freed["V"][j % 4], v.frees(j))
                if ci < T // RC - 1:
                    j = v.take("V")
                    v.wait_ge(full["V"][j % 4], v.fills(j))
                    bank = banks["V"][j % 4]
                    S1 = S[:, (ci + 1) % 2, :]
                    if ci:
                        v.wait_ge(full["A"][(v.job["A"] + ci - 1) % 4], v.fills(v.job["A"] + ci - 1))
                    E.tensor_tensor(S1, bank[:, 0:192], S[:, ci % 2, :], ALU.add).then_inc(freed["V"][j % 4], 1)
                    v.wait_ge(freed["V"][j % 4], v.frees(j))
                    for t in range(3):
                        e = RC * ci + RC - 1
                        ins = E.tensor_scalar(S1[:, 64 * t:64 * t + 64], S1[:, 64 * t:64 * t + 64], ec[:, t, e:e + 1], None, ALU.mult)
                    ins.then_inc(v_self, 1)
                    v.wait_ge(v_self, v.next(v_self))
                    v.eng.sem_inc(v_pe, 1)
            v.job["A"] += 4
            for t in range(3):
                j = v.take("V")
                v.wait_ge(full["V"][j % 4], v.fills(j))
                bank = banks["V"][j % 4]
                E.scalar_tensor_tensor(yr[:, t, :], bank[:, 0:T], -1.0 / 64, yr[:, t, :], ALU.mult, ALU.add).then_inc(freed["V"][j % 4], 1)
                v.wait_ge(freed["V"][j % 4], v.frees(j))
            E.tensor_tensor(Kf[:, :, :], yr[:, :, :], yr[:, :, :], ALU.mult).then_inc(v_self, 1)
            v.wait_ge(v_self, v.next(v_self))
            v.eng.sem_inc(v_pe, 1)
            for t in range(3):
                j = v.take("V")
                v.wait_ge(freed["V"][j % 4], v.frees(j))
            E.reciprocal(Bf[:, :, :], Bf[:, :, :]).then_inc(v_self, 1)
            v.wait_ge(v_self, v.next(v_self))
            E.tensor_tensor(yr[:, :, :], yr[:, :, :], Bf[:, :, :], ALU.mult).then_inc(v_self, 1)
            v.wait_ge(v_self, v.next(v_self))
            for t in range(3):
                ins = E.tensor_scalar(yr[:, t, :], yr[:, t, :], par(f"lnw_{l}", t), par(f"lnb_{l}", t), ALU.mult, ALU.add)
            ins.then_inc(v_self, 1)
            v.wait_ge(v_self, v.next(v_self))
            E.tensor_tensor(yr[:, :, :], yr[:, :, :], k_, ALU.add).then_inc(v_self, 1)
            v.wait_ge(v_self, v.next(v_self))
            E.tensor_tensor(yT[:, 0:3, 0:T], yr[:, :, :], gate[:, :, :], ALU.mult).then_inc(v_self, 1)
            v.wait_ge(v_self, v.next(v_self))
            E.sem_inc(v_a, 1)
            vec_heads(v, c_items(l), two(rtr), inr, ror)
            v.job["A"] += 7
            for tt in range(2):
                for h in range(8):
                    j = v.take("V")
                    v.wait_ge(full["V"][j % 4], v.fills(j))
                    bank = banks["V"][j % 4]
                    dst = tmp[:, :] if h else acc[:, tt, :]
                    E.tensor_scalar(dst, bank[:, 0:T], 0.0, iw[:, tt, h:h + 1], ALU.max, ALU.mult).then_inc(freed["V"][j % 4], 1)
                    v.wait_ge(freed["V"][j % 4], v.frees(j))
                    if h:
                        E.tensor_tensor(acc[:, tt, :], acc[:, tt, :], tmp[:, :], ALU.add).then_inc(v_self, 1)
                        v.wait_ge(v_self, v.next(v_self))
            for tt in range(2):
                causal = cat["causal"][:, tt * T:(tt + 1) * T]
                w = acc[:, tt, :]
                E.tensor_tensor(w, w, causal, ALU.add).then_inc(v_self, 1)
                v.wait_ge(v_self, v.next(v_self))
                for _ in range(TOPK // 8):
                    E.max(top8[:, :], w).then_inc(v_self, 1)
                    v.wait_ge(v_self, v.next(v_self))
                    E.match_replace(w, top8[:, :], w, TAKEN).then_inc(v_self, 1)
                    v.wait_ge(v_self, v.next(v_self))
                E.tensor_scalar(w, w, TAKEN / 2, NEG, ALU.is_gt, ALU.mult).then_inc(v_self, 1)
                v.wait_ge(v_self, v.next(v_self))
                E.tensor_tensor(madd[:, tt, :], w, causal, ALU.add).then_inc(v_self, 1)
                v.wait_ge(v_self, v.next(v_self))
            vec_att(v, att2(), W2)
            v.job["A"] += 3
            vec_heads(v, ret_items(), two(rtr), inr, ror)
            for h in range(4):
                j = v.take("V")
                v.wait_ge(full["V"][j % 4], v.fills(j))
                bank = banks["V"][j % 4]
                E.tensor_tensor(sT[:, h, :], bank[:, 0:384], cat["retm"][:, 384 * h:384 * h + 384], ALU.mult).then_inc(freed["V"][j % 4], 1)
                v.wait_ge(freed["V"][j % 4], v.frees(j))
            v.job["A"] += 2
            vec_heads(v, ret_norms(), two(rtr), inr, ror)
            v.wait_ge(a_v, v.next(a_v))
            E.tensor_tensor(yT[:, 6:8, 0:T], yT[:, 6:8, 0:T], sg[:, :, :], ALU.mult).then_inc(v_self, 1)
            v.wait_ge(v_self, v.next(v_self))
            v.eng.sem_inc(v_pe, 1)
            vec_out(v, T, "one")

        NAMES = ["pre", "mod0", "f0a", "mix0", "f0b", "mod1", "f1a", "mix1", "f1b", "g0a", "mix2", "g0b", "g1a", "mix3", "g1b", "end"]
        upto = len(NAMES) if stop is None else NAMES.index(stop) + 1

        def on(name):
            return NAMES.index(name) < upto

        block = ctx.enter_context(nc.Block())

        @block.tensor
        def _(eng):
            pe = Hand(eng, plan)
            plan["writer"] = pe
            for p in "AV":
                for b in range(4):
                    eng.sem_inc(freed[p][b], 1)
            eng.wait_ge(s_par, 16 * 4)
            pe.wait_ge(v_pe, pe.next(v_pe))
            j = pe.take("V")
            pe.wait_ge(freed["V"][j % 4], pe.opens(j))
            bank = banks["V"][j % 4]
            eng.matmul(bank[:, 0:2], ones[128], small[:, 2:4], start=True, stop=True).then_inc(full["V"][j % 4], 1)

            def ffn(name, n, f):
                if on(name):
                    pe_norm(pe, n)
                    pe_ffn(pe, n, f)

            if on("mod0"):
                pe_mod(pe)
            ffn("f0a", TC, F1)
            if on("mix0"):
                eng.wait_ge(s_tab, 16)
                pe_norm(pe, TC)
                pe_mix0(pe)
            ffn("f0b", TC, F1)
            if on("mod1"):
                pe_mod(pe)
            ffn("f1a", TC, F1)
            if on("mix1"):
                pe_norm(pe, TC)
                pe_mix1(pe)
            ffn("f1b", T, F1)
            for l in range(2):
                ffn(f"g{l}a", T, F2)
                if on(f"mix{2 + l}"):
                    pe_norm(pe, T)
                    plan[f"mix{2 + l}"] = pe.job["A"]
                    pe_mix2(pe, l)
                ffn(f"g{l}b", T, F2)
            if on("end"):
                pe_norm(pe, T)

        @block.scalar
        def _(eng):
            act = Hand(eng, plan)
            for dst, src in ((pk, "pack"), (const, "const"), (bmod, "bmod"), (cT, "cT")):
                eng.dma_start(dst[:], A[src]).then_inc(s_par, 16)
            eng.dma_start(xT[:], A["xT"]).then_inc(s_x, 16)
            eng.dma_start(shared[:, 0:sum(w for _, w in SHARED)], A["tab1"]).then_inc(s_tab, 16)
            eng.wait_ge(s_par, 16 * 4)
            act.wait_ge(v_a, act.next(v_a))
            eng.activation(small[:, 5:7], small[:, 5:7], ACT.Exp).then_inc(a_v, 1)
            eng.activation(cT[:], cT[:], ACT.Silu).then_inc(a_self, 1)
            act.wait_ge(a_self, act.next(a_self))
            if on("mod0"):
                eng.sem_inc(a_pe, 1)
                act_mod(act)

            def ffn(name, n, f, m):
                if on(name):
                    act_norm(act, n, m, split=True)
                    act_ffn(act, n, f)

            eng.wait_ge(s_x, 16)
            ffn("f0a", TC, F1, 1)
            if on("mix0"):
                act_norm(act, TC, 4)
                act_mix0(act)
                act.stage()
            ffn("f0b", TC, F1, 7)
            if on("mod1"):
                eng.sem_inc(a_pe, 1)
                act_mod(act)
            ffn("f1a", TC, F1, 1)
            if on("mix1"):
                act_norm(act, TC, 4)
                act_mix1(act)
                act.stage()
            ffn("f1b", T, F1, 7)
            for l in range(2):
                ffn(f"g{l}a", T, F2, None)
                if on(f"mix{2 + l}"):
                    act_norm(act, T, None)
                    act_mix2(act, l)
                    act.stage()
                ffn(f"g{l}b", T, F2, None)
            if on("end"):
                act_norm(act, T, None)

        @block.vector
        def _(eng):
            v = Hand(eng, plan)
            eng.wait_ge(s_par, 16 * 4)
            lam = par("lam", 0, 4)
            eng.tensor_tensor(small[:, 2:3], lam[:, 0:1], lam[:, 1:2], ALU.mult)
            v.eng.tensor_tensor(small[:, 3:4], lam[:, 2:3], lam[:, 3:4], ALU.mult).then_inc(v_pe, 1)
            eng.tensor_scalar(small[:, 4:5], par("sub"), 1.0 - LAM_INIT, None, ALU.mult)
            j = v.take("V")
            v.wait_ge(full["V"][j % 4], v.fills(j))
            bank = banks["V"][j % 4]
            eng.tensor_copy(small[:, 5:7], bank[:, 0:2]).then_inc(freed["V"][j % 4], 1)
            v.wait_ge(freed["V"][j % 4], v.frees(j))
            eng.sem_inc(v_a, 1)
            v.wait_ge(a_v, v.next(a_v))
            eng.tensor_tensor(small[:, 7:8], small[:, 5:6], small[:, 6:7], ALU.subtract).then_inc(v_self, 1)
            v.wait_ge(v_self, v.next(v_self))
            eng.tensor_scalar(small[:, 1:2], small[:, 7:8], LAM_INIT, -1.0, ALU.add, ALU.mult).then_inc(v_self, 1)
            v.wait_ge(v_self, v.next(v_self))
            eng.wait_ge(s_x, 16)

            def ffn(name, n, f, affine, gain, m):
                if on(name):
                    vec_norm(v, n, affine, gain, split=True)
                    vec_ffn(v, n, f, m)

            if on("mod0"):
                vec_mod(v, 0)
            ffn("f0a", TC, F1, 1, None, 2)
            if on("mix0"):
                eng.wait_ge(s_tab, 16)
                vec_norm(v, TC, 4)
                vec_mix0(v)
            ffn("f0b", TC, F1, 7, None, 8)
            if on("mod1"):
                vec_mod(v, 1)
            ffn("f1a", TC, F1, 1, None, 2)
            if on("mix1"):
                vec_norm(v, TC, 4)
                eng.sem_inc(s_biasroom, 1)
                vec_mix1(v)
                eng.sem_inc(s_room, 1)
            ffn("f1b", T, F1, 7, None, 8)
            if on("g0a"):
                eng.wait_ge(s_tab2, 16)
            for l in range(2):
                ffn(f"g{l}a", T, F2, None, f"n1_{l}", None)
                if on(f"mix{2 + l}"):
                    vec_norm(v, T, None, f"nm_{l}")
                    vec_mix2(v, l)
                ffn(f"g{l}b", T, F2, None, f"n2_{l}", None)
            if on("end"):
                vec_norm(v, T, None, "final")

        @block.gpsimd
        def _(eng):
            g = Hand(eng, plan)
            if stop is not None:
                eng.wait_ge(s_tab, 16)
            if on("mix1"):
                eng.wait_ge(s_biasroom, 1)
                eng.dma_start(bias1, A["bias"]).then_inc(s_bias, 16)
            if on("g0a"):
                eng.wait_ge(s_room, 1)
                eng.dma_start(shared[:], A["tab2"]).then_inc(s_tab2, 16)
            for l in range(2):
                if on(f"mix{2 + l}"):
                    first = plan[f"mix{2 + l}"] + 30 + (12 if l else 9) + 6
                    g.wait_ge(v_g, g.next(v_g))
                    for lev in range(LEVELS):
                        if lev:
                            g.wait_ge(full["A"][(first + 3 * lev - 1) % 4], g.fills(first + 3 * lev - 1))
                        mask = cat["levelm"][:, lev * P:(lev + 1) * P]
                        for i in range(12):
                            ins = eng.tensor_tensor(NM[:, i, :], prod[:, i, 0:P], mask, ALU.mult)
                        ins.then_inc(g_pe, 1)

        @block.sync
        def _(eng):
            for s in range(WEIGHT_SLOTS):
                eng.sem_inc(used[s], 1)
            n = n_chunks if stop is None else plan["writer"].job["chunk"]
            whole = n // WEIGHT_SLOTS
            with eng.Fori(0, whole) as i:
                for s in range(WEIGHT_SLOTS):
                    eng.wait_ge(used[s], i + 1)
                    eng.dma_start(ring[:, s, :], A["stream"][bass.ds(i * WEIGHT_SLOTS + s, 1), :, :].rearrange("a p f -> (a p) f"))\
                       .then_inc(landed[s], 16)
            for s in range(n - whole * WEIGHT_SLOTS):
                eng.wait_ge(used[s], whole + 1)
                eng.dma_start(ring[:, s, :], A["stream"][whole * WEIGHT_SLOTS + s, :, :]).then_inc(landed[s], 16)
            if on("end"):
                eng.wait_ge(s_vdone, 1)
                eng.dma_start(A["out"], hT[:, :, 0:T]).then_inc(s_out, 16)
                eng.wait_ge(s_out, 16)

        assert plan["writer"].job["chunk"] == n_chunks or stop is not None


def _feature_major(a):
    a = np.asarray(a).reshape(-1, a.shape[-1])
    c = a.shape[-1]
    out = np.zeros((a.shape[0], -(-c // P) * P), np.float32)
    out[:, :c] = a
    return np.ascontiguousarray(out.reshape(a.shape[0], -1, P).transpose(2, 1, 0))


def _twice(g):
    return np.concatenate([g] * (P // g.shape[0]))[:, None]


def _columns(chunks, w, width=CH):
    kt = w.shape[0] // P
    for c in range(0, w.shape[1], width):
        part = w[:, c:c + width]
        out = np.zeros((P, kt, width), np.float32)
        out[:, :, :part.shape[1]] = part.reshape(kt, P, -1).transpose(1, 0, 2)
        flat = np.zeros((P, CHUNK), np.float32)
        flat[:, :kt * width] = out.reshape(P, -1)
        chunks.append(flat)


def _rows(chunks, w):
    for r in range(0, w.shape[0], CH):
        out = np.zeros((2, P, D), np.float32)
        part = w[r:r + CH]
        out.reshape(-1, D)[:part.shape[0]] = part
        chunks.append(out.transpose(1, 0, 2).reshape(P, -1))


def _ffn(chunks, g, u, d):
    for s in range(0, g.shape[1], SEG):
        for c in range(s, min(s + SEG, g.shape[1]), CH):
            _columns(chunks, g[:, c:c + CH])
            _columns(chunks, u[:, c:c + CH])
        _rows(chunks, d[s:s + SEG])


def _stream(I):
    ch = []
    heads = np.arange(512).reshape(8, 64)
    for l in range(2):
        _columns(ch, I["w_mod"][l])
        _ffn(ch, I["ffn1_w_gate"][l], I["ffn1_w_up"][l], I["ffn1_w_down"][l])
        if l == 0:
            w = I["ab_w_in"][0]
            aq, bq, ak, av, bk, bv = np.split(w, np.cumsum([512, 512, 128, 128, 512]), axis=1)
            pairs = np.concatenate([np.concatenate([heads[h], heads[h + 4]]) for h in range(4)])
            _columns(ch, np.concatenate([aq[:, pairs], bq, ak, bk, av, bv], axis=1))
            _columns(ch, I["ab_w_out"][0])
        else:
            w = I["cd_w_in"][0]
            cq, dq, ckv, kr, dk, dv = np.split(w, np.cumsum([768, 512, 256, 32, 512]), axis=1)
            _columns(ch, np.concatenate([cq, dq, ckv, kr, kr, kr, kr, dk], axis=1))
            _columns(ch, dv)
            uq = I["c_w_uq"][0].reshape(768, 8, 96)
            _columns(ch, np.concatenate([uq[:, :, :64].reshape(768, 512), uq[:, :, 64:].reshape(768, 256)], axis=1))
            ukv = I["c_w_ukv"][0].reshape(256, 8, 128)
            _columns(ch, np.concatenate([ukv[:, :, :64].reshape(256, 512), ukv[:, :, 64:].reshape(256, 512)], axis=1), D)
            _columns(ch, I["cd_w_out"][0])
        _ffn(ch, I["ffn2_w_gate"][l], I["ffn2_w_up"][l], I["ffn2_w_down"][l])
    for l in range(2):
        _ffn(ch, I["ffn1_w_gate_2"][l], I["ffn1_w_up_2"][l], I["ffn1_w_down_2"][l])
        w = I["w_in_2"][l]
        rwkv, q, c, iq, ik, iw, rq, rk, rv, rg = np.split(w, np.cumsum([1280, 384, 128, 512, 64, 8, 256, 256, 256]), axis=1)
        mv = I["rwkv_vres_w_in_2"][0] if l else np.zeros((D, 16), np.float32)
        last = np.concatenate([mv, iw, np.zeros((D, P - 24), np.float32)], axis=1)
        _columns(ch, np.concatenate([rwkv, q, c, iq, ik, ik, rq, rk, rg, last], axis=1))
        _columns(ch, rv)
        _columns(ch, I["w_out_2"][l])
        _ffn(ch, I["ffn2_w_gate_2"][l], I["ffn2_w_up_2"][l], I["ffn2_w_down_2"][l])
    return np.stack(ch)


def _pack(I):
    PK, PW = param_layout()
    out = np.zeros((P, PW), np.float32)

    def put(name, a):
        at, w = PK[name]
        assert a.shape[1] == w, (name, a.shape, w)
        out[:a.shape[0], at:at + w] = a

    for n, key in (("a_q", "a_q_norm"), ("a_k", "a_k_norm"), ("b_q", "b_q_norm"), ("b_k", "b_k_norm"), ("sub", "b_sub_norm"),
                   ("c_qn", "c_q_nope_norm"), ("c_qr", "c_q_rope_norm"), ("c_kn", "c_k_nope_norm"), ("c_kr", "c_k_rope_norm"),
                   ("d_q", "d_q_norm"), ("d_k", "d_k_norm")):
        put(n, _twice(I[key][0]))
    put("sink", np.broadcast_to(I["a_sink"], (P, 8)))
    put("lam", np.stack([I[f"b_lambda_{n}"][0] for n in ("q1", "k1", "q2", "k2")], axis=1))
    put("c_qa", _feature_major(I["c_q_a_norm"])[:, :, 0])
    put("c_kva", _feature_major(I["c_kv_a_norm"])[:, :, 0])
    put("final", _feature_major(I["final_norm_2"][None])[:, :, 0])
    for n, value in (("one", 1.0), ("eps", EPS), ("gn_eps", GN_EPS)):
        put(n, np.full((P, 1), value, np.float32))
    for l in range(2):
        for n, key in (("n1_", "ffn1_norm_2"), ("nm_", "mix_norm_2"), ("n2_", "ffn2_norm_2"), ("mu_", "rwkv_mu_2"),
                       ("w0_", "rwkv_w0_2"), ("a0_", "rwkv_a0_2"), ("kk_", "rwkv_k_k_2"), ("ka_", "rwkv_k_a_2"),
                       ("lnw_", "rwkv_ln_w_2"), ("lnb_", "rwkv_ln_b_2"), ("kv_", "dsa_kv_norm_2")):
            put(f"{n}{l}", _feature_major(I[key][l][None])[:, :, 0])
        put(f"rk_{l}", _feature_major(I["rwkv_r_k_2"][l].reshape(1, -1))[:, :, 0])
        put(f"lora_{l}", np.concatenate([I["rwkv_w2_2"][l], I["rwkv_a2_2"][l], I["rwkv_g2_2"][l]]))
        put(f"uk_{l}", I["dsa_w_uk_2"][l].reshape(3, P, P).transpose(1, 0, 2).reshape(P, 384))
        put(f"uv_{l}", I["dsa_w_uv_2"][l].transpose(1, 0, 2).reshape(P, 384))
        if l:
            put(f"vmu_{l}", _feature_major(I["rwkv_vres_mu_2"][0][None])[:, :, 0])
            put(f"v0_{l}", _feature_major(I["rwkv_v0_2"][0][None])[:, :, 0])
            put(f"v2_{l}", I["rwkv_v2_2"][0])
    return out


def _constants():
    p = np.arange(P)
    parts = {"sel": (p[:, None] % 32 == np.arange(2)[None]) * 1.0, "ident": np.eye(P), "ones128": np.ones((P, P))}
    for g in (64, 32):
        parts[f"ones{g}"] = (p[:, None] // g == p[None] // g) * 1.0
    for h in (32, 16, 8):
        R = np.zeros((P, P))
        for i in p:
            if i % (2 * h) < h:
                R[i, i + h] = -1
            else:
                R[i, i - h] = 1
        parts[f"rot{h}"] = R.T
    return np.concatenate([parts[n] for n, _ in CONST], axis=1).astype(np.float32)


def _axial(nf):
    f32 = np.float32
    i = np.arange(P) % (4 * nf)
    inv = (f32(10000.0) ** (-np.arange(nf, dtype=f32) / f32(nf)))[i % nf]
    t = np.arange(T)
    pos = np.where((i // (2 * nf) == 0)[:, None], (t // 64)[None], (t % 64)[None]).astype(f32)
    ang = pos * inv[:, None]
    cos, sin = np.ones((P, TC), f32), np.zeros((P, TC), f32)
    cos[:, :T], sin[:, :T] = np.cos(ang), np.sin(ang)
    return cos, sin


def _tables():
    f32 = np.float32
    q, k = np.arange(T)[:, None], np.arange(T)[None]
    am = np.where(np.abs(q - k) <= 128, 0.0, NEG).reshape(2, P, T).transpose(1, 0, 2).reshape(P, -1)
    first = np.concatenate([am, *_axial(16), *_axial(8)], axis=1).astype(f32)
    i = np.arange(P) % 32
    theta = f32(10000.0) ** (-np.linspace(0.0, 1.0, 32, dtype=f32))
    ang = theta[i][:, None] * np.arange(T, dtype=f32)[None]
    gamma = np.log(1.0 - 2.0 ** (-5.0 - np.arange(4)))
    d = np.arange(T)[None] - np.arange(P)[:, None]
    one = [np.where(d >= 0, np.exp(np.maximum(d, 0) * g), 0.0) * 0.125 for g in gamma]
    retm = np.concatenate([np.concatenate([m, m[:, :P]], axis=1) for m in one], axis=1)
    s, t = np.arange(P)[:, None], np.arange(P)[None]
    same = s // RC == t // RC
    prodm = np.concatenate([same & (s < t), same & (s <= t)] * 2, axis=1) * 1.0
    levels = []
    for j in range(LEVELS):
        b = 2 << j
        levels.append((s // b == t // b) & (s % b < b // 2) & (t % b >= b // 2))
    scan = np.broadcast_to((np.arange(768) % RC != 0) * 1.0, (P, 768))
    causal = np.where(k <= q, 0.0, NEG).reshape(2, P, T).transpose(1, 0, 2).reshape(P, -1)
    second = np.concatenate([np.cos(ang), np.sin(ang), retm, prodm, np.concatenate(levels, axis=1) * 1.0, scan, causal],
                            axis=1).astype(f32)
    return first, second


def _bias(rpb):
    q, k = np.arange(T)[:, None], np.arange(T)[None]
    start = np.clip(q % 64 - 8, 0, 48)
    inside = (k % 64 >= start) & (k % 64 < start + 16)
    dr = k // 64 - q // 64 + 7
    dc = np.clip(k % 64 - q % 64, -15, 15) + 15
    out = np.full((8, T, T), NEG, np.float32)
    out[:, inside] = rpb[:, dr[inside], dc[inside]]
    return np.ascontiguousarray(out.reshape(8, 2, P, T).transpose(2, 0, 1, 3).reshape(P, 16, T))


def layout(inputs):
    I = {n: np.asarray(a) for n, a in inputs.items()}
    first, second = _tables()
    xt = np.concatenate([I["x"][0], I["ctx"][0]])
    b = [_feature_major(I["b_mod"][l][None])[:, :, 0] for l in range(2)]
    return {
        "stream": _stream(I), "pack": _pack(I), "const": _constants(), "tab1": first, "tab2": second,
        "bias": _bias(I["d_rpb"][0]), "xT": _feature_major(xt), "cT": np.pad(_feature_major(np.stack([I["c"][0], I["c_ctx"]])), ((0, 0), (0, 0), (0, 30))),
        "bmod": np.ascontiguousarray(np.repeat(np.stack(b, axis=1), 2, axis=2)),
    }


def kernel(**inputs):
    import concourse.bacc as bacc
    from concourse.bass_utils import run_bass_kernel_spmd as run

    nc = bacc.Bacc("TRN2", target_bir_lowering=False, num_devices=1)
    arrays = layout(inputs)
    A = {n: nc.dram_tensor(f"in_{n}", a.shape, F32, kind="ExternalInput").ap() for n, a in arrays.items()}
    A["out"] = nc.dram_tensor("out_0", [P, KD, T], F32, kind="ExternalOutput").ap()
    build(nc, A)
    r = run(nc, [{f"in_{n}": a for n, a in arrays.items()}], core_ids=[0])
    out = r.results[0]["out_0"]
    return np.ascontiguousarray(out.transpose(2, 1, 0).reshape(1, T, D))
```

```python
from contextlib import ExitStack, contextmanager

import numpy as np
import concourse.bass as bass
from concourse import mybir

F32 = mybir.dt.float32
ALU = mybir.AluOpType
ACT = mybir.ActivationFunctionType
AX = mybir.AxisListType

P = 128
D = 1024
KD = D // P
T = 256
TC = 512
CH = 256
CHUNK = KD * CH
WEIGHT_SLOTS = 4
N_MOD = 9
F1, F2 = 2816, 2752
SEG = 1024
SEG_TURNS = 2
FR = mybir.dt.float32r
EPS = 1e-6
GN_EPS = 64e-5
NEG = -1e30
TAKEN = -3e38
TOPK = 64
PICKS = TOPK // 8 + 1
LAM_INIT = 0.8 - 0.6
DEEP = 3
LAG = 3
HEADS_R = 6
RC = 64
LEVELS = 6
DECAY = float(np.exp(-0.5))
LORA, MV = 9, 25

AQ, BQ, AK, BK = 0, 4, 8, 9
CQ, DQ, CKV, KR, DK = 0, 6, 10, 12, 13
RR, RK, RV, SQ, SC, SIQ, SIK, TQ, TK, TG = 0, 3, 6, 10, 13, 14, 18, 19, 21, 23


def param_layout():
    widths = [("c", 16), ("a_q", 1), ("a_k", 1), ("b_q", 1), ("b_k", 1), ("sub", 1), ("sink", 8), ("lam", 4),
              ("c_qa", 6), ("c_kva", 2), ("c_qn", 1), ("c_qr", 1), ("c_kn", 1), ("c_kr", 1), ("d_q", 1), ("d_k", 1),
              ("final", 8), ("one", 1), ("eps", 1), ("gn_eps", 1)]
    for l in range(2):
        widths += [(f"{n}{l}", w) for n, w in (
            ("n1_", 8), ("nm_", 8), ("n2_", 8), ("mu_", 10), ("w0_", 3), ("a0_", 3), ("kk_", 3), ("ka_", 3),
            ("rk_", 3), ("lnw_", 3), ("lnb_", 3), ("kv_", 1), ("vmu_", 1), ("v0_", 3),
            ("lora_", 384), ("v2_", 384), ("uk_", 384), ("uv_", 384))]
    out, at = {}, 0
    for n, w in widths:
        out[n] = (at, w)
        at += w
    return out, at


CONST = [("ident", 128), ("ones128", 128), ("ones64", 128), ("ones32", 128), ("rot32", 128), ("rot16", 128),
         ("rot8", 128), ("sel", 2)]
SHARED = [("amask", 512), ("cosh", TC), ("sinh", TC), ("cosm", TC), ("sinm", TC)]
SHARED2 = [("cosr", T), ("sinr", T), ("retm", 4 * 384), ("prodm", 512), ("levelm", LEVELS * 128), ("scanm", 768),
           ("causal", 2 * T)]


class Hand:

    def __init__(self, eng, plan):
        self.eng, self.plan = eng, plan
        self.wait_ge = eng.wait_ge
        self.seen, self.per = {}, {}
        self.turn, self.stages, self.per_turn = None, 0, {}
        self.job = {"A": 0, "V": 0, "chunk": 0, "split": 0}

    def next(self, sem, n=1):
        self.seen[sem] = self.seen.get(sem, 0) + n
        return self.seen[sem] if self.turn is None or not self.per.get(sem) else self.turn * self.per[sem] + self.seen[sem]

    @contextmanager
    def repeat(self, turns, jobs, per=None):
        per = per or {}
        before = dict(self.seen)
        with self.eng.Fori(0, turns) as i:
            self.turn, self.per, self.per_turn = i, per, jobs
            yield i
        for sem, n in self.seen.items():
            assert n - before.get(sem, 0) == per.get(sem, 0), (sem, n - before.get(sem, 0))
        self.turn = None
        for sem, n in per.items():
            self.seen[sem] += n * (turns - 1)
        for kind, n in jobs.items():
            self.job[kind] += n * (turns - 1)

    def take(self, pool):
        self.job[pool] += 1
        return self.job[pool] - 1

    def _turns(self, value, kind="A"):
        return value if self.turn is None else self.turn * (self.per_turn[kind] // 4) + value

    def opens(self, job):
        return self._turns(job // 4 + 1)

    def fills(self, job):
        return self._turns(job // 4 + 1)

    def frees(self, job):
        return self._turns(job // 4 + 2)

    def lands(self, chunk):
        value = 16 * (chunk // WEIGHT_SLOTS + 1)
        return value if self.turn is None else self.turn * (4 * self.per_turn["chunk"]) + value

    def splits(self, chunk):
        return self._turns(chunk // WEIGHT_SLOTS + 2, "chunk")

    def uses(self, split):
        return split if self.turn is None else self.turn * self.per_turn["split"] + split

    def stage(self):
        if self.plan["writer"] is self:
            self.plan[self.stages] = dict(self.job)
        else:
            self.job = dict(self.plan[self.stages])
        self.stages += 1


def build(nc, A, stop=None):
    PK, PW = param_layout()
    n_chunks = A["stream"].shape[0]
    ctx = ExitStack()
    with ctx:
        def sb(name, shape):
            return ctx.enter_context(nc.sbuf_tensor(name, shape, F32))

        def sem(name):
            return ctx.enter_context(nc.semaphore(name))

        xT = sb("xT", [P, KD, TC])
        ring = sb("ring", [P, WEIGHT_SLOTS, CHUNK])
        pk = sb("pk", [P, PW])
        mods = sb("mods", [P, 72, 2])
        bmod = sb("bmod", [P, 2, 144])
        cT = sb("cT", [P, KD, 32])
        const = sb("const", [P, sum(w for _, w in CONST)])
        shared = sb("shared", [P, sum(w for _, w in SHARED2)])
        vfirst = sb("vfirst", [P, 3, T])
        small = sb("small", [P, 64])
        ARENA = 25600
        hT_at = -(-nc.sbuf_base // 32) * 32
        hT = sb("hT", [P, KD, TC])
        arena_at = hT_at + 4 * KD * TC
        arena = sb("arena", [P, ARENA])

        def over(name, at, shape):
            return nc.alloc_sbuf_tensor_at(name, shape, FR, offset=at)

        h_hi = over("h_hi", hT_at, [P, KD, TC])
        h_lo = over("h_lo", arena_at, [P, KD, TC])
        hid_hi = over("hid_hi", arena_at + 4 * 4096, [P, SEG // P, TC])
        hid_lo = over("hid_lo", arena_at + 4 * 8192, [P, SEG // P, TC])
        w_hi = over("w_hi", arena_at + 4 * 12288, [P, 2, CHUNK])
        w_lo = over("w_lo", arena_at + 4 * 16384, [P, 2, CHUNK])

        banks = {p: [ctx.enter_context(nc.psum_tensor(f"bank{p}{b}", [P, 512], F32)) for b in range(4)] for p in "AV"}
        full = {p: [sem(f"full_{p}{b}") for b in range(4)] for p in "AV"}
        freed = {p: [sem(f"freed_{p}{b}") for b in range(4)] for p in "AV"}
        landed = [sem(f"chunk_landed{s}") for s in range(WEIGHT_SLOTS)]
        used = [sem(f"chunk_used{s}") for s in range(WEIGHT_SLOTS)]
        s_par, s_x, s_tab, s_tab2 = sem("params_in"), sem("x_in"), sem("tables1_in"), sem("tables2_in")
        s_bias, s_biasroom, s_room = sem("biases_in"), sem("biases_room"), sem("tables2_room")
        s_out, s_vdone = sem("out_stored"), sem("out_ready")
        v_self, a_self, pe_self = sem("vector_step"), sem("scalar_step"), sem("tensor_step")
        v_pe, a_pe = sem("vector_made_operand"), sem("scalar_made_operand")
        v_a, a_v = sem("vector_made_for_scalar"), sem("scalar_made_for_vector")
        v_g, g_pe = sem("vector_made_for_pool"), sem("pool_made_operand")
        mod_turn = sem("modulation_turn")
        x_made, h_made = sem("x_tiles_made"), sem("h_tile_made")
        head_summed = sem("index_head_summed")
        split_used, hi_made = sem("split_used"), sem("leading_part_made")
        plan = {"writer": None}

        def par(name, i=0, n=1, rows=slice(0, P)):
            at = PK[name][0] + i
            return pk[rows, at:at + n]

        cat = {}
        for tensor, items in ((const, CONST), (shared, SHARED2)):
            at = 0
            for n, w in items:
                cat[n] = tensor[:, at:at + w]
                at += w
        at = 0
        for n, w in SHARED:
            cat[n] = shared[:, at:at + w]
            at += w
        ones = {128: cat["ones128"], 64: cat["ones64"], 32: cat["ones32"]}

        def room(at, *shape):
            n = int(np.prod(shape))
            assert at + n <= ARENA, (at, shape)
            v = arena[:, at:at + n]
            if len(shape) == 2:
                v = v.rearrange("p (a b) -> p a b", a=shape[0])
            if len(shape) == 3:
                v = v.rearrange("p (a b c) -> p a b c", a=shape[0], b=shape[1])
            return v, at + n

        squares, _ = room(0, KD, TC)
        silb, _end = room(20480, 4, TC)
        hid32, _end = room(_end, 2, TC)
        rsum, _end = room(_end, TC)
        cond_rows, _ = room(0, 4, CH)
        side_mods, _ = room(24064, 4 * N_MOD * 4)
        side_rows, _ = room(24064 + 4 * N_MOD * 4, 2, CH)

        def groups(n):
            return [(0, 0)] if n == T else [(0, 0), (1, T)]

        def pe_norm(pe, n):
            pe.stage()
            j = pe.take("V")
            pe.wait_ge(freed["V"][j % 4], pe.opens(j))
            bank = banks["V"][j % 4]
            stream.let_go()
            for k in range(KD):
                if k % 2 == 0:
                    pe.wait_ge(a_pe, pe.next(a_pe))
                ins = stream.mm(pe, bank[:, 0:n], ones[128], squares[:, k, 0:n], k == 0, k == KD - 1)
            ins.then_inc(full["V"][j % 4], 1)

        def act_norm(act, n, affine, split=False):
            act.stage()
            if split:
                act_hi(act, 0)
            for k in range(0, KD, 2):
                act.wait_ge(x_made, act.next(x_made))
                act.eng.activation(squares[:, k:k + 2, 0:n], xT[:, k:k + 2, 0:n], ACT.Square).then_inc(a_pe, 1)
            act_root(act, act.take("V"), rsum[:, 0:n], D, par("eps"))
            for k in range(KD if affine or split else 0):
                act.wait_ge(v_a, act.next(v_a))
                out = silb[:, k % 4, :] if split else hT[:, k, :]
                if affine:
                    for g, o in groups(n):
                        ins = act.eng.activation(out[:, o:o + T], out[:, o:o + T], ACT.Identity,
                                                 bias=mods[:, 8 * (affine - 1) + k, g:g + 1],
                                                 scale=mods[:, 8 * affine + k, g:g + 1])
                if split:
                    if affine:
                        ins.then_inc(a_self, 1)
                        act.wait_ge(a_self, act.next(a_self))
                    act.eng.activation(h_hi[:, k, 0:n], out[:, 0:n], ACT.Copy).then_inc(a_v, 1)
                else:
                    ins.then_inc(h_made, 1)

        def act_hi(act, ahead):
            c, sp = act.job["chunk"] + ahead, act.job["split"] + ahead
            act.wait_ge(landed[c % WEIGHT_SLOTS], act.lands(c))
            if sp:
                act.wait_ge(split_used, act.uses(sp))
            act.eng.activation(w_hi[:, sp % 2, :], ring[:, c % WEIGHT_SLOTS, :], ACT.Copy).then_inc(hi_made, 1)

        def vec_lo(v, ahead):
            c, sp = v.job["chunk"] + ahead, v.job["split"] + ahead
            v.wait_ge(hi_made, v.next(hi_made))
            v.eng.tensor_tensor(w_lo[:, sp % 2, :], ring[:, c % WEIGHT_SLOTS, :], w_hi[:, sp % 2, :].bitcast(F32),
                                ALU.subtract).then_inc(used[c % WEIGHT_SLOTS], 1)

        def act_root(act, job, out, over, eps):
            act.wait_ge(full["V"][job % 4], act.fills(job))
            bank = banks["V"][job % 4]
            act.eng.activation(out, bank[:, 0:out.shape[1]], ACT.Sqrt, bias=eps, scale=1.0 / over).then_inc(freed["V"][job % 4], 1)

        def vec_norm(v, n, affine=None, gain=None, split=False):
            v.stage()
            if split:
                vec_lo(v, 0)
            j = v.take("V")
            v.wait_ge(freed["V"][j % 4], v.frees(j))
            v.eng.reciprocal(rsum[:, 0:n], rsum[:, 0:n]).then_inc(v_self, 1)
            v.wait_ge(v_self, v.next(v_self))
            for k in range(KD + 2 * split):
                if k < KD:
                    out = silb[:, k % 4, 0:n] if split else hT[:, k, 0:n]
                    if affine:
                        ins = v.eng.tensor_tensor(out, xT[:, k, 0:n], rsum[:, 0:n], ALU.mult)
                    else:
                        ins = v.eng.scalar_tensor_tensor(out, xT[:, k, 0:n], par(gain, k), rsum[:, 0:n], ALU.mult, ALU.mult)
                    if affine or split:
                        ins.then_inc(v_self, 1)
                        v.wait_ge(v_self, v.next(v_self))
                        v.eng.sem_inc(v_a, 1)
                    elif gain != "final":
                        ins.then_inc(h_made, 1)
                if split and k >= 2:
                    v.wait_ge(a_v, v.next(a_v))
                    v.eng.tensor_tensor(h_lo[:, k - 2, 0:n], silb[:, (k - 2) % 4, 0:n], h_hi[:, k - 2, 0:n].bitcast(F32),
                                        ALU.subtract).then_inc(h_made, 1)
            if gain == "final":
                ins.then_inc(s_vdone, 1)

        class Stream:

            def __init__(self):
                self.pending, self.held = None, None

            def next(self, pe):
                c = pe.job["chunk"]
                pe.job["chunk"] += 1
                pe.wait_ge(landed[c % WEIGHT_SLOTS], pe.lands(c))
                self.pending, self.held = self.held, c % WEIGHT_SLOTS
                return ring[:, c % WEIGHT_SLOTS, :]

            def mm(self, pe, out, lhsT, rhs, start, stop):
                ins = pe.eng.matmul(out, lhsT, rhs, start=start, stop=stop)
                if self.pending is not None:
                    ins.then_inc(used[self.pending], 1)
                    self.pending = None
                return ins

            def let_go(self):
                self.pending, self.held = self.held, None

        stream = Stream()

        def by_k(chunk, kt=KD, w=CH):
            return chunk[:, 0:kt * w].rearrange("p (k c) -> p k c", k=kt)

        def segment(cols):
            out = []
            for c in range(0, cols, CH):
                tiles = [(q, min(P, cols - c - q)) for q in range(0, min(CH, cols - c), P)]
                out += [("gate", tiles), ("up", tiles)]
            return out + [("down", [(q, min(P, cols - c - q)) for q in range(0, min(CH, cols - c), P)])
                          for c in range(0, cols, CH)]

        PER_SEG = {"A": 12, "V": 12, "chunk": 12, "split": 12}

        def pe_ffn(pe, n, f):
            pe.stage()

            h_tiles = [pe.next(h_made) for _ in range(KD)]

            def products(out, w, wc, rhs, start, stop, first):
                hi, lo = w
                a, b = rhs
                pairs = ((lo, a), (hi, b), (hi, a))
                for q, (l, r) in enumerate(pairs):
                    ins = pe.eng.matmul(out, l[wc], r, start=start and q == 0, stop=stop and q == 2)
                    if first and q == 0:
                        ins.then_inc(split_used, 1)
                return ins

            def run(cols):
                hidden_at = 0
                jobs = None
                chunks = segment(cols)
                for i, (kind, tiles) in enumerate(chunks):
                    c, b = pe.job["chunk"], pe.job["split"] % 2
                    pe.job["chunk"] += 1
                    pe.job["split"] += 1
                    if kind == "down":
                        if jobs is None:
                            jobs = []
                            for p in "AAAAVVVV":
                                j = pe.take(p)
                                pe.wait_ge(freed[p][j % 4], pe.opens(j))
                                jobs.append((p, j))
                            hidden_at = 0
                        pe.wait_ge(v_pe, pe.next(v_pe))
                    pe.wait_ge(used[c % WEIGHT_SLOTS], pe.splits(c))
                    if kind == "down":
                        w = [m[:, b, :].rearrange("p (r c) -> p r c", r=2) for m in (w_hi, w_lo)]
                        for q, (_, rows) in enumerate(tiles):
                            r = slice(0, rows)
                            rhs = [m[r, hidden_at, 0:n] for m in (hid_hi, hid_lo)]
                            last = i == len(chunks) - 1 and q == len(tiles) - 1
                            for t, (p, j) in enumerate(jobs):
                                ins = products(banks[p][j % 4][:, 0:n], w, (r, q, slice(t * P, t * P + P)), rhs,
                                               hidden_at == 0, last, q == 0 and t == 0)
                                if last:
                                    ins.then_inc(full[p][j % 4], 1)
                            hidden_at += 1
                        continue
                    w = [m[:, b, :].rearrange("p (k c) -> p k c", k=KD) for m in (w_hi, w_lo)]
                    p = "A" if kind == "gate" else "V"
                    for q, (col, width) in enumerate(tiles):
                        j = pe.take(p)
                        pe.wait_ge(freed[p][j % 4], pe.opens(j))
                        for k in range(KD):
                            if i == 0 and q == 0:
                                pe.wait_ge(h_made, h_tiles[k])
                            ins = products(banks[p][j % 4][0:width, 0:n], w, (slice(0, P), k, slice(col, col + width)),
                                           [m[:, k, 0:n] for m in (h_hi, h_lo)], k == 0, k == KD - 1, q == 0 and k == 0)
                        ins.then_inc(full[p][j % 4], 1)

            with pe.repeat(SEG_TURNS, PER_SEG, {v_pe: 4}):
                run(SEG)
            run(f - SEG_TURNS * SEG)

        def act_ffn(act, n, f):
            act.stage()

            def run(cols, end):
                at, chunks = 0, segment(cols)
                for i, (kind, tiles) in enumerate(chunks):
                    if not end or i < len(chunks) - 1:
                        act_hi(act, 1)
                    act.job["chunk"] += 1
                    act.job["split"] += 1
                    if kind == "gate":
                        for _, w in tiles:
                            j = act.take("A")
                            act.wait_ge(full["A"][j % 4], act.fills(j))
                            act.eng.activation(silb[0:w, j % 4, 0:n], banks["A"][j % 4][0:w, 0:n],
                                               ACT.Silu).then_inc(freed["A"][j % 4], 1)
                    if kind == "up":
                        for q, (_, w) in enumerate(tiles):
                            act.wait_ge(v_a, act.next(v_a))
                            act.eng.activation(hid_hi[0:w, at, 0:n], hid32[0:w, q, 0:n], ACT.Copy).then_inc(a_v, 1)
                            at += 1
                act.job["A"] += 4

            with act.repeat(SEG_TURNS, PER_SEG, {v_a: 8}):
                run(SEG, False)
            run(f - SEG_TURNS * SEG, True)

        def vec_ffn(v, n, f, m):
            v.stage()

            def run(cols, end):
                at, chunks = 0, segment(cols)
                a0 = v.job["A"]
                for i, (kind, tiles) in enumerate(chunks):
                    if not end or i < len(chunks) - 1:
                        vec_lo(v, 1)
                    v.job["chunk"] += 1
                    v.job["split"] += 1
                    if kind != "up":
                        continue
                    for q, (_, w) in enumerate(tiles):
                        jv, ja = v.take("V"), v.take("A")
                        v.wait_ge(freed["A"][ja % 4], v.frees(ja))
                        v.wait_ge(full["V"][jv % 4], v.fills(jv))
                        v.eng.tensor_tensor(hid32[0:w, q, 0:n], silb[0:w, ja % 4, 0:n], banks["V"][jv % 4][0:w, 0:n],
                                            ALU.mult).then_inc(freed["V"][jv % 4], 1)
                        v.wait_ge(freed["V"][jv % 4], v.frees(jv))
                        v.eng.sem_inc(v_a, 1)
                    for q, (_, w) in enumerate(tiles):
                        v.wait_ge(a_v, v.next(a_v))
                        v.eng.tensor_tensor(hid_lo[0:w, at, 0:n], hid32[0:w, q, 0:n], hid_hi[0:w, at, 0:n].bitcast(F32),
                                            ALU.subtract).then_inc(v_self, 1)
                        v.wait_ge(v_self, v.next(v_self))
                        at += 1
                    v.eng.sem_inc(v_pe, 1)
                add_to_x(v, [("A", v.take("A")) for _ in range(4)] + [("V", v.take("V")) for _ in range(4)], n, m, end)

            with v.repeat(SEG_TURNS, PER_SEG, {hi_made: 12, a_v: 8, v_self: 8}):
                run(SEG, False)
            run(f - SEG_TURNS * SEG, True)

        def add_to_x(v, jobs, n, m, last):
            for c, (p, j) in enumerate(jobs):
                v.wait_ge(full[p][j % 4], v.fills(j))
                bank = banks[p][j % 4]
                for g, o in groups(n):
                    s = 0.5 if m is None else 1.0 if m == "one" else mods[:, 8 * m + c, g:g + 1]
                    ins = v.eng.scalar_tensor_tensor(xT[:, c, o:o + T], bank[:, o:o + T], s, xT[:, c, o:o + T],
                                                     ALU.mult, ALU.add)
                ins.then_inc(freed[p][j % 4], 1)
                v.wait_ge(freed[p][j % 4], v.frees(j))
                if last and c % 2:
                    v.eng.sem_inc(x_made, 1)

        def pe_tiles(pe, chunk, kt, plan_, rhs_of, first=False):
            for q, (c, w, n) in enumerate(plan_):
                j = pe.take("A")
                pe.wait_ge(freed["A"][j % 4], pe.opens(j))
                bank = banks["A"][j % 4]
                for k in range(kt):
                    if first and q == 0:
                        pe.wait_ge(h_made, pe.next(h_made))
                    ins = stream.mm(pe, bank[0:w, 0:n], chunk[:, k, c:c + w], rhs_of(k, n), k == 0, k == kt - 1)
                ins.then_inc(full["A"][j % 4], 1)

        def pe_rows(pe, chunk, kt, c, w, n, lhs_of):
            for tt in range(n // P):
                j = pe.take("A")
                pe.wait_ge(freed["A"][j % 4], pe.opens(j))
                bank = banks["A"][j % 4]
                for k in range(kt):
                    ins = stream.mm(pe, bank[:, 0:w], lhs_of(k, tt), chunk[:, k, c:c + w], k == 0, k == kt - 1)
                ins.then_inc(full["A"][j % 4], 1)

        def act_out(act, dst, rows=slice(0, P), width=None, func=ACT.Copy, bias=None, scale=1.0):
            j = act.take("A")
            act.wait_ge(full["A"][j % 4], act.fills(j))
            bank = banks["A"][j % 4]
            src = bank[rows, 0:width]
            if len(dst.shape) == 3:
                src = src.rearrange("p (a b) -> p a b", a=dst.shape[1])
            if bias is None:
                ins = act.eng.activation(dst, src, func, scale=scale)
            else:
                ins = act.eng.activation(dst, src, func, bias=bias, scale=scale)
            ins.then_inc(freed["A"][j % 4], 1)
            return j

        def pe_heads(pe, items, sq):
            pe.stage()
            for i in range(len(items) + 1):
                pe_heads_step(pe, items, sq, i)
            pe.wait_ge(v_pe, pe.next(v_pe))

        def pe_heads_step(pe, items, sq, i):
            if i < len(items):
                it = items[i]
                if it["size"]:
                    j = pe.take("V")
                    pe.wait_ge(freed["V"][j % 4], pe.opens(j))
                    bank = banks["V"][j % 4]
                    pe.wait_ge(a_pe, pe.next(a_pe))
                    for q in range(len(it["tiles"])):
                        ins = pe.eng.matmul(bank[:, 0:it["n"]], ones[it["size"]], sq[i % 2][:, q * it["n"]:(q + 1) * it["n"]],
                                            start=q == 0, stop=q == len(it["tiles"]) - 1)
                    ins.then_inc(full["V"][j % 4], 1)
            if i and items[i - 1]["rot"]:
                it = items[i - 1]
                for tile in it["tiles"]:
                    j = pe.take("V")
                    pe.wait_ge(freed["V"][j % 4], pe.opens(j))
                    bank = banks["V"][j % 4]
                    pe.wait_ge(v_pe, pe.next(v_pe))
                    pe.eng.matmul(bank[:, 0:it["n"]], cat[it["rot"][0]], tile, start=True, stop=True).then_inc(full["V"][j % 4], 1)

        def heads_jobs(items, base):
            norm, rot = {}, {}
            for i in range(len(items) + 1):
                if i < len(items) and items[i]["size"]:
                    norm[i] = base
                    base += 1
                if i and items[i - 1]["rot"]:
                    rot[i - 1] = [base + q for q in range(len(items[i - 1]["tiles"]))]
                    base += len(items[i - 1]["tiles"])
            return norm, rot, base

        def act_heads(act, items, sq, rt):
            act.stage()
            norm, _, _ = heads_jobs(items, act.job["V"])
            for i in range(len(items) + 1):
                act_heads_step(act, items, sq, rt, norm, i)
            act.wait_ge(v_a, act.next(v_a, min(2, len(norm))))

        def act_heads_step(act, items, sq, rt, norm, i):
            if i in norm:
                n = items[i]["n"]
                if i - 2 in norm:
                    act.wait_ge(full["V"][(norm[i - 2]) % 4], act.fills(norm[i - 2]))
                for q, tile in enumerate(items[i]["tiles"]):
                    ins = act.eng.activation(sq[i % 2][:, q * n:(q + 1) * n], tile, ACT.Square)
                ins.then_inc(a_self, 1)
                act.wait_ge(a_self, act.next(a_self))
                act.eng.sem_inc(a_pe, 1)
            if i - 1 in norm:
                it = items[i - 1]
                if i - 3 in norm:
                    act.wait_ge(v_a, act.next(v_a))
                act_root(act, norm[i - 1], rt[(i - 1) % 2][:, 0:it["n"]], it["over"], par("eps"))

        def vec_heads(v, items, rt, inv_t, rot_t):
            v.stage()
            norm, rot, end = heads_jobs(items, v.job["V"])

            def scale(i):
                it = items[i]
                n = it["n"]
                if it["size"]:
                    v.wait_ge(freed["V"][norm[i] % 4], v.frees(norm[i]))
                    v.eng.reciprocal(inv_t[:, 0:n], rt[i % 2][:, 0:n]).then_inc(v_self, 1)
                    v.wait_ge(v_self, v.next(v_self))
                    v.eng.sem_inc(v_a, 1)
                    for q, tile in enumerate(it["tiles"]):
                        ins = v.eng.scalar_tensor_tensor(tile, tile, it["gains"][q], inv_t[:, 0:n], ALU.mult, ALU.mult)
                        if it["rot"]:
                            ins.then_inc(v_self, 1)
                            v.wait_ge(v_self, v.next(v_self))
                            v.eng.sem_inc(v_pe, 1)
                        elif q == len(it["tiles"]) - 1:
                            ins.then_inc(v_self, 1)
                            v.wait_ge(v_self, v.next(v_self))
                elif it["rot"]:
                    for _ in it["tiles"]:
                        v.eng.sem_inc(v_pe, 1)

            def rotate(i):
                it = items[i]
                n = it["n"]
                for q, tile in enumerate(it["tiles"]):
                    v.wait_ge(full["V"][rot[i][q] % 4], v.fills(rot[i][q]))
                    bank = banks["V"][rot[i][q] % 4]
                    _, cos, sin = it["rot"]
                    v.eng.tensor_tensor(rot_t[:, 0:n], bank[:, 0:n], cat[sin][:, 0:n], ALU.mult).then_inc(freed["V"][rot[i][q] % 4], 1)
                    v.wait_ge(freed["V"][rot[i][q] % 4], v.frees(rot[i][q]))
                    v.eng.tensor_tensor(tile, tile, cat[cos][:, 0:n], ALU.mult).then_inc(v_self, 1)
                    v.wait_ge(v_self, v.next(v_self))
                    v.eng.tensor_tensor(tile, tile, rot_t[:, 0:n], ALU.add).then_inc(v_self, 1)
                    v.wait_ge(v_self, v.next(v_self))

            for i in range(len(items) + 1):
                if i < len(items):
                    scale(i)
                if i and items[i - 1]["rot"]:
                    rotate(i - 1)
            v.eng.sem_inc(v_pe, 1)
            v.job["V"] = end

        def item(tiles, n, size, over=None, gains=None, rot=None):
            return {"tiles": tiles, "n": n, "size": size, "over": over or size, "gains": gains, "rot": rot}

        def att_steps(gs, side):
            us = flat(gs)

            def chunk_at(i):
                c = i - i // 4
                return c if i % 4 < 3 and c < side else None

            steps = []
            for i in range(len(us) + LAG + 1):
                done = i - LAG - 1
                steps.append({"front": i if i < len(us) else None,
                              "turned": i - LAG if 0 <= i - LAG < len(us) else None,
                              "group": us[done][0] if done >= 0 and us[done][1] == len(gs[us[done][0]]["units"]) - 1 else None,
                              "rows": chunk_at(i), "sums": chunk_at(i - 1) if i else None})
            assert not side or sum(st["sums"] is not None for st in steps) == side
            return steps

        def att_jobs(gs, base, side):
            jobs = {}
            for i, st in enumerate(att_steps(gs, side)):
                for kind in ("rows", "turned", "group", "sums"):
                    if st[kind] is not None:
                        jobs[kind, st[kind]] = base
                        base += 1
            return jobs, base

        def flat(gs):
            return [(g, qi, un) for g, grp in enumerate(gs) for qi, un in enumerate(grp["units"])]

        def pe_att(pe, gs, W, side=0):
            pe.stage()
            us = flat(gs)
            for st in att_steps(gs, side):
                u = st["front"]
                if u is not None:
                    for parts in us[u][2]["maps"]:
                        j = pe.take("V")
                        pe.wait_ge(freed["V"][j % 4], pe.opens(j))
                        bank = banks["V"][j % 4]
                        for i, (q, k) in enumerate(parts):
                            ins = pe.eng.matmul(bank[:, 0:us[u][2]["nk"]], q, k, start=i == 0, stop=i == len(parts) - 1)
                        ins.then_inc(full["V"][j % 4], 1)
                if st["rows"] is not None:
                    w = by_k(stream.next(pe))
                    jr = pe.take("A")
                    pe.wait_ge(freed["A"][jr % 4], pe.opens(jr))
                    for k in range(KD):
                        g = slice(32 * (k % 4), 32 * (k % 4) + 32)
                        ins = stream.mm(pe, banks["A"][jr % 4][g, 0:CH], cT[:, k, :], w[:, k, :], k < 4, k >= 4)
                    ins.then_inc(full["A"][jr % 4], 1)
                if st["turned"] is not None:
                    u = st["turned"]
                    un = us[u][2]
                    j = pe.take("A")
                    pe.wait_ge(freed["A"][j % 4], pe.opens(j))
                    bank = banks["A"][j % 4]
                    pe.wait_ge(v_pe, pe.next(v_pe))
                    for c in range(un["nk"] // P):
                        ins = pe.eng.transpose(bank[:, c * P:(c + 1) * P], W["pn"][:, u % DEEP, c * P:(c + 1) * P], cat["ident"])
                    ins.then_inc(full["A"][j % 4], 1)
                if st["group"] is not None:
                    g = st["group"]
                    pe.wait_ge(freed["A"][turned % 4], pe.frees(turned))
                    jo = pe.take("A")
                    pe.wait_ge(freed["A"][jo % 4], pe.opens(jo))
                    bank = banks["A"][jo % 4]
                    n = P * len(gs[g]["units"])
                    r = gs[g]["rows"]
                    for c, val in enumerate(gs[g]["vals"]):
                        ins = pe.eng.matmul(bank[r, 0:n], val, W["pT"][:, g % 2, c, 0:n], start=c == 0,
                                            stop=c == len(gs[g]["vals"]) - 1)
                    ins.then_inc(full["A"][jo % 4], 1)
                if st["turned"] is not None:
                    turned = j
                if st["sums"] is not None:
                    pe.wait_ge(freed["A"][rows % 4], pe.frees(rows))
                    js = pe.take("A")
                    pe.wait_ge(freed["A"][js % 4], pe.opens(js))
                    for t in range(2):
                        ins = pe.eng.matmul(banks["A"][js % 4][:, 2 * t:2 * t + 2], side_rows[:, st["sums"] % 2, t * P:(t + 1) * P],
                                            cat["sel"], start=True, stop=True)
                    ins.then_inc(full["A"][js % 4], 1)
                if st["rows"] is not None:
                    rows = jr

        def act_att(act, gs, W, side=0):
            act.stage()
            us = flat(gs)
            jobs, end = att_jobs(gs, act.job["A"], side)
            scores = act.job["V"]
            for st in att_steps(gs, side):
                u = st["front"]
                if st["rows"] is not None:
                    c, j = st["rows"], jobs["rows", st["rows"]]
                    act.job["chunk"] += 1
                    act.wait_ge(full["A"][j % 4], act.fills(j))
                    act.eng.activation(side_rows[:, c % 2, :], banks["A"][j % 4][:, 0:CH], ACT.Copy).then_inc(freed["A"][j % 4], 1)
                if u is not None:
                    un = us[u][2]
                    for m in range(len(un["maps"])):
                        act.wait_ge(v_a, act.next(v_a))
                        s = W["s"][:, u % DEEP, m, 0:un["nk"]]
                        nm = W["st"][:, u % DEEP, m:m + 1]
                        if un["sink"] is not None:
                            act.eng.activation(W["st"][:, u % DEEP, 4:5], un["sink"], ACT.Exp, bias=nm)
                        total = W["st"][:, u % DEEP, 2 + m:3 + m]
                        if un["mask"] is None:
                            act.eng.activation(s, banks["V"][scores % 4][:, 0:un["nk"]], ACT.Exp, bias=nm, scale=un["scale"],
                                               accum_out=total).then_inc(freed["V"][scores % 4], 1)
                            act.wait_ge(freed["V"][scores % 4], act.frees(scores))
                        else:
                            act.eng.activation(s, s, ACT.Exp, bias=nm, accum_out=total).then_inc(a_self, 1)
                            act.wait_ge(a_self, act.next(a_self))
                        act.eng.sem_inc(a_v, 1)
                        scores += 1
                if st["turned"] is not None:
                    u = st["turned"]
                    g, qi, un = us[u]
                    nc_ = un["nk"] // P
                    j = jobs["turned", u]
                    act.wait_ge(full["A"][j % 4], act.fills(j))
                    act.eng.activation(W["pT"][:, g % 2, 0:nc_, qi * P:(qi + 1) * P],
                                       banks["A"][j % 4][:, 0:nc_ * P].rearrange("p (c q) -> p c q", c=nc_),
                                       ACT.Copy).then_inc(freed["A"][j % 4], 1)
                if st["group"] is not None:
                    g = st["group"]
                    j = jobs["group", g]
                    act.wait_ge(full["A"][j % 4], act.fills(j))
                    act.eng.activation(gs[g]["dst"], banks["A"][j % 4][gs[g]["rows"], 0:P * len(gs[g]["units"])],
                                       ACT.Copy).then_inc(freed["A"][j % 4], 1)
                if st["sums"] is not None:
                    c, j = st["sums"], jobs["sums", st["sums"]]
                    act.wait_ge(full["A"][j % 4], act.fills(j))
                    act.eng.activation(side_mods[:, 4 * c:4 * c + 4], banks["A"][j % 4][:, 0:4], ACT.Copy).then_inc(freed["A"][j % 4], 1)
            act.job["A"] = end

        def vec_att(v, gs, W, side=0):
            v.stage()
            us = flat(gs)
            jobs, end = att_jobs(gs, v.job["A"], side)
            v.job["chunk"] += side
            for u in range(len(us) + DEEP - 1):
                if u < len(us):
                    un = us[u][2]
                    nk = un["nk"]
                    for m in range(len(un["maps"])):
                        j = v.take("V")
                        v.wait_ge(full["V"][j % 4], v.fills(j))
                        bank = banks["V"][j % 4]
                        s = W["s"][:, u % DEEP, m, :]
                        nm = W["st"][:, u % DEEP, m:m + 1]
                        if un["mask"] is not None:
                            if nk > T:
                                v.eng.tensor_scalar(s[:, T:nk], bank[:, T:nk], un["scale"], None, ALU.mult)
                            v.eng.scalar_tensor_tensor(s[:, 0:T], bank[:, 0:T], un["scale"], un["mask"], ALU.mult,
                                                       ALU.add).then_inc(freed["V"][j % 4], 1)
                            v.wait_ge(freed["V"][j % 4], v.frees(j))
                            v.eng.tensor_reduce(nm, s[:, 0:nk], AX.X, ALU.max, negate=True).then_inc(v_self, 1)
                        else:
                            v.eng.tensor_reduce(nm, bank[:, 0:nk], AX.X, ALU.max, negate=True).then_inc(v_self, 1)
                            v.wait_ge(v_self, v.next(v_self))
                            v.eng.tensor_scalar(nm, nm, un["scale"], None, ALU.mult).then_inc(v_self, 1)
                        v.wait_ge(v_self, v.next(v_self))
                        if un["sink"] is not None:
                            v.eng.scalar_tensor_tensor(nm, un["sink"], -1.0, nm, ALU.mult, ALU.min).then_inc(v_self, 1)
                            v.wait_ge(v_self, v.next(v_self))
                        v.eng.sem_inc(v_a, 1)
                done = u - DEEP + 1
                if done >= 0:
                    g, qi, un = us[done]
                    b = done % DEEP
                    nk = un["nk"]
                    nm_ = len(un["maps"])
                    v.wait_ge(a_v, v.next(a_v, nm_))
                    st = W["st"]
                    if un["sink"] is not None:
                        v.eng.tensor_tensor(st[:, b, 2:3], st[:, b, 2:3], st[:, b, 4:5], ALU.add).then_inc(v_self, 1)
                        v.wait_ge(v_self, v.next(v_self))
                    v.eng.reciprocal(st[:, b, 5:5 + nm_], st[:, b, 2:2 + nm_]).then_inc(v_self, 1)
                    v.wait_ge(v_self, v.next(v_self))
                    if done >= DEEP:
                        j = jobs["turned", done - DEEP]
                        v.wait_ge(full["A"][j % 4], v.fills(j))
                    pn = W["pn"][:, b, 0:nk]
                    if nm_ == 1:
                        v.eng.tensor_scalar(pn, W["s"][:, b, 0, 0:nk], st[:, b, 5:6], None, ALU.mult).then_inc(v_self, 1)
                        v.wait_ge(v_self, v.next(v_self))
                        v.eng.sem_inc(v_pe, 1)
                    else:
                        v.eng.tensor_scalar(pn, W["s"][:, b, 0, 0:nk], st[:, b, 5:6], None, ALU.mult)
                        v.eng.tensor_tensor(st[:, b, 6:7], st[:, b, 6:7], small[:, 1:2], ALU.mult).then_inc(v_self, 1)
                        v.wait_ge(v_self, v.next(v_self))
                        v.eng.scalar_tensor_tensor(pn, W["s"][:, b, 1, 0:nk], st[:, b, 6:7], pn, ALU.mult, ALU.add).then_inc(v_self, 1)
                        v.wait_ge(v_self, v.next(v_self))
                        v.eng.sem_inc(v_pe, 1)
            v.job["A"] = end

        fm0, e0 = room(0, 13, TC)
        vt0, e0 = room(e0, 4, 640)
        sq0a, e1 = room(e0, TC)
        sq0b, e1 = room(e1, TC)
        rt0, e1 = room(e1, 2, TC)
        in0, e1 = room(e1, TC)
        ro0, e1 = room(e1, TC)
        W0 = {}
        W0["s"], e1 = room(e0, DEEP, 2, TC)
        W0["pn"], e1 = room(e1, DEEP, TC)
        W0["pT"], e1 = room(e1, 2, 4 * T)
        W0["pT"] = W0["pT"].rearrange("p g (c q) -> p g c q", c=4)
        W0["st"], e1 = room(e1, DEEP, 8)
        sqy, e2 = room(e0, 2, TC)
        rty, e2 = room(e2, 2, TC)
        iny, e2 = room(e2, TC)
        yT = hT

        def rope_items0():
            rope = ("rot16", "cosh", "sinh")
            its = []
            for t in range(13):
                g = "a_q" if t < BQ else "b_q" if t < AK else "a_k" if t < BK else "b_k"
                its.append(item([fm0[:, t, :]], TC, 64, gains=[par(g)], rot=rope))
            return its

        def att0():
            gs = []
            for side in range(2):
                nk, k0 = (TC, 0) if side == 0 else (T, T)
                kts = range(4) if side == 0 else range(2, 4)
                for h in range(8):
                    r = slice(64 * (h // 4), 64 * (h // 4) + 64)
                    units = []
                    for qt in range(2):
                        q0 = T * side + P * qt
                        units.append({"maps": [[(fm0[r, AQ + h % 4, q0:q0 + P], fm0[r, AK, k0:k0 + nk])]], "nk": nk,
                                      "scale": 0.125, "sink": par("sink", h),
                                      "mask": cat["amask"][:, qt * T:(qt + 1) * T] if side == 0 else None})
                    o = slice(64 * (h % 2), 64 * (h % 2) + 64)
                    gs.append({"units": units, "rows": o, "dst": yT[o, h // 2, T * side:T * side + T],
                               "vals": [vt0[:, kt, 64 * (h // 4):64 * (h // 4) + 64] for kt in kts]})
                for h in range(4):
                    units = []
                    for qt in range(2):
                        q0 = T * side + P * qt
                        maps = [[(fm0[64 * m:64 * m + 64, BQ + h, q0:q0 + P], fm0[64 * m:64 * m + 64, BK + h, k0:k0 + nk])]
                                for m in range(2)]
                        units.append({"maps": maps, "nk": nk, "scale": 0.125, "sink": None, "mask": None})
                    gs.append({"units": units, "rows": slice(0, P), "dst": yT[:, 4 + h, T * side:T * side + T],
                               "vals": [vt0[:, kt, 128 + 128 * h:256 + 128 * h] for kt in kts]})
            return gs

        def sub_items():
            return [item([yT[:, 4 + h, :]], TC, 128, gains=[small[:, 4:5]]) for h in range(4)]

        fm1, f0 = room(0, 17, TC)
        vt1, f0 = room(f0, 4, 512)
        bias1, _ = room(16000, 16, T)
        sq1, f1_ = room(f0, 2, 3 * TC)
        rt1, f1_ = room(f1_, 2, TC)
        in1, f1_ = room(f1_, TC)
        ro1, f1_ = room(f1_, TC)
        W1 = {}
        W1["s"], g0 = room(f0, DEEP, TC)
        W1["s"] = W1["s"].rearrange("p u (m k) -> p u m k", m=1)
        W1["pn"], g0 = room(g0, DEEP, TC)
        W1["pT"], g0 = room(g0, 2, 4 * T)
        W1["pT"] = W1["pT"].rearrange("p g (c q) -> p g c q", c=4)
        W1["st"], g0 = room(g0, DEEP, 8)

        qn1 = hT[:, 0:2, :].rearrange("p a (b t) -> p (a b) t", b=2)
        qr1 = hT[:, 2, :].rearrange("p (b t) -> p b t", b=2)
        kn1 = hT[:, 3:7, :]
        vm1 = fm1[:, CQ:CQ + 4, :]
        ym1 = xT[:, :, T:TC]

        def items1a():
            its = [item([fm1[:, CQ + t, 0:T] for t in range(6)], T, 128, 768, [par("c_qa", t) for t in range(6)])]
            its += [item([fm1[:, DQ + t, 0:T]], T, 64, gains=[par("d_q")]) for t in range(4)]
            its += [item([fm1[:, CKV + t, :] for t in range(2)], TC, 128, 256, [par("c_kva", t) for t in range(2)]),
                    item([fm1[:, KR, :]], TC, 32, gains=[par("c_kr")], rot=("rot8", "cosm", "sinm"))]
            its += [item([fm1[:, DK + t, :]], TC, 64, gains=[par("d_k")]) for t in range(4)]
            return its

        READY1 = [5, 6, 7, 8, 9, 11, 12, 13, 14, 15, 16]

        def items1b():
            its = [item([qn1[:, t, :]], T, 64, gains=[par("c_qn")]) for t in range(4)]
            its += [item([qr1[:, t, :]], T, 32, gains=[par("c_qr")], rot=("rot8", "cosm", "sinm")) for t in range(2)]
            its += [item([kn1[:, t, :]], TC, 64, gains=[par("c_kn")]) for t in range(4)]
            return its

        def att1(which):
            gs = []
            for h in range(8):
                o = slice(64 * (h % 2), 64 * (h % 2) + 64)
                units = []
                for qt in range(2):
                    q = slice(P * qt, P * qt + P)
                    if which == 0:
                        ro = slice(32 * (h % 4), 32 * (h % 4) + 32)
                        units.append({"maps": [[(qn1[o, h // 2, q], kn1[o, h // 2, :]), (qr1[ro, h // 4, q], fm1[ro, KR, :])]],
                                      "nk": TC, "scale": 96 ** -0.5, "sink": None, "mask": None})
                    else:
                        units.append({"maps": [[(fm1[o, DQ + h // 2, q], fm1[o, DK + h // 2, :])]], "nk": TC,
                                      "scale": 0.125, "sink": None, "mask": bias1[:, 2 * h + qt, :]})
                vals = [(vm1 if which == 0 else vt1)[:, kt, 64 * h:64 * h + 64] for kt in range(4)]
                gs.append({"units": units, "rows": o, "dst": ym1[o, 4 * which + h // 2, :], "vals": vals})
            return gs

        fs, s0 = room(0, 26, T)
        vtr, s0 = room(s0, 2, T)
        iw, s0 = room(s0, 2, 8)
        diff, _d = room(s0, 11, T)
        AR, s1 = room(s0, 3, 4 * P)
        AR = AR.rearrange("p a (b c t) -> p a b c t", b=2, c=2)
        Bf, s1 = room(s1, 3, T)
        Kf, s1 = room(s1, 3, T)
        gate, s1 = room(s1, 3, T)
        yr, s1 = room(s1, 3, T)
        ec, s1 = room(s1, 3, T)
        lo, s2 = room(s1, T)
        sgw, s2 = room(s2, 3, T)
        sa, s2 = room(s2, 3, T)
        sv, s2 = room(s2, 3, T)
        kk, s2 = room(s2, 3, T)
        w1, s2 = room(s2, 3, T)
        w2, s2 = room(s2, 3, T)
        tok, s3 = room(s1, 6, 384)
        prod, s3 = room(s3, 12, 512)
        NM, s3 = room(s3, 12, P)
        Y, s3 = room(s3, 12, P)
        U, _ = room(s3 - 2 * 12 * P, 384)
        SA, _ = room(s3 - 2 * 12 * P + 384, 384)
        S, _ = room(s3 - 2 * 12 * P + 768, 2, 192)
        acc, i0 = room(s3, 2, T)
        relu, i0 = room(i0, 2, T)
        top8, i0 = room(i0, 8)
        Xh, XTh = xT[:, 0:6, T:TC], hT[:, 0:6, T:TC]

        def at(m, i, r=slice(0, P), c=slice(0, P)):
            return m[r, i // 2, 128 * (i % 2) + c.start:128 * (i % 2) + c.stop]

        ctok, d0 = room(s0, 2, P)
        qlat, d0 = room(d0, 6, T)
        olat, d0 = room(d0, 6, T)
        W2 = {}
        sS, d0 = room(d0, DEEP, T)
        W2["s"] = sS.rearrange("p u (m k) -> p u m k", m=1)
        W2["pn"], d0 = room(d0, DEEP, T)
        W2["pT"], d0 = room(d0, 2, 2 * T)
        W2["pT"] = W2["pT"].rearrange("p g (c q) -> p g c q", c=2)
        W2["st"], d0 = room(d0, DEEP, 8)
        sT, r0 = room(d0, 4, 384)
        sg, r0 = room(r0, 2, T)
        sqr, r0 = room(r0, 2, T)
        rtr, r0 = room(r0, 2, T)
        inr, r0 = room(r0, T)
        ror, r0 = room(r0, T)

        def two(t):
            return t[:, 0, :], t[:, 1, :]

        def half(h):
            return slice(64 * (h % 2), 64 * (h % 2) + 64)

        def pe_mod(pe):
            pe.stage()
            stream.let_go()
            pe.wait_ge(a_pe, pe.next(a_pe))
            jm = pe.take("V")
            pe.wait_ge(freed["V"][jm % 4], pe.opens(jm))
            if stream.pending is not None:
                stream.mm(pe, banks["V"][jm % 4][0:32, 0:32], cT[:, 0, :], cT[:, 0, :], True, True)
            with pe.repeat(9, {"A": 4, "chunk": 4}) as i:
                jobs = []
                for c in range(4):
                    w = by_k(stream.next(pe))
                    j = pe.take("A")
                    pe.wait_ge(freed["A"][j % 4], pe.opens(j))
                    for k in range(KD):
                        g = slice(32 * (k % 4), 32 * (k % 4) + 32)
                        ins = stream.mm(pe, banks["A"][j % 4][g, 0:CH], cT[:, k, :], w[:, k, :], k < 4, k >= 4)
                    ins.then_inc(full["A"][j % 4], 1)
                    jobs.append(j)
                stream.let_go()
                for c, j in enumerate(jobs):
                    pe.wait_ge(freed["A"][j % 4], pe.frees(j))
                    for t in range(2):
                        ins = stream.mm(pe, banks["V"][jm % 4][:, bass.ds(i * 16 + 4 * c + 2 * t, 2)],
                                        cond_rows[:, c, t * P:(t + 1) * P], cat["sel"], True, True)
                ins.then_inc(mod_turn, 1)
            pe.eng.sem_inc(full["V"][jm % 4], 1)

        def act_mod(act):
            act.stage()
            with act.repeat(9, {"A": 4, "chunk": 4}):
                for c in range(4):
                    j = act.take("A")
                    act.job["chunk"] += 1
                    act.wait_ge(full["A"][j % 4], act.fills(j))
                    act.eng.activation(cond_rows[:, c, :], banks["A"][j % 4][:, 0:CH], ACT.Copy).then_inc(freed["A"][j % 4], 1)

        def vec_mod(v):
            v.stage()
            j = v.take("V")
            v.wait_ge(mod_turn, v.next(mod_turn, N_MOD))
            vec_mods(v, 0, banks["V"][j % 4][:, 0:144])
            v.eng.sem_inc(freed["V"][j % 4], 1)

        def vec_mods(v, l, src):
            m2 = mods[:, :, :].rearrange("p a b -> p (a b)")
            v.eng.tensor_tensor(m2, src, bmod[:, l, :], ALU.add).then_inc(v_self, 1)
            v.wait_ge(v_self, v.next(v_self))
            for m, add, mul in ((1, 1.0, 1.0), (4, 1.0, 1.0), (7, 1.0, 1.0), (2, 0.0, 0.5), (8, 0.0, 0.5)):
                seg = m2[:, 16 * m:16 * m + 16]
                ins = v.eng.tensor_scalar(seg, seg, add, mul, ALU.add, ALU.mult)
            ins.then_inc(v_self, 1)
            v.wait_ge(v_self, v.next(v_self))

        def pe_out(pe, n, rhs_of):
            pe.stage()
            for c in range(KD):
                if c % 2 == 0:
                    w = by_k(stream.next(pe))
                p = "A" if c < 4 else "V"
                j = pe.take(p)
                pe.wait_ge(freed[p][j % 4], pe.opens(j))
                bank = banks[p][j % 4]
                for k in range(KD):
                    ins = stream.mm(pe, bank[:, 0:n], w[:, k, (c % 2) * P:(c % 2 + 1) * P], rhs_of(k), k == 0, k == KD - 1)
                ins.then_inc(full[p][j % 4], 1)

        def vec_out(v, n, m):
            v.stage()
            add_to_x(v, [("A", v.take("A")) for _ in range(4)] + [("V", v.take("V")) for _ in range(4)], n, m, True)

        def pe_mix0(pe):
            def h_rhs(k, n):
                return hT[:, k, 0:n]

            def h_lhs(k, tt):
                return hT[:, k, tt * P:(tt + 1) * P]

            pe.stage()
            items = rope_items0()
            for t in range(13):
                if t % 2 == 0:
                    w = by_k(stream.next(pe))
                pe_tiles(pe, w, KD, [(P * (t % 2), P, TC)], h_rhs, t == 0)
                if t:
                    pe_heads_step(pe, items, (sq0a, sq0b), t - 1)
            pe_rows(pe, w, KD, P, P, TC, h_lhs)
            pe_heads_step(pe, items, (sq0a, sq0b), 12)
            for c in range(2):
                pe_rows(pe, by_k(stream.next(pe)), KD, 0, CH, TC, h_lhs)
                if c == 0:
                    pe_heads_step(pe, items, (sq0a, sq0b), 13)
            pe.wait_ge(v_pe, pe.next(v_pe))
            pe_att(pe, att0(), W0, 4 * N_MOD)
            pe_heads(pe, sub_items(), two(sqy))
            pe_out(pe, TC, lambda k: yT[:, k, :])

        def act_mix0(act):
            act.stage()
            items = rope_items0()
            norm, _, _ = heads_jobs(items, act.job["V"])
            for t in range(13):
                if t:
                    act.wait_ge(freed["A"][j % 4], act.frees(j))
                    act_heads_step(act, items, (sq0a, sq0b), two(rt0), norm, t - 1)
                j = act_out(act, fm0[:, t, :], width=TC)
            act.wait_ge(freed["A"][j % 4], act.frees(j))
            act_heads_step(act, items, (sq0a, sq0b), two(rt0), norm, 12)
            for tt in range(4):
                act_out(act, vt0[:, tt, 0:P], width=P)
            for c in range(2):
                if c == 0:
                    act_heads_step(act, items, (sq0a, sq0b), two(rt0), norm, 13)
                for tt in range(4):
                    j = act_out(act, vt0[:, tt, P + CH * c:P + CH * c + CH], width=CH)
            act.wait_ge(v_a, act.next(v_a, 2))
            act_att(act, att0(), W0, 4 * N_MOD)
            act.wait_ge(freed["A"][(act.job["A"] - 1) % 4], act.frees(act.job["A"] - 1))
            act_heads(act, sub_items(), two(sqy), two(rty))

        def vec_mix0(v):
            vec_heads(v, rope_items0(), two(rt0), in0, ro0)
            vec_att(v, att0(), W0, 4 * N_MOD)
            vec_heads(v, sub_items(), two(rty), iny, None)
            vec_out(v, TC, 5)

        def pe_mix1(pe):
            def h_lhs(k, tt):
                return hT[:, k, tt * P:(tt + 1) * P]

            pe.stage()
            items = items1a()
            for t in range(17):
                if t % 2 == 0:
                    w = by_k(stream.next(pe))
                pe_tiles(pe, w, KD, [(P * (t % 2), P, T if t < CKV else TC)], lambda k, n: hT[:, k, 0:n], t == 0)
                if t - 1 in READY1:
                    pe_heads_step(pe, items, two(sq1), READY1.index(t - 1))
            for c in range(2):
                pe_rows(pe, by_k(stream.next(pe)), KD, 0, CH, TC, h_lhs)
                pe_heads_step(pe, items, two(sq1), len(items) - 1 + c)
            pe.wait_ge(v_pe, pe.next(v_pe))
            pe.stage()
            items = items1b()
            for t in range(6):
                if t % 2 == 0:
                    w = by_k(stream.next(pe), 6)
                pe_tiles(pe, w, 6, [(P * (t % 2), P, T)], lambda k, n: fm1[:, CQ + k, 0:n])
                if t:
                    pe_heads_step(pe, items, two(sq1), t - 1)
            w = by_k(stream.next(pe), 2, D)
            for t in range(4):
                pe_tiles(pe, w, 2, [(P * t, P, TC)], lambda k, n: fm1[:, CKV + k, 0:n])
                pe_heads_step(pe, items, two(sq1), t + 5)
            for tt in range(4):
                pe_rows(pe, w, 2, 512, 512, P, lambda k, _: fm1[:, CKV + k, tt * P:(tt + 1) * P])
                if tt < 2:
                    pe_heads_step(pe, items, two(sq1), tt + 9)
            pe.wait_ge(v_pe, pe.next(v_pe))
            pe_att(pe, att1(0), W1)
            pe_att(pe, att1(1), W1)
            pe.wait_ge(freed["A"][(pe.job["A"] - 1) % 4], pe.frees(pe.job["A"] - 1))
            pe_out(pe, T, lambda k: ym1[:, k, :])

        def act_mix1(act):
            act.stage()
            items = items1a()
            norm, _, _ = heads_jobs(items, act.job["V"])
            for t in range(17):
                if t - 1 in READY1:
                    act.wait_ge(freed["A"][j % 4], act.frees(j))
                    act_heads_step(act, items, two(sq1), two(rt1), norm, READY1.index(t - 1))
                n = T if t < CKV else TC
                j = act_out(act, fm1[:, t, 0:n], width=n)
            act.wait_ge(freed["A"][j % 4], act.frees(j))
            for c in range(2):
                act_heads_step(act, items, two(sq1), two(rt1), norm, len(items) - 1 + c)
                for tt in range(4):
                    act_out(act, vt1[:, tt, CH * c:CH * c + CH], width=CH)
            act.wait_ge(v_a, act.next(v_a, 2))
            act.stage()
            items = items1b()
            norm, _, _ = heads_jobs(items, act.job["V"])
            for t in range(10):
                if t:
                    act.wait_ge(freed["A"][j % 4], act.frees(j))
                    act_heads_step(act, items, two(sq1), two(rt1), norm, t - 1)
                if t < 4:
                    j = act_out(act, qn1[:, t, :], width=T)
                elif t < 6:
                    j = act_out(act, qr1[:, t - 4, :], width=T)
                else:
                    j = act_out(act, kn1[:, t - 6, :], width=TC)
            act.wait_ge(freed["A"][j % 4], act.frees(j))
            for tt in range(4):
                if tt < 2:
                    act_heads_step(act, items, two(sq1), two(rt1), norm, tt + 9)
                act_out(act, vm1[:, tt, :], width=TC)
            act.wait_ge(v_a, act.next(v_a, 2))
            act_att(act, att1(0), W1)
            act_att(act, att1(1), W1)

        def vec_mix1(v):
            vec_heads(v, items1a(), two(rt1), in1, ro1)
            vec_heads(v, items1b(), two(rt1), in1, ro1)
            vec_att(v, att1(0), W1)
            v.eng.wait_ge(s_bias, 16)
            vec_att(v, att1(1), W1)
            vec_out(v, T, 5)

        def c_items(l):
            return [item([fs[:, SC, :]], T, 128, gains=[par(f"kv_{l}")])]

        def ret_items():
            return [item([fs[:, t, :]], T, 0, rot=("rot32", "cosr", "sinr")) for t in (TQ, TQ + 1, TK, TK + 1)]

        def ret_norms():
            return [item([yT[:, 6 + t, 0:T]], T, 64, gains=[par("one")]) for t in range(2)]

        def att2():
            gs = []
            for h in range(6):
                units = [{"maps": [[(qlat[:, h, P * qt:P * qt + P], fs[:, SC, :])]], "nk": T, "scale": 1.0, "sink": None,
                          "mask": acc[:, qt, :]} for qt in range(2)]
                gs.append({"units": units, "rows": slice(0, P), "dst": olat[:, h, :], "vals": [ctok[:, kt, :] for kt in range(2)]})
            return gs

        EARLY = 7
        INDEX_AT = [range(16 * lev // LEVELS, 16 * (lev + 1) // LEVELS) for lev in range(LEVELS)]
        SIXES = [(h, tt) for h in range(HEADS_R) for tt in range(2)]

        def pe_sums(pe, src):
            for t in range(3):
                j = pe.take("V")
                pe.wait_ge(freed["V"][j % 4], pe.opens(j))
                bank = banks["V"][j % 4]
                pe.eng.matmul(bank[:, 0:T], ones[64], src[:, t, :], start=True, stop=True).then_inc(full["V"][j % 4], 1)

        def pe_mix2(pe, l):
            def h_lhs(k, tt):
                return hT[:, k, tt * P:(tt + 1) * P]


            def tiles(chunks, width=P):
                for _ in range(chunks):
                    w = by_k(stream.next(pe))
                    pe_tiles(pe, w, KD, [(0, P, T), (P, width, T)], lambda k, n: hT[:, k, 0:n], width < P)
                return w

            w = tiles(1, 24)
            pe_rows(pe, w, KD, P + 16, 8, T, h_lhs)
            tiles(EARLY)
            pe.wait_ge(a_pe, pe.next(a_pe))
            lora = par(f"lora_{l}", 0, 384)
            for r in (slice(0, 32), slice(32, 64), slice(64, P)):
                for t in range(3):
                    j = pe.take("A")
                    pe.wait_ge(freed["A"][j % 4], pe.opens(j))
                    bank = banks["A"][j % 4]
                    pe.eng.matmul(bank[:, 0:T], lora[r, t * P:(t + 1) * P], lo[r, :], start=True, stop=True).then_inc(full["A"][j % 4], 1)
            if l:
                for t in range(3):
                    j = pe.take("A")
                    pe.wait_ge(freed["A"][j % 4], pe.opens(j))
                    bank = banks["A"][j % 4]
                    pe.eng.matmul(bank[:, 0:T], par(f"v2_{l}", 0, 384)[0:16, t * P:(t + 1) * P], fs[0:16, MV, :],
                                          start=True, stop=True).then_inc(full["A"][j % 4], 1)
            pe.wait_ge(v_pe, pe.next(v_pe))
            pe_sums(pe, w1)
            tiles(12 - EARLY)
            pe_rows(pe, by_k(stream.next(pe)), KD, 0, CH, T, h_lhs)
            pe.wait_ge(v_pe, pe.next(v_pe))
            pe_sums(pe, w1)
            for h, tt in SIXES:
                j = pe.take("V")
                pe.wait_ge(freed["V"][j % 4], pe.opens(j))
                bank = banks["V"][j % 4]
                ts = slice(P * tt, P * tt + P)
                rhs = AR[half(h), h // 2, tt, :, :].rearrange("p c t -> p (c t)")
                pe.eng.matmul(bank[:, 0:T], Bf[half(h), h // 2, ts], rhs, start=True, stop=True)
                pe.eng.matmul(bank[:, T:TC], Kf[half(h), h // 2, ts], rhs, start=True, stop=True).then_inc(full["V"][j % 4], 1)
            for src in (Bf, Kf, fs[:, RV:RV + 3, :]):
                for tt in range(2):
                    j = pe.take("A")
                    pe.wait_ge(freed["A"][j % 4], pe.opens(j))
                    bank = banks["A"][j % 4]
                    for t in range(3):
                        ins = pe.eng.transpose(bank[:, t * P:(t + 1) * P], src[:, t, P * tt:P * tt + P], cat["ident"])
                    ins.then_inc(full["A"][j % 4], 1)
            pe.wait_ge(v_pe, pe.next(v_pe))
            plan[f"index{l}"] = []
            for lev in range(LEVELS):
                pe.wait_ge(g_pe, pe.next(g_pe))
                if lev:
                    pe.wait_ge(v_pe, pe.next(v_pe))
                for q in range(3):
                    j = pe.take("A")
                    pe.wait_ge(freed["A"][j % 4], pe.opens(j))
                    bank = banks["A"][j % 4]
                    for i in range(4 * q, 4 * q + 4):
                        ins = pe.eng.matmul(bank[:, (i % 4) * P:(i % 4 + 1) * P], NM[:, i, :], at(Xh, i), start=True, stop=True)
                    ins.then_inc(full["A"][j % 4], 1)
                for i in INDEX_AT[lev]:
                    tt, h = divmod(i, 8)
                    jj = pe.take("V")
                    plan[f"index{l}"].append(jj)
                    pe.wait_ge(freed["V"][jj % 4], pe.opens(jj))
                    pe.eng.matmul(banks["V"][jj % 4][:, 0:T], fs[half(h), SIQ + h // 2, P * tt:P * tt + P], fs[half(h), SIK, :],
                                  start=True, stop=True).then_inc(full["V"][jj % 4], 1)
                pe.wait_ge(freed["A"][j % 4], pe.frees(j))
                if lev:
                    pe.wait_ge(v_pe, pe.next(v_pe))
                if lev < LEVELS - 1:
                    for q in range(3):
                        j = pe.take("V")
                        pe.wait_ge(freed["V"][j % 4], pe.opens(j))
                        bank = banks["V"][j % 4]
                        for i in range(4 * q, 4 * q + 4):
                            ins = pe.eng.matmul(bank[:, (i % 4) * P:(i % 4 + 1) * P], at(XTh, i), Y[:, i, :], start=True, stop=True)
                        ins.then_inc(full["V"][j % 4], 1)
                for q in range(3):
                    j = pe.take("V")
                    pe.wait_ge(freed["V"][j % 4], pe.opens(j))
                    bank = banks["V"][j % 4]
                    for i in range(4 * q, 4 * q + 4):
                        ins = pe.eng.matmul(bank[:, (i % 4) * P:(i % 4 + 1) * P], Y[:, i, :], at(XTh, i), start=True, stop=True)
                    ins.then_inc(full["V"][j % 4], 1)
            pe.wait_ge(v_pe, pe.next(v_pe))
            for ci in range(T // RC):
                tt, o = ci // 2, slice(64 * (ci % 2), 64 * (ci % 2) + 64)
                S0 = S[:, ci % 2, :]
                same = [h for h in range(HEADS_R) if half(h) == o]
                other = [h for h in range(HEADS_R) if half(h) != o]

                def col(h):
                    return slice(64 * h, 64 * h + 64)

                def duo(h):
                    return slice(64 * (h // 2), 64 * (h // 2) + 64)

                jU = pe.take("V")
                pe.wait_ge(freed["V"][jU % 4], pe.opens(jU))
                bank = banks["V"][jU % 4]
                for h in other + same:
                    pe.eng.matmul(bank[o, col(h)], prod[o, 2 * h + tt, T + o.start:T + o.stop], tok[o, 4 + tt, col(h)],
                                  start=h == other[0], stop=False)
                    if ci and h == other[-1]:
                        pe.wait_ge(v_pe, pe.next(v_pe))
                    if h in same:
                        ins = pe.eng.matmul(bank[o, col(h)], AR[half(h), h // 2, tt, 0, o], S0[half(h), duo(h)],
                                            start=False, stop=False)
                ins.then_inc(pe_self, 1)
                pe.wait_ge(pe_self, pe.next(pe_self))
                for h in other:
                    ins = pe.eng.matmul(bank[o, col(h)], AR[half(h), h // 2, tt, 0, o], S0[half(h), duo(h)],
                                        start=False, stop=h == other[-1])
                ins.then_inc(full["V"][jU % 4], 1)
                jSA = pe.take("V")
                pe.wait_ge(freed["V"][jSA % 4], pe.opens(jSA))
                bank = banks["V"][jSA % 4]
                pe.wait_ge(freed["V"][jU % 4], pe.frees(jU))
                for h in range(HEADS_R):
                    c = slice(64 * h, 64 * h + 64)
                    ins = pe.eng.matmul(bank[o, c], at(XTh, 2 * h + tt, o, o), U[o, c], start=True, stop=True)
                ins.then_inc(full["V"][jSA % 4], 1)
                pe.wait_ge(freed["V"][jSA % 4], pe.frees(jSA))
                if ci < T // RC - 1:
                    j = pe.take("V")
                    pe.wait_ge(freed["V"][j % 4], pe.opens(j))
                    bank = banks["V"][j % 4]
                    for h in range(HEADS_R):
                        c, hs = slice(64 * h, 64 * h + 64), slice(64 * (h // 2), 64 * (h // 2) + 64)
                        pe.eng.matmul(bank[half(h), hs], tok[o, tt, c], SA[o, c], start=True, stop=False)
                        ins = pe.eng.matmul(bank[half(h), hs], tok[o, 2 + tt, c], tok[o, 4 + tt, c], start=False, stop=True)
                    ins.then_inc(full["V"][j % 4], 1)
                j = pe.take("A")
                pe.wait_ge(freed["A"][j % 4], pe.opens(j))
                bank = banks["A"][j % 4]
                for h in other + same:
                    i, out = 2 * h + tt, bank[half(h), duo(h)]
                    pe.eng.matmul(out, SA[o, col(h)], prod[o, i, P + o.start:P + o.stop], start=h in (other[0], same[0]), stop=False)
                    ins = pe.eng.matmul(out, tok[o, 4 + tt, col(h)], prod[o, i, 384 + o.start:384 + o.stop],
                                        start=False, stop=False)
                    if h in same:
                        ins = pe.eng.matmul(out, S0[half(h), duo(h)], AR[half(h), h // 2, tt, 1, o], start=False, stop=h == same[-1])
                ins.then_inc(pe_self, 1)
                pe.wait_ge(pe_self, pe.next(pe_self))
                for h in other:
                    ins = pe.eng.matmul(bank[half(h), duo(h)], S0[half(h), duo(h)], AR[half(h), h // 2, tt, 1, o],
                                        start=False, stop=h == other[-1])
                ins.then_inc(full["A"][j % 4], 1)
            pe.wait_ge(freed["A"][j % 4], pe.frees(j))
            pe_sums(pe, yr)
            pe.wait_ge(v_pe, pe.next(v_pe))
            plan[f"variance{l}"] = pe.job["V"]
            pe_sums(pe, Kf)
            pe_heads(pe, c_items(l), two(sqr))
            j = pe.take("A")
            pe.wait_ge(freed["A"][j % 4], pe.opens(j))
            bank = banks["A"][j % 4]
            for tt in range(2):
                ins = pe.eng.transpose(bank[:, P * tt:P * tt + P], fs[:, SC, P * tt:P * tt + P], cat["ident"])
            ins.then_inc(full["A"][j % 4], 1)
            uk, uv = par(f"uk_{l}", 0, 384), par(f"uv_{l}", 0, 384)
            for h in range(6):
                j = pe.take("A")
                pe.wait_ge(freed["A"][j % 4], pe.opens(j))
                bank = banks["A"][j % 4]
                pe.eng.matmul(bank[:, 0:T], uk[half(h), P * (h // 2):P * (h // 2) + P], fs[half(h), SQ + h // 2, :],
                                      start=True, stop=True).then_inc(full["A"][j % 4], 1)
            pe.wait_ge(freed["A"][j % 4], pe.frees(j))
            pe_att(pe, att2(), W2)
            pe.wait_ge(freed["A"][(pe.job["A"] - 1) % 4], pe.frees(pe.job["A"] - 1))
            for t in range(3):
                j = pe.take("A")
                pe.wait_ge(freed["A"][j % 4], pe.opens(j))
                bank = banks["A"][j % 4]
                for h in (2 * t, 2 * t + 1):
                    ins = pe.eng.matmul(bank[half(h), 0:T], uv[:, 64 * h:64 * h + 64], olat[:, h, :], start=True, stop=True)
                ins.then_inc(full["A"][j % 4], 1)
            pe_heads(pe, ret_items(), None)
            for h in range(4):
                j = pe.take("V")
                pe.wait_ge(freed["V"][j % 4], pe.opens(j))
                bank = banks["V"][j % 4]
                q, k = fs[half(h), TQ + h // 2, :], fs[half(h), TK + h // 2, :]
                pe.eng.matmul(bank[:, 0:T], k[:, 0:P], q, start=True, stop=True)
                pe.eng.matmul(bank[:, T:T + P], k[:, P:T], q[:, P:T], start=True, stop=True).then_inc(full["V"][j % 4], 1)
            pe.wait_ge(freed["V"][j % 4], pe.frees(j))
            for t in range(2):
                j = pe.take("A")
                pe.wait_ge(freed["A"][j % 4], pe.opens(j))
                bank = banks["A"][j % 4]
                for h in (2 * t, 2 * t + 1):
                    c = slice(64 * h, 64 * h + 64)
                    pe.eng.matmul(bank[half(h), 0:P], vtr[:, 0, c], sT[:, h, 0:P], start=True, stop=True)
                    pe.eng.matmul(bank[half(h), P:T], vtr[:, 0, c], sT[:, h, P:T], start=True, stop=False)
                    ins = pe.eng.matmul(bank[half(h), P:T], vtr[:, 1, c], sT[:, h, T:T + P], start=False, stop=True)
                ins.then_inc(full["A"][j % 4], 1)
            pe_heads(pe, ret_norms(), two(sqr))
            pe.wait_ge(v_pe, pe.next(v_pe))
            pe_out(pe, T, lambda k: yT[:, k, 0:T])

        def act_mix2(act, l):
            def tiles(first, n):
                for t in range(first, first + n):
                    r = slice(0, 24 if t == MV else P)
                    act_out(act, fs[r, t, :], rows=r, width=T)

            tiles(MV - 1, 2)
            for tt in range(2):
                act_out(act, iw[:, tt, :], width=8, scale=8 ** -0.5 * 0.125)
            tiles(0, 2 * EARLY)
            act.wait_ge(v_a, act.next(v_a))
            act.eng.activation(lo[0:32, :], fs[0:32, LORA, :], ACT.Tanh)
            act.eng.activation(lo[32:64, :], fs[32:64, LORA, :], ACT.Copy)
            act.eng.activation(lo[64:P, :], fs[64:P, LORA, :], ACT.Sigmoid).then_inc(a_self, 1)
            act.wait_ge(a_self, act.next(a_self))
            act.eng.sem_inc(a_pe, 1)
            for dst, name in ((sgw, "w0_"), (sa, "a0_"), (gate, None), (sv, "v0_")):
                if dst is sv and not l:
                    continue
                for t in range(3):
                    if name:
                        act_out(act, dst[:, t, :], width=T, func=ACT.Sigmoid, bias=par(f"{name}{l}", t))
                    else:
                        act_out(act, dst[:, t, :], width=T)
            act.wait_ge(v_a, act.next(v_a))
            act.eng.activation(w2[:, :, :], w2[:, :, :], ACT.Sqrt).then_inc(a_self, 1)
            act.wait_ge(a_self, act.next(a_self))
            act.eng.sem_inc(a_v, 1)
            tiles(2 * EARLY, 4)
            act.wait_ge(v_a, act.next(v_a))
            act.eng.activation(ec[:, :, :], w1[:, :, :], ACT.Exp)
            act.wait_ge(v_a, act.next(v_a))
            act.eng.activation(sgw[:, :, :], w1[:, :, :], ACT.Exp, scale=-1.0)
            act.eng.activation(sv[:, :, :], w2[:, :, :], ACT.Exp).then_inc(a_self, 1)
            act.wait_ge(a_self, act.next(a_self))
            act.eng.sem_inc(a_v, 1)
            tiles(2 * EARLY + 4, 24 - 2 * EARLY - 4)
            for tt in range(2):
                act_out(act, vtr[:, tt, :], width=T)
            for q in range(6):
                act_out(act, tok[:, q, :], width=384)
            for lev in range(LEVELS):
                for q in range(3):
                    act_out(act, Y[:, 4 * q:4 * q + 4, :], width=TC)
                for i in INDEX_AT[lev]:
                    j = plan[f"index{l}"][i]
                    act.wait_ge(full["V"][j % 4], act.fills(j))
                    if i >= 2:
                        act.wait_ge(head_summed, act.next(head_summed))
                    act.eng.activation(relu[:, i % 2, :], banks["V"][j % 4][:, 0:T], ACT.Relu).then_inc(freed["V"][j % 4], 1)
            act.wait_ge(head_summed, act.next(head_summed, 2))
            for ci in range(T // RC):
                act_out(act, yr[:, :, RC * ci:RC * ci + RC], width=192)
            for t in range(3):
                act_root(act, plan[f"variance{l}"] + t, Bf[:, t, :], 64, par("gn_eps"))
            act.wait_ge(v_a, act.next(v_a))
            act_heads(act, c_items(l), two(sqr), two(rtr))
            act_out(act, ctok[:, :, :], width=T)
            for h in range(6):
                act_out(act, qlat[:, h, :], width=T, scale=0.125)
            act_att(act, att2(), W2)
            for t in range(3):
                act_out(act, yT[:, 3 + t, 0:T], width=T)
            act_heads(act, ret_items(), None, None)
            for t in range(2):
                j = act_out(act, yT[:, 6 + t, 0:T], width=T)
            act.wait_ge(freed["A"][j % 4], act.frees(j))
            act_heads(act, ret_norms(), two(sqr), two(rtr))
            act.eng.activation(sg[:, :, :], fs[:, TG:TG + 2, :], ACT.Silu).then_inc(a_self, 1)
            act.wait_ge(a_self, act.next(a_self))
            act.eng.sem_inc(a_v, 1)

        def vec_pick(v, first, n):
            for i in range(first, min(first + n, 2 * PICKS)):
                tt, step = divmod(i, PICKS)
                w = acc[:, tt, :]
                if step < PICKS - 1:
                    v.eng.max(top8[:, :], w).then_inc(v_self, 1)
                    v.wait_ge(v_self, v.next(v_self))
                    v.eng.match_replace(w, top8[:, :], w, TAKEN).then_inc(v_self, 1)
                    v.wait_ge(v_self, v.next(v_self))
                else:
                    v.eng.tensor_scalar(w, w, TAKEN / 2, NEG, ALU.is_gt, ALU.mult).then_inc(v_self, 1)
                    v.wait_ge(v_self, v.next(v_self))
                    v.eng.tensor_tensor(w, w, cat["causal"][:, tt * T:(tt + 1) * T], ALU.add).then_inc(v_self, 1)
                    v.wait_ge(v_self, v.next(v_self))
            return min(first + n, 2 * PICKS)

        def vec_mix2(v, l):
            E = v.eng
            a0 = v.job["A"]
            first = a0 + 4 + LORA
            v.wait_ge(freed["A"][first % 4], v.frees(first))
            v.job["A"] += 4 + 2 * EARLY
            spans = [(0, 10, "mu_")] + ([(MV, 1, "vmu_")] if l else [])
            for t0, nt, _ in spans:
                d = diff[:, min(t0, 10):min(t0, 10) + nt, :]
                E.tensor_tensor(d[:, :, 1:T], fs[:, t0:t0 + nt, 0:T - 1], fs[:, t0:t0 + nt, 1:T], ALU.subtract) if t0 == 0 else \
                    E.tensor_tensor(d[0:16, :, 1:T], fs[0:16, t0:t0 + nt, 0:T - 1], fs[0:16, t0:t0 + nt, 1:T], ALU.subtract)
                r = slice(0, P if t0 == 0 else 16)
                E.tensor_scalar(d[r, :, 0:1], fs[r, t0:t0 + nt, 0:1], -1.0, None, ALU.mult).then_inc(v_self, 1)
                v.wait_ge(v_self, v.next(v_self))
            for t0, nt, name in spans:
                r = slice(0, P if t0 == 0 else 16)
                for t in range(nt):
                    x_ = fs[r, t0 + t, :]
                    ins = E.scalar_tensor_tensor(x_, diff[r, min(t0, 10) + t, :], par(f"{name}{l}", t, rows=r), x_, ALU.mult, ALU.add)
            ins.then_inc(v_self, 1)
            v.wait_ge(v_self, v.next(v_self))
            E.sem_inc(v_a, 1)
            k_, r_, v_ = fs[:, RK:RK + 3, :], fs[:, RR:RR + 3, :], fs[:, RV:RV + 3, :]
            for t in range(3):
                ins = E.tensor_scalar(kk[:, t, :], k_[:, t, :], par(f"kk_{l}", t), None, ALU.mult)
            ins.then_inc(v_self, 1)
            v.wait_ge(v_self, v.next(v_self))
            E.tensor_tensor(w1[:, :, :], kk[:, :, :], kk[:, :, :], ALU.mult).then_inc(v_self, 1)
            v.wait_ge(v_self, v.next(v_self))
            v.eng.sem_inc(v_pe, 1)
            for t in range(3):
                j = v.take("V")
                v.wait_ge(full["V"][j % 4], v.fills(j))
                bank = banks["V"][j % 4]
                E.tensor_scalar(w2[:, t, :], bank[:, 0:T], 1e-24, None, ALU.max).then_inc(freed["V"][j % 4], 1)
                v.wait_ge(freed["V"][j % 4], v.frees(j))
            E.sem_inc(v_a, 1)
            v.wait_ge(a_v, v.next(a_v))
            E.reciprocal(w2[:, :, :], w2[:, :, :]).then_inc(v_self, 1)
            v.wait_ge(v_self, v.next(v_self))
            E.tensor_tensor(kk[:, :, :], kk[:, :, :], w2[:, :, :], ALU.mult).then_inc(v_self, 1)
            v.wait_ge(v_self, v.next(v_self))
            n_lo = 12 if l else 9
            v.wait_ge(freed["A"][(v.job["A"] + n_lo - 1) % 4], v.frees(v.job["A"] + n_lo - 1))
            v.job["A"] += n_lo + 24 - 2 * EARLY + 2
            for t in range(3):
                ins = E.tensor_scalar(w1[:, t, :], sa[:, t, :], 1.0, par(f"ka_{l}", t), ALU.subtract, ALU.mult)
            ins.then_inc(v_self, 1)
            v.wait_ge(v_self, v.next(v_self))
            E.scalar_tensor_tensor(k_, w1[:, :, :], 1.0, k_, ALU.add, ALU.mult).then_inc(v_self, 1)
            v.wait_ge(v_self, v.next(v_self))
            if l:
                E.tensor_tensor(w2[:, :, :], vfirst[:, :, :], v_, ALU.subtract).then_inc(v_self, 1)
                v.wait_ge(v_self, v.next(v_self))
                E.tensor_tensor(w2[:, :, :], w2[:, :, :], sv[:, :, :], ALU.mult).then_inc(v_self, 1)
                v.wait_ge(v_self, v.next(v_self))
                E.tensor_tensor(v_, v_, w2[:, :, :], ALU.add).then_inc(v_self, 1)
                v.wait_ge(v_self, v.next(v_self))
            else:
                E.tensor_copy(vfirst[:, :, :], v_).then_inc(v_self, 1)
                v.wait_ge(v_self, v.next(v_self))
            E.tensor_scalar(w2[:, :, :], sgw[:, :, :], -DECAY, None, ALU.mult).then_inc(v_self, 1)
            v.wait_ge(v_self, v.next(v_self))
            f2 = "p a b -> p (a b)"
            E.tensor_tensor_scan(w1[:, :, :].rearrange(f2), cat["scanm"], w2[:, :, :].rearrange(f2), 0.0, ALU.mult, ALU.add).then_inc(v_self, 1)
            v.wait_ge(v_self, v.next(v_self))
            E.sem_inc(v_a, 1)
            E.tensor_tensor(w2[:, :, :], w1[:, :, :], w2[:, :, :], ALU.subtract).then_inc(v_self, 1)
            v.wait_ge(v_self, v.next(v_self))
            E.sem_inc(v_a, 1)
            E.tensor_tensor(Bf[:, :, :], kk[:, :, :], sa[:, :, :], ALU.mult).then_inc(v_self, 1)
            v.wait_ge(v_self, v.next(v_self))
            v.wait_ge(a_v, v.next(a_v))
            E.tensor_tensor(Bf[:, :, :], Bf[:, :, :], sgw[:, :, :], ALU.mult)
            E.tensor_tensor(Kf[:, :, :], k_, sgw[:, :, :], ALU.mult)
            by2 = "p (b t) -> p b t"
            for t in range(3):
                E.scalar_tensor_tensor(AR[:, t, :, 0, :], kk[:, t, :].rearrange(by2, b=2), -1.0, sv[:, t, :].rearrange(by2, b=2),
                                       ALU.mult, ALU.mult)
                E.tensor_tensor(AR[:, t, :, 1, :], r_[:, t, :].rearrange(by2, b=2), ec[:, t, :].rearrange(by2, b=2), ALU.mult)
            for t in range(3):
                ins = E.scalar_tensor_tensor(w1[:, t, :], r_[:, t, :], par(f"rk_{l}", t), k_[:, t, :], ALU.mult, ALU.mult)
            ins.then_inc(v_self, 1)
            v.wait_ge(v_self, v.next(v_self))
            v.eng.sem_inc(v_pe, 1)
            for t in range(3):
                j = v.take("V")
                v.wait_ge(full["V"][j % 4], v.fills(j))
                bank = banks["V"][j % 4]
                E.tensor_tensor(k_[:, t, :], bank[:, 0:T], v_[:, t, :], ALU.mult).then_inc(freed["V"][j % 4], 1)
                v.wait_ge(freed["V"][j % 4], v.frees(j))
            for i in range(12):
                j = v.take("V")
                v.wait_ge(full["V"][j % 4], v.fills(j))
                bank = banks["V"][j % 4]
                E.tensor_tensor(prod[:, i, :], bank[:, :], cat["prodm"], ALU.mult).then_inc(freed["V"][j % 4], 1)
                v.wait_ge(freed["V"][j % 4], v.frees(j))
            v.wait_ge(freed["V"][j % 4], v.frees(j))
            E.sem_inc(v_g, 1)
            for m in (Xh, XTh):
                for i in range(12):
                    ins = E.tensor_copy(at(m, i), cat["ident"])
            ins.then_inc(v_self, 1)
            v.wait_ge(v_self, v.next(v_self))
            v.eng.sem_inc(v_pe, 1)
            v.job["A"] += 6 + 3 * LEVELS
            for lev in range(LEVELS):
                for i in INDEX_AT[lev]:
                    tt, h = divmod(i, 8)
                    j = v.take("V")
                    v.wait_ge(freed["V"][j % 4], v.frees(j))
                    if h:
                        E.scalar_tensor_tensor(acc[:, tt, :], relu[:, i % 2, :], iw[:, tt, h:h + 1], acc[:, tt, :],
                                               ALU.mult, ALU.add).then_inc(head_summed, 1)
                    else:
                        causal = cat["causal"][:, tt * T:(tt + 1) * T]
                        E.scalar_tensor_tensor(acc[:, tt, :], relu[:, i % 2, :], iw[:, tt, h:h + 1], causal,
                                               ALU.mult, ALU.add).then_inc(head_summed, 1)
                    v.wait_ge(head_summed, v.next(head_summed))
                for m in ([Xh, XTh] if lev < LEVELS - 1 else [XTh]):
                    for q in range(3):
                        j = v.take("V")
                        v.wait_ge(full["V"][j % 4], v.fills(j))
                        bank = banks["V"][j % 4]
                        dst = m[:, 2 * q:2 * q + 2, :]
                        E.tensor_tensor(dst, dst, bank[:, :].rearrange("p (a b) -> p a b", a=2), ALU.add).then_inc(freed["V"][j % 4], 1)
                        v.wait_ge(freed["V"][j % 4], v.frees(j))
                    if lev < LEVELS - 1:
                        v.wait_ge(freed["V"][j % 4], v.frees(j))
                        E.sem_inc(v_pe, 1)
            v.wait_ge(freed["V"][j % 4], v.frees(j))
            E.memset(S[:, 0, :], 0.0).then_inc(v_self, 1)
            v.wait_ge(v_self, v.next(v_self))
            v.eng.sem_inc(v_pe, 1)
            picks = 0
            for ci in range(T // RC):
                o = slice(64 * (ci % 2), 64 * (ci % 2) + 64)
                for dst in (U, SA):
                    j = v.take("V")
                    v.wait_ge(full["V"][j % 4], v.fills(j))
                    bank = banks["V"][j % 4]
                    E.tensor_copy(dst[o, :], bank[o, 0:384]).then_inc(freed["V"][j % 4], 1)
                    v.wait_ge(freed["V"][j % 4], v.frees(j))
                    picks = vec_pick(v, picks, 2)
                if ci < T // RC - 1:
                    j = v.take("V")
                    v.wait_ge(full["V"][j % 4], v.fills(j))
                    bank = banks["V"][j % 4]
                    S1 = S[:, (ci + 1) % 2, :]
                    if ci:
                        v.wait_ge(full["A"][(v.job["A"] + ci - 1) % 4], v.fills(v.job["A"] + ci - 1))
                    E.tensor_tensor(S1, bank[:, 0:192], S[:, ci % 2, :], ALU.add).then_inc(freed["V"][j % 4], 1)
                    v.wait_ge(freed["V"][j % 4], v.frees(j))
                    for t in range(3):
                        e = RC * ci + RC - 1
                        ins = E.tensor_scalar(S1[:, 64 * t:64 * t + 64], S1[:, 64 * t:64 * t + 64], ec[:, t, e:e + 1], None, ALU.mult)
                    ins.then_inc(v_self, 1)
                    v.wait_ge(v_self, v.next(v_self))
                    v.eng.sem_inc(v_pe, 1)
                picks = vec_pick(v, picks, 1)
            vec_pick(v, picks, 2 * PICKS - picks)
            v.job["A"] += 4
            for t in range(3):
                j = v.take("V")
                v.wait_ge(full["V"][j % 4], v.fills(j))
                bank = banks["V"][j % 4]
                E.scalar_tensor_tensor(yr[:, t, :], bank[:, 0:T], -1.0 / 64, yr[:, t, :], ALU.mult, ALU.add).then_inc(freed["V"][j % 4], 1)
                v.wait_ge(freed["V"][j % 4], v.frees(j))
            E.tensor_tensor(Kf[:, :, :], yr[:, :, :], yr[:, :, :], ALU.mult).then_inc(v_self, 1)
            v.wait_ge(v_self, v.next(v_self))
            v.eng.sem_inc(v_pe, 1)
            for t in range(3):
                j = v.take("V")
                v.wait_ge(freed["V"][j % 4], v.frees(j))
            E.reciprocal(Bf[:, :, :], Bf[:, :, :]).then_inc(v_self, 1)
            v.wait_ge(v_self, v.next(v_self))
            E.tensor_tensor(yr[:, :, :], yr[:, :, :], Bf[:, :, :], ALU.mult).then_inc(v_self, 1)
            v.wait_ge(v_self, v.next(v_self))
            for t in range(3):
                ins = E.tensor_scalar(yr[:, t, :], yr[:, t, :], par(f"lnw_{l}", t), par(f"lnb_{l}", t), ALU.mult, ALU.add)
            ins.then_inc(v_self, 1)
            v.wait_ge(v_self, v.next(v_self))
            E.tensor_tensor(yr[:, :, :], yr[:, :, :], k_, ALU.add).then_inc(v_self, 1)
            v.wait_ge(v_self, v.next(v_self))
            E.tensor_tensor(yT[:, 0:3, 0:T], yr[:, :, :], gate[:, :, :], ALU.mult).then_inc(v_self, 1)
            v.wait_ge(v_self, v.next(v_self))
            E.sem_inc(v_a, 1)
            vec_heads(v, c_items(l), two(rtr), inr, ror)
            v.job["A"] += 7
            vec_att(v, att2(), W2)
            v.job["A"] += 3
            vec_heads(v, ret_items(), two(rtr), inr, ror)
            for h in range(4):
                j = v.take("V")
                v.wait_ge(full["V"][j % 4], v.fills(j))
                bank = banks["V"][j % 4]
                E.tensor_tensor(sT[:, h, :], bank[:, 0:384], cat["retm"][:, 384 * h:384 * h + 384], ALU.mult).then_inc(freed["V"][j % 4], 1)
                v.wait_ge(freed["V"][j % 4], v.frees(j))
            v.job["A"] += 2
            vec_heads(v, ret_norms(), two(rtr), inr, ror)
            v.wait_ge(a_v, v.next(a_v))
            E.tensor_tensor(yT[:, 6:8, 0:T], yT[:, 6:8, 0:T], sg[:, :, :], ALU.mult).then_inc(v_self, 1)
            v.wait_ge(v_self, v.next(v_self))
            v.eng.sem_inc(v_pe, 1)
            vec_out(v, T, "one")

        NAMES = ["pre", "mod0", "f0a", "mix0", "f0b", "mod1", "f1a", "mix1", "f1b", "g0a", "mix2", "g0b", "g1a", "mix3", "g1b", "end"]
        upto = len(NAMES) if stop is None else NAMES.index(stop) + 1

        def on(name):
            return NAMES.index(name) < upto

        block = ctx.enter_context(nc.Block())

        @block.tensor
        def _(eng):
            pe = Hand(eng, plan)
            plan["writer"] = pe
            for p in "AV":
                for b in range(4):
                    eng.sem_inc(freed[p][b], 1)
            eng.wait_ge(s_par, 16 * 4)
            pe.wait_ge(v_pe, pe.next(v_pe))
            j = pe.take("V")
            pe.wait_ge(freed["V"][j % 4], pe.opens(j))
            bank = banks["V"][j % 4]
            eng.matmul(bank[:, 0:2], ones[128], small[:, 2:4], start=True, stop=True).then_inc(full["V"][j % 4], 1)

            def ffn(name, n, f):
                if on(name):
                    pe_norm(pe, n)
                    pe_ffn(pe, n, f)

            if on("mod0"):
                pe_mod(pe)
            ffn("f0a", TC, F1)
            if on("mix0"):
                eng.wait_ge(s_tab, 16)
                pe_norm(pe, TC)
                pe_mix0(pe)
            ffn("f0b", TC, F1)
            ffn("f1a", TC, F1)
            if on("mix1"):
                pe_norm(pe, TC)
                pe_mix1(pe)
            ffn("f1b", T, F1)
            for l in range(2):
                ffn(f"g{l}a", T, F2)
                if on(f"mix{2 + l}"):
                    pe_norm(pe, T)
                    plan[f"mix{2 + l}"] = pe.job["A"]
                    pe_mix2(pe, l)
                ffn(f"g{l}b", T, F2)
            if on("end"):
                pe_norm(pe, T)

        @block.scalar
        def _(eng):
            act = Hand(eng, plan)
            for dst, src in ((pk, "pack"), (const, "const"), (bmod, "bmod"), (cT, "cT")):
                eng.dma_start(dst[:], A[src]).then_inc(s_par, 16)
            eng.dma_start(xT[:], A["xT"]).then_inc(s_x, 16)
            eng.dma_start(shared[:, 0:sum(w for _, w in SHARED)], A["tab1"]).then_inc(s_tab, 16)
            eng.wait_ge(s_par, 16 * 4)
            act.wait_ge(v_a, act.next(v_a))
            eng.activation(small[:, 5:7], small[:, 5:7], ACT.Exp).then_inc(a_v, 1)
            eng.activation(cT[:], cT[:], ACT.Silu).then_inc(a_self, 1)
            act.wait_ge(a_self, act.next(a_self))
            if on("mod0"):
                eng.sem_inc(a_pe, 1)
                act_mod(act)

            def ffn(name, n, f, m):
                if on(name):
                    act_norm(act, n, m, split=True)
                    act_ffn(act, n, f)

            eng.wait_ge(s_x, 16)
            ffn("f0a", TC, F1, 1)
            if on("mix0"):
                act_norm(act, TC, 4)
                act_mix0(act)
                act.stage()
            ffn("f0b", TC, F1, 7)
            ffn("f1a", TC, F1, 1)
            if on("mix1"):
                act_norm(act, TC, 4)
                act_mix1(act)
                act.stage()
            ffn("f1b", T, F1, 7)
            for l in range(2):
                ffn(f"g{l}a", T, F2, None)
                if on(f"mix{2 + l}"):
                    act_norm(act, T, None)
                    act_mix2(act, l)
                    act.stage()
                ffn(f"g{l}b", T, F2, None)
            if on("end"):
                act_norm(act, T, None)

        @block.vector
        def _(eng):
            v = Hand(eng, plan)
            eng.wait_ge(s_par, 16 * 4)
            lam = par("lam", 0, 4)
            eng.tensor_tensor(small[:, 2:3], lam[:, 0:1], lam[:, 1:2], ALU.mult)
            v.eng.tensor_tensor(small[:, 3:4], lam[:, 2:3], lam[:, 3:4], ALU.mult).then_inc(v_pe, 1)
            eng.tensor_scalar(small[:, 4:5], par("sub"), 1.0 - LAM_INIT, None, ALU.mult)
            j = v.take("V")
            v.wait_ge(full["V"][j % 4], v.fills(j))
            bank = banks["V"][j % 4]
            eng.tensor_copy(small[:, 5:7], bank[:, 0:2]).then_inc(freed["V"][j % 4], 1)
            v.wait_ge(freed["V"][j % 4], v.frees(j))
            eng.sem_inc(v_a, 1)
            v.wait_ge(a_v, v.next(a_v))
            eng.tensor_tensor(small[:, 7:8], small[:, 5:6], small[:, 6:7], ALU.subtract).then_inc(v_self, 1)
            v.wait_ge(v_self, v.next(v_self))
            eng.tensor_scalar(small[:, 1:2], small[:, 7:8], LAM_INIT, -1.0, ALU.add, ALU.mult).then_inc(v_self, 1)
            v.wait_ge(v_self, v.next(v_self))
            eng.wait_ge(s_x, 16)

            def ffn(name, n, f, affine, gain, m):
                if on(name):
                    vec_norm(v, n, affine, gain, split=True)
                    vec_ffn(v, n, f, m)

            if on("mod0"):
                vec_mod(v)
            eng.sem_inc(x_made, KD // 2)
            ffn("f0a", TC, F1, 1, None, 2)
            if on("mix0"):
                eng.wait_ge(s_tab, 16)
                vec_norm(v, TC, 4)
                vec_mix0(v)
            ffn("f0b", TC, F1, 7, None, 8)
            if on("mod1"):
                vec_mods(v, 1, side_mods)
            ffn("f1a", TC, F1, 1, None, 2)
            if on("mix1"):
                vec_norm(v, TC, 4)
                eng.sem_inc(s_biasroom, 1)
                vec_mix1(v)
                eng.sem_inc(s_room, 1)
            ffn("f1b", T, F1, 7, None, 8)
            if on("g0a"):
                eng.wait_ge(s_tab2, 16)
            for l in range(2):
                ffn(f"g{l}a", T, F2, None, f"n1_{l}", None)
                if on(f"mix{2 + l}"):
                    vec_norm(v, T, None, f"nm_{l}")
                    vec_mix2(v, l)
                ffn(f"g{l}b", T, F2, None, f"n2_{l}", None)
            if on("end"):
                vec_norm(v, T, None, "final")

        @block.gpsimd
        def _(eng):
            g = Hand(eng, plan)
            if stop is not None:
                eng.wait_ge(s_tab, 16)
            if on("mix1"):
                eng.wait_ge(s_biasroom, 1)
                eng.dma_start(bias1, A["bias"]).then_inc(s_bias, 16)
            if on("g0a"):
                eng.wait_ge(s_room, 1)
                eng.dma_start(shared[:], A["tab2"]).then_inc(s_tab2, 16)
            for l in range(2):
                if on(f"mix{2 + l}"):
                    first = plan[f"mix{2 + l}"] + 30 + (12 if l else 9) + 6
                    g.wait_ge(v_g, g.next(v_g))
                    for lev in range(LEVELS):
                        if lev:
                            g.wait_ge(full["A"][(first + 3 * lev - 1) % 4], g.fills(first + 3 * lev - 1))
                        mask = cat["levelm"][:, lev * P:(lev + 1) * P]
                        for i in range(12):
                            ins = eng.tensor_tensor(NM[:, i, :], prod[:, i, 0:P], mask, ALU.mult)
                        ins.then_inc(g_pe, 1)

        @block.sync
        def _(eng):
            for s in range(WEIGHT_SLOTS):
                eng.sem_inc(used[s], 1)
            n = n_chunks if stop is None else plan["writer"].job["chunk"]
            whole = n // WEIGHT_SLOTS
            with eng.Fori(0, whole) as i:
                for s in range(WEIGHT_SLOTS):
                    eng.wait_ge(used[s], i + 1)
                    eng.dma_start(ring[:, s, :], A["stream"][bass.ds(i * WEIGHT_SLOTS + s, 1), :, :].rearrange("a p f -> (a p) f"))\
                       .then_inc(landed[s], 16)
            for s in range(n - whole * WEIGHT_SLOTS):
                eng.wait_ge(used[s], whole + 1)
                eng.dma_start(ring[:, s, :], A["stream"][whole * WEIGHT_SLOTS + s, :, :]).then_inc(landed[s], 16)
            if on("end"):
                eng.wait_ge(s_vdone, 1)
                eng.dma_start(A["out"], hT[:, :, 0:T]).then_inc(s_out, 16)
                eng.wait_ge(s_out, 16)

        assert plan["writer"].job["chunk"] == n_chunks or stop is not None


def _feature_major(a):
    a = np.asarray(a).reshape(-1, a.shape[-1])
    c = a.shape[-1]
    out = np.zeros((a.shape[0], -(-c // P) * P), np.float32)
    out[:, :c] = a
    return np.ascontiguousarray(out.reshape(a.shape[0], -1, P).transpose(2, 1, 0))


def _twice(g):
    return np.concatenate([g] * (P // g.shape[0]))[:, None]


def _columns(chunks, w, width=CH):
    kt = w.shape[0] // P
    for c in range(0, w.shape[1], width):
        part = w[:, c:c + width]
        out = np.zeros((P, kt, width), np.float32)
        out[:, :, :part.shape[1]] = part.reshape(kt, P, -1).transpose(1, 0, 2)
        flat = np.zeros((P, CHUNK), np.float32)
        flat[:, :kt * width] = out.reshape(P, -1)
        chunks.append(flat)


def _rows(chunks, w):
    for r in range(0, w.shape[0], CH):
        out = np.zeros((2, P, D), np.float32)
        part = w[r:r + CH]
        out.reshape(-1, D)[:part.shape[0]] = part
        chunks.append(out.transpose(1, 0, 2).reshape(P, -1))


def _ffn(chunks, g, u, d):
    for s in range(0, g.shape[1], SEG):
        for c in range(s, min(s + SEG, g.shape[1]), CH):
            _columns(chunks, g[:, c:c + CH])
            _columns(chunks, u[:, c:c + CH])
        _rows(chunks, d[s:s + SEG])


def _stream(I):
    ch = []
    heads = np.arange(512).reshape(8, 64)
    for l in range(2):
        if l == 0:
            _columns(ch, I["w_mod"][0])
        _ffn(ch, I["ffn1_w_gate"][l], I["ffn1_w_up"][l], I["ffn1_w_down"][l])
        if l == 0:
            w = I["ab_w_in"][0]
            aq, bq, ak, av, bk, bv = np.split(w, np.cumsum([512, 512, 128, 128, 512]), axis=1)
            pairs = np.concatenate([np.concatenate([heads[h], heads[h + 4]]) for h in range(4)])
            _columns(ch, np.concatenate([aq[:, pairs], bq, ak, bk, av, bv], axis=1))
            _columns(ch, I["w_mod"][1])
            _columns(ch, I["ab_w_out"][0])
        else:
            w = I["cd_w_in"][0]
            cq, dq, ckv, kr, dk, dv = np.split(w, np.cumsum([768, 512, 256, 32, 512]), axis=1)
            _columns(ch, np.concatenate([cq, dq, ckv, kr, kr, kr, kr, dk], axis=1))
            _columns(ch, dv)
            uq = I["c_w_uq"][0].reshape(768, 8, 96)
            _columns(ch, np.concatenate([uq[:, :, :64].reshape(768, 512), uq[:, :, 64:].reshape(768, 256)], axis=1))
            ukv = I["c_w_ukv"][0].reshape(256, 8, 128)
            _columns(ch, np.concatenate([ukv[:, :, :64].reshape(256, 512), ukv[:, :, 64:].reshape(256, 512)], axis=1), D)
            _columns(ch, I["cd_w_out"][0])
        _ffn(ch, I["ffn2_w_gate"][l], I["ffn2_w_up"][l], I["ffn2_w_down"][l])
    for l in range(2):
        _ffn(ch, I["ffn1_w_gate_2"][l], I["ffn1_w_up_2"][l], I["ffn1_w_down_2"][l])
        w = I["w_in_2"][l]
        rwkv, q, c, iq, ik, iw, rq, rk, rv, rg = np.split(w, np.cumsum([1280, 384, 128, 512, 64, 8, 256, 256, 256]), axis=1)
        mv = I["rwkv_vres_w_in_2"][0] if l else np.zeros((D, 16), np.float32)
        last = np.concatenate([mv, iw, np.zeros((D, P - 24), np.float32)], axis=1)
        w = np.concatenate([rwkv, q, c, iq, ik, ik, rq, rk, rg, last], axis=1)
        _columns(ch, w[:, P * (MV - 1):])
        _columns(ch, w[:, :P * (MV - 1)])
        _columns(ch, rv)
        _columns(ch, I["w_out_2"][l])
        _ffn(ch, I["ffn2_w_gate_2"][l], I["ffn2_w_up_2"][l], I["ffn2_w_down_2"][l])
    return np.stack(ch)


def _pack(I):
    PK, PW = param_layout()
    out = np.zeros((P, PW), np.float32)

    def put(name, a):
        at, w = PK[name]
        assert a.shape[1] == w, (name, a.shape, w)
        out[:a.shape[0], at:at + w] = a

    for n, key in (("a_q", "a_q_norm"), ("a_k", "a_k_norm"), ("b_q", "b_q_norm"), ("b_k", "b_k_norm"), ("sub", "b_sub_norm"),
                   ("c_qn", "c_q_nope_norm"), ("c_qr", "c_q_rope_norm"), ("c_kn", "c_k_nope_norm"), ("c_kr", "c_k_rope_norm"),
                   ("d_q", "d_q_norm"), ("d_k", "d_k_norm")):
        put(n, _twice(I[key][0]))
    put("sink", np.broadcast_to(I["a_sink"], (P, 8)))
    put("lam", np.stack([I[f"b_lambda_{n}"][0] for n in ("q1", "k1", "q2", "k2")], axis=1))
    put("c_qa", _feature_major(I["c_q_a_norm"])[:, :, 0])
    put("c_kva", _feature_major(I["c_kv_a_norm"])[:, :, 0])
    put("final", _feature_major(I["final_norm_2"][None])[:, :, 0])
    for n, value in (("one", 1.0), ("eps", EPS), ("gn_eps", GN_EPS)):
        put(n, np.full((P, 1), value, np.float32))
    for l in range(2):
        for n, key in (("n1_", "ffn1_norm_2"), ("nm_", "mix_norm_2"), ("n2_", "ffn2_norm_2"), ("mu_", "rwkv_mu_2"),
                       ("w0_", "rwkv_w0_2"), ("a0_", "rwkv_a0_2"), ("kk_", "rwkv_k_k_2"), ("ka_", "rwkv_k_a_2"),
                       ("lnw_", "rwkv_ln_w_2"), ("lnb_", "rwkv_ln_b_2"), ("kv_", "dsa_kv_norm_2")):
            put(f"{n}{l}", _feature_major(I[key][l][None])[:, :, 0])
        put(f"rk_{l}", _feature_major(I["rwkv_r_k_2"][l].reshape(1, -1))[:, :, 0])
        put(f"lora_{l}", np.concatenate([I["rwkv_w2_2"][l], I["rwkv_a2_2"][l], I["rwkv_g2_2"][l]]))
        put(f"uk_{l}", I["dsa_w_uk_2"][l].reshape(3, P, P).transpose(1, 0, 2).reshape(P, 384))
        put(f"uv_{l}", I["dsa_w_uv_2"][l].transpose(1, 0, 2).reshape(P, 384))
        if l:
            put(f"vmu_{l}", _feature_major(I["rwkv_vres_mu_2"][0][None])[:, :, 0])
            put(f"v0_{l}", _feature_major(I["rwkv_v0_2"][0][None])[:, :, 0])
            put(f"v2_{l}", I["rwkv_v2_2"][0])
    return out


def _constants():
    p = np.arange(P)
    parts = {"sel": (p[:, None] % 32 == np.arange(2)[None]) * 1.0, "ident": np.eye(P), "ones128": np.ones((P, P))}
    for g in (64, 32):
        parts[f"ones{g}"] = (p[:, None] // g == p[None] // g) * 1.0
    for h in (32, 16, 8):
        R = np.zeros((P, P))
        for i in p:
            if i % (2 * h) < h:
                R[i, i + h] = -1
            else:
                R[i, i - h] = 1
        parts[f"rot{h}"] = R.T
    return np.concatenate([parts[n] for n, _ in CONST], axis=1).astype(np.float32)


def _axial(nf):
    f32 = np.float32
    i = np.arange(P) % (4 * nf)
    inv = (f32(10000.0) ** (-np.arange(nf, dtype=f32) / f32(nf)))[i % nf]
    t = np.arange(T)
    pos = np.where((i // (2 * nf) == 0)[:, None], (t // 64)[None], (t % 64)[None]).astype(f32)
    ang = pos * inv[:, None]
    cos, sin = np.ones((P, TC), f32), np.zeros((P, TC), f32)
    cos[:, :T], sin[:, :T] = np.cos(ang), np.sin(ang)
    return cos, sin


def _tables():
    f32 = np.float32
    q, k = np.arange(T)[:, None], np.arange(T)[None]
    am = np.where(np.abs(q - k) <= 128, 0.0, NEG).reshape(2, P, T).transpose(1, 0, 2).reshape(P, -1)
    first = np.concatenate([am, *_axial(16), *_axial(8)], axis=1).astype(f32)
    i = np.arange(P) % 32
    theta = f32(10000.0) ** (-np.linspace(0.0, 1.0, 32, dtype=f32))
    ang = theta[i][:, None] * np.arange(T, dtype=f32)[None]
    gamma = np.log(1.0 - 2.0 ** (-5.0 - np.arange(4)))
    d = np.arange(T)[None] - np.arange(P)[:, None]
    one = [np.where(d >= 0, np.exp(np.maximum(d, 0) * g), 0.0) * 0.125 for g in gamma]
    retm = np.concatenate([np.concatenate([m, m[:, :P]], axis=1) for m in one], axis=1)
    s, t = np.arange(P)[:, None], np.arange(P)[None]
    same = s // RC == t // RC
    prodm = np.concatenate([same & (s < t), same & (s <= t)] * 2, axis=1) * 1.0
    levels = []
    for j in range(LEVELS):
        b = 2 << j
        levels.append((s // b == t // b) & (s % b < b // 2) & (t % b >= b // 2))
    scan = np.broadcast_to((np.arange(768) % RC != 0) * 1.0, (P, 768))
    causal = np.where(k <= q, 0.0, NEG).reshape(2, P, T).transpose(1, 0, 2).reshape(P, -1)
    second = np.concatenate([np.cos(ang), np.sin(ang), retm, prodm, np.concatenate(levels, axis=1) * 1.0, scan, causal],
                            axis=1).astype(f32)
    return first, second


def _bias(rpb):
    q, k = np.arange(T)[:, None], np.arange(T)[None]
    start = np.clip(q % 64 - 8, 0, 48)
    inside = (k % 64 >= start) & (k % 64 < start + 16)
    dr = k // 64 - q // 64 + 7
    dc = np.clip(k % 64 - q % 64, -15, 15) + 15
    out = np.full((8, T, T), NEG, np.float32)
    out[:, inside] = rpb[:, dr[inside], dc[inside]]
    return np.ascontiguousarray(out.reshape(8, 2, P, T).transpose(2, 0, 1, 3).reshape(P, 16, T))


def layout(inputs):
    I = {n: np.asarray(a) for n, a in inputs.items()}
    first, second = _tables()
    xt = np.concatenate([I["x"][0], I["ctx"][0]])
    b = [_feature_major(I["b_mod"][l][None])[:, :, 0] for l in range(2)]
    return {
        "stream": _stream(I), "pack": _pack(I), "const": _constants(), "tab1": first, "tab2": second,
        "bias": _bias(I["d_rpb"][0]), "xT": _feature_major(xt), "cT": np.pad(_feature_major(np.stack([I["c"][0], I["c_ctx"]])), ((0, 0), (0, 0), (0, 30))),
        "bmod": np.ascontiguousarray(np.repeat(np.stack(b, axis=1), 2, axis=2)),
    }


def kernel(**inputs):
    import concourse.bacc as bacc
    from concourse.bass_utils import run_bass_kernel_spmd as run

    nc = bacc.Bacc("TRN2", target_bir_lowering=False, num_devices=1)
    arrays = layout(inputs)
    A = {n: nc.dram_tensor(f"in_{n}", a.shape, F32, kind="ExternalInput").ap() for n, a in arrays.items()}
    A["out"] = nc.dram_tensor("out_0", [P, KD, T], F32, kind="ExternalOutput").ap()
    build(nc, A)
    r = run(nc, [{f"in_{n}": a for n, a in arrays.items()}], core_ids=[0])
    out = r.results[0]["out_0"]
    return np.ascontiguousarray(out.transpose(2, 1, 0).reshape(1, T, D))
```

```python
from contextlib import ExitStack, contextmanager

import numpy as np
import concourse.bass as bass
from concourse import mybir

F32 = mybir.dt.float32
ALU = mybir.AluOpType
ACT = mybir.ActivationFunctionType
AX = mybir.AxisListType

P = 128
D = 1024
KD = D // P
T = 256
TC = 512
CH = 256
CHUNK = KD * CH
WEIGHT_SLOTS = 4
N_MOD = 9
F1, F2 = 2816, 2752
SEG = 1024
SEG_TURNS = 2
BESIDE = 8
MOD_FIRST = 3
MOD_CH = D // CH
FR = mybir.dt.float32r
EPS = 1e-6
GN_EPS = 64e-5
NEG = -1e30
TAKEN = -3e38
TOPK = 64
PICKS = TOPK // 8 + 1
LAM_INIT = 0.8 - 0.6
DEEP = 3
LAG = 3
HEADS_R = 6
RC = 64
LEVELS = 6
DECAY = float(np.exp(-0.5))
LORA, MV = 9, 25

AQ, BQ, AK, BK = 0, 4, 8, 9
CQ, DQ, CKV, KR, DK = 0, 6, 10, 12, 13
RR, RK, RV, SQ, SC, SIQ, SIK, TQ, TK, TG = 0, 3, 6, 10, 13, 14, 18, 19, 21, 23


def param_layout():
    widths = [("a_q", 1), ("a_k", 1), ("b_q", 1), ("b_k", 1), ("sub", 1), ("sink", 8), ("lam", 4),
              ("c_qa", 6), ("c_kva", 2), ("c_qn", 1), ("c_qr", 1), ("c_kn", 1), ("c_kr", 1), ("d_q", 1), ("d_k", 1),
              ("final", 8), ("one", 1), ("eps", 1), ("gn_eps", 1)]
    for l in range(2):
        widths += [(f"{n}{l}", w) for n, w in (
            ("n1_", 8), ("nm_", 8), ("n2_", 8), ("mu_", 10), ("w0_", 3), ("a0_", 3), ("kk_", 3), ("ka_", 3),
            ("rk_", 3), ("lnw_", 3), ("lnb_", 3), ("kv_", 1), ("vmu_", 1), ("v0_", 3),
            ("lora_", 384), ("v2_", 384), ("uk_", 384), ("uv_", 384))]
    out, at = {}, 0
    for n, w in widths:
        out[n] = (at, w)
        at += w
    return out, at


def beside(cols):
    n = 2 * -(-cols // CH)
    return [1 + (0 < q <= BESIDE - n) for q in range(n)]


CONST = [("ident", 128), ("ones128", 128), ("ones64", 128), ("ones32", 128), ("rot32", 128), ("rot16", 128),
         ("rot8", 128), ("sel", 2)]
SHARED = [("amask", 512), ("cosh", TC), ("sinh", TC), ("cosm", TC), ("sinm", TC)]
SHARED2 = [("cosr", T), ("sinr", T), ("retm", 4 * 384), ("prodm", 512), ("levelm", LEVELS * 128), ("scanm", 768),
           ("causal", 2 * T)]


class Hand:

    def __init__(self, eng, plan):
        self.eng, self.plan = eng, plan
        self.wait_ge = eng.wait_ge
        self.seen, self.per = {}, {}
        self.turn, self.stages, self.per_turn = None, 0, {}
        self.job = {"A": 0, "V": 0, "chunk": 0, "split": 0}

    def next(self, sem, n=1):
        self.seen[sem] = self.seen.get(sem, 0) + n
        return self.seen[sem] if self.turn is None or not self.per.get(sem) else self.turn * self.per[sem] + self.seen[sem]

    @contextmanager
    def repeat(self, turns, jobs, per=None):
        per = per or {}
        before = dict(self.seen)
        with self.eng.Fori(0, turns) as i:
            self.turn, self.per, self.per_turn = i, per, jobs
            yield i
        for sem, n in self.seen.items():
            assert n - before.get(sem, 0) == per.get(sem, 0), (sem, n - before.get(sem, 0))
        self.turn = None
        for sem, n in per.items():
            self.seen[sem] += n * (turns - 1)
        for kind, n in jobs.items():
            self.job[kind] += n * (turns - 1)

    def take(self, pool):
        self.job[pool] += 1
        return self.job[pool] - 1

    def _turns(self, value, kind):
        return value if self.turn is None else self.turn * (self.per_turn[kind] // 4) + value

    def opens(self, job, pool="A"):
        return self._turns(job // 4 + 1, pool)

    def fills(self, job, pool="A"):
        return self._turns(job // 4 + 1, pool)

    def frees(self, job, pool="A"):
        return self._turns(job // 4 + 2, pool)

    def lands(self, chunk):
        value = 16 * (chunk // WEIGHT_SLOTS + 1)
        return value if self.turn is None else self.turn * (4 * self.per_turn["chunk"]) + value

    def splits(self, chunk):
        return self._turns(chunk // WEIGHT_SLOTS + 2, "chunk")

    def uses(self, split):
        return split if self.turn is None else self.turn * self.per_turn["split"] + split

    def stage(self):
        if self.plan["writer"] is self:
            self.plan[self.stages] = dict(self.job)
        else:
            self.job = dict(self.plan[self.stages])
        self.stages += 1


def build(nc, A):
    PK, PW = param_layout()
    n_chunks = A["stream"].shape[0]
    ctx = ExitStack()
    with ctx:
        def sb(name, shape):
            return ctx.enter_context(nc.sbuf_tensor(name, shape, F32))

        def sem(name):
            return ctx.enter_context(nc.semaphore(name))

        xT = sb("xT", [P, KD, TC])
        ring = sb("ring", [P, WEIGHT_SLOTS, CHUNK])
        pk = sb("pk", [P, PW])
        mods = sb("mods", [P, 72, 2])
        bmod = sb("bmod", [P, 2, 144])
        cT = sb("cT", [P, KD, 32])
        const = sb("const", [P, sum(w for _, w in CONST)])
        shared = sb("shared", [P, sum(w for _, w in SHARED2)])
        vfirst = sb("vfirst", [P, 3, T])
        small = sb("small", [P, 64])
        ARENA = 25616
        hT_at = -(-nc.sbuf_base // 32) * 32
        hT = sb("hT", [P, KD, TC])
        arena_at = hT_at + 4 * KD * TC
        arena = sb("arena", [P, ARENA])

        def over(name, at, shape):
            return nc.alloc_sbuf_tensor_at(name, shape, FR, offset=at)

        h_hi = over("h_hi", hT_at, [P, KD, TC])
        h_lo = over("h_lo", arena_at, [P, KD, TC])
        hid_hi = over("hid_hi", arena_at + 4 * 4096, [P, SEG // P, TC])
        hid_lo = over("hid_lo", arena_at + 4 * 8192, [P, SEG // P, TC])
        w_hi = over("w_hi", arena_at + 4 * 12288, [P, 2, CHUNK])
        w_lo = over("w_lo", arena_at + 4 * 16384, [P, 2, CHUNK])

        banks = {p: [ctx.enter_context(nc.psum_tensor(f"bank{p}{b}", [P, 512], F32)) for b in range(4)] for p in "AV"}
        full = {p: [sem(f"full_{p}{b}") for b in range(4)] for p in "AV"}
        freed = {p: [sem(f"freed_{p}{b}") for b in range(4)] for p in "AV"}
        landed = [sem(f"chunk_landed{s}") for s in range(WEIGHT_SLOTS)]
        used = [sem(f"chunk_used{s}") for s in range(WEIGHT_SLOTS)]
        s_par, s_x, s_tab, s_tab2 = sem("params_in"), sem("x_in"), sem("tables1_in"), sem("tables2_in")
        s_bias, s_biasroom, s_room = sem("biases_in"), sem("biases_room"), sem("tables2_room")
        s_out, s_vdone = sem("out_stored"), sem("out_ready")
        v_self, a_self, pe_self = sem("vector_step"), sem("scalar_step"), sem("tensor_step")
        v_pe, a_pe = sem("vector_made_operand"), sem("scalar_made_operand")
        v_a, a_v = sem("vector_made_for_scalar"), sem("scalar_made_for_vector")
        v_g, g_pe = sem("vector_made_for_pool"), sem("pool_made_operand")
        mod_turn = sem("modulation_turn")
        x_made, h_made = sem("x_tiles_made"), sem("h_tile_made")
        side_read = sem("side_modulation_read")
        head_summed = sem("index_head_summed")
        split_used, hi_made = sem("split_used"), sem("leading_part_made")
        plan = {"writer": None}

        def par(name, i=0, n=1, rows=slice(0, P)):
            at = PK[name][0] + i
            return pk[rows, at:at + n]

        cat = {}
        for tensor, items in ((const, CONST), (shared, SHARED2)):
            at = 0
            for n, w in items:
                cat[n] = tensor[:, at:at + w]
                at += w
        at = 0
        for n, w in SHARED:
            cat[n] = shared[:, at:at + w]
            at += w
        ones = {128: cat["ones128"], 64: cat["ones64"], 32: cat["ones32"]}

        def room(at, *shape):
            n = int(np.prod(shape))
            assert at + n <= ARENA, (at, shape)
            v = arena[:, at:at + n]
            if len(shape) == 2:
                v = v.rearrange("p (a b) -> p a b", a=shape[0])
            if len(shape) == 3:
                v = v.rearrange("p (a b c) -> p a b c", a=shape[0], b=shape[1])
            return v, at + n

        squares, _ = room(0, KD, TC)
        silb, _end = room(20480, 4, TC)
        hid32, _end = room(_end, 2, TC)
        rsum, _ = room(22528, TC)
        assert _end <= 24064
        cond_rows, _ = room(0, 4, CH)
        side_mods, _ = room(24064, 4 * N_MOD * 4)
        side_rows, _ = room(24064 + 4 * N_MOD * 4, 2, CH)

        def groups(n):
            return [(0, 0)] if n == T else [(0, 0), (1, T)]

        def pe_norm(pe, n):
            pe.stage()
            j = pe.take("V")
            pe.wait_ge(freed["V"][j % 4], pe.opens(j))
            bank = banks["V"][j % 4]
            stream.let_go()
            for k in range(KD):
                if k % 2 == 0:
                    pe.wait_ge(a_pe, pe.next(a_pe))
                ins = stream.mm(pe, bank[:, 0:n], ones[128], squares[:, k, 0:n], k == 0, k == KD - 1)
            ins.then_inc(full["V"][j % 4], 1)

        FFN = {"h_lo": h_lo, "ahead": 0}
        FFN_SIDE = {"h_lo": h_lo, "ahead": 1}
        SPLIT0 = {"name": "split0", "hi": w_hi, "h_lo": over("mix0_h_lo", arena_at + 4 * 16384, [P, KD, TC]),
                  "lo": [over("mix0_w_lo0", arena_at + 4 * (ARENA - CHUNK), [P, CHUNK]),
                         over("mix0_w_lo1", arena_at + 4 * 20480, [P, CHUNK])]}

        def act_norm(act, n, affine, split=None):
            act.stage()
            if split in (FFN, FFN_SIDE):
                act_hi(act, split["ahead"], 0)
            for k in range(0, KD, 2):
                act.wait_ge(x_made, act.next(x_made))
                act.eng.activation(squares[:, k:k + 2, 0:n], xT[:, k:k + 2, 0:n], ACT.Square).then_inc(a_pe, 1)
            act_root(act, act.take("V"), rsum[:, 0:n], D, par("eps"))
            if split and split not in (FFN, FFN_SIDE):
                act_first(act, split, 0)
            for k in range(KD if affine or split else 0):
                act.wait_ge(v_a, act.next(v_a))
                out = silb[:, k % 4, :] if split else hT[:, k, :]
                if affine:
                    for g, o in groups(n):
                        ins = act.eng.activation(out[:, o:o + T], out[:, o:o + T], ACT.Identity,
                                                 bias=mods[:, 8 * (affine - 1) + k, g:g + 1],
                                                 scale=mods[:, 8 * affine + k, g:g + 1])
                if split:
                    if affine:
                        ins.then_inc(a_self, 1)
                        act.wait_ge(a_self, act.next(a_self))
                    act.eng.activation(h_hi[:, k, 0:n], out[:, 0:n], ACT.Copy).then_inc(a_v, 1)
                else:
                    ins.then_inc(h_made, 1)

        def act_first(act, S, i):
            c, sp = plan[S["name"]]["chunk"] + i, plan[S["name"]]["split"] + i
            act.wait_ge(landed[c % WEIGHT_SLOTS], act.lands(c))
            act.wait_ge(split_used, act.uses(sp))
            act.eng.activation(S["hi"][:, i % 2, :], ring[:, c % WEIGHT_SLOTS, :], ACT.Copy).then_inc(hi_made, 1)

        def pool_rest(g, S, n):
            at = plan[S["name"]]
            for i in range(n):
                if i == 1:
                    g.wait_ge(h_made, at["h"])
                g.wait_ge(hi_made, at["split"] + i + 1)
                if i >= 2:
                    g.wait_ge(split_used, at["split"] + i)
                slot = (at["chunk"] + i) % WEIGHT_SLOTS
                g.eng.tensor_tensor(S["lo"][i % 2][:, :], ring[:, slot, :], S["hi"][:, i % 2, :].bitcast(F32),
                                    ALU.subtract).then_inc(used[slot], 1)

        def pe_split_next(pe, S):
            i = pe.job["split"] - plan[S["name"]]["split"]
            pe.wait_ge(hi_made, pe.job["split"] + 1)
            chunk = {"slot": pe.job["chunk"] % WEIGHT_SLOTS, "whole": pe.splits(pe.job["chunk"]), "fresh": True, "rest": False}
            chunk["hi"], chunk["lo"] = by_k(S["hi"][:, i % 2, :]), by_k(S["lo"][i % 2][:, :])
            pe.job["chunk"] += 1
            pe.job["split"] += 1
            return chunk

        def pe_split(pe, S, chunk, out, cols, tokens, rows=False, first=False):
            h = {"hi": h_hi, "lo": S["h_lo"]}
            steps = [("hi", part, k) for k in range(KD) for part in ("lo", "hi")] + [("lo", "hi", k) for k in range(KD)]
            for i, (wp, hp, k) in enumerate(steps):
                if first and hp == "lo":
                    pe.wait_ge(h_made, pe.next(h_made))
                if wp == "lo" and not chunk["rest"]:
                    pe.wait_ge(used[chunk["slot"]], chunk["whole"])
                    chunk["rest"] = True
                w, m = chunk[wp][:, k, cols], h[hp][:, k, tokens]
                ins = pe.eng.matmul(out, m if rows else w, w if rows else m, start=i == 0, stop=i == len(steps) - 1)
                if chunk["fresh"]:
                    ins.then_inc(split_used, 1)
                    chunk["fresh"] = False
            return ins

        def pe_split_tile(pe, S, chunk, c, w, n, first=False):
            j = pe.take("A")
            pe.wait_ge(freed["A"][j % 4], pe.opens(j))
            pe_split(pe, S, chunk, banks["A"][j % 4][0:w, 0:n], slice(c, c + w), slice(0, n),
                     first=first).then_inc(full["A"][j % 4], 1)

        def pe_split_rows(pe, S, chunk, c, w, n):
            for tt in range(n // P):
                j = pe.take("A")
                pe.wait_ge(freed["A"][j % 4], pe.opens(j))
                pe_split(pe, S, chunk, banks["A"][j % 4][:, 0:w], slice(c, c + w), slice(tt * P, tt * P + P),
                         rows=True).then_inc(full["A"][j % 4], 1)

        def act_hi(act, ahead, split):
            c, sp = act.job["chunk"] + ahead, act.job["split"] + split
            act.wait_ge(landed[c % WEIGHT_SLOTS], act.lands(c))
            if sp:
                act.wait_ge(split_used, act.uses(sp))
            act.eng.activation(w_hi[:, sp % 2, :], ring[:, c % WEIGHT_SLOTS, :], ACT.Copy).then_inc(hi_made, 1)

        def vec_lo(v, ahead, split):
            c, sp = v.job["chunk"] + ahead, v.job["split"] + split
            v.wait_ge(hi_made, v.next(hi_made))
            v.eng.tensor_tensor(w_lo[:, sp % 2, :], ring[:, c % WEIGHT_SLOTS, :], w_hi[:, sp % 2, :].bitcast(F32),
                                ALU.subtract).then_inc(used[c % WEIGHT_SLOTS], 1)

        def act_root(act, job, out, over, eps):
            act.wait_ge(full["V"][job % 4], act.fills(job))
            bank = banks["V"][job % 4]
            act.eng.activation(out, bank[:, 0:out.shape[1]], ACT.Sqrt, bias=eps, scale=1.0 / over).then_inc(freed["V"][job % 4], 1)

        def vec_norm(v, n, affine=None, gain=None, split=None):
            v.stage()
            if split in (FFN, FFN_SIDE):
                v.seen[hi_made] = v.job["split"]
                vec_lo(v, split["ahead"], 0)
            j = v.take("V")
            v.wait_ge(freed["V"][j % 4], v.frees(j))
            v.eng.reciprocal(rsum[:, 0:n], rsum[:, 0:n]).then_inc(v_self, 1)
            v.wait_ge(v_self, v.next(v_self))
            for k in range(KD + 2 * bool(split)):
                if k < KD:
                    out = silb[:, k % 4, 0:n] if split else hT[:, k, 0:n]
                    if affine:
                        ins = v.eng.tensor_tensor(out, xT[:, k, 0:n], rsum[:, 0:n], ALU.mult)
                    else:
                        ins = v.eng.scalar_tensor_tensor(out, xT[:, k, 0:n], par(gain, k), rsum[:, 0:n], ALU.mult, ALU.mult)
                    if affine or split:
                        ins.then_inc(v_self, 1)
                        v.wait_ge(v_self, v.next(v_self))
                        v.eng.sem_inc(v_a, 1)
                    elif gain != "final":
                        ins.then_inc(h_made, 1)
                if split and k >= 2:
                    v.wait_ge(a_v, v.next(a_v))
                    v.eng.tensor_tensor(split["h_lo"][:, k - 2, 0:n], silb[:, (k - 2) % 4, 0:n], h_hi[:, k - 2, 0:n].bitcast(F32),
                                        ALU.subtract).then_inc(h_made, 1)
            if gain == "final":
                ins.then_inc(s_vdone, 1)

        class Stream:

            def __init__(self):
                self.pending, self.held = None, None

            def next(self, pe):
                c = pe.job["chunk"]
                pe.job["chunk"] += 1
                pe.wait_ge(landed[c % WEIGHT_SLOTS], pe.lands(c))
                self.pending, self.held = self.held, c % WEIGHT_SLOTS
                return ring[:, c % WEIGHT_SLOTS, :]

            def mm(self, pe, out, lhsT, rhs, start, stop):
                ins = pe.eng.matmul(out, lhsT, rhs, start=start, stop=stop)
                if self.pending is not None:
                    ins.then_inc(used[self.pending], 1)
                    self.pending = None
                return ins

            def let_go(self):
                self.pending, self.held = self.held, None

        stream = Stream()

        def by_k(chunk, kt=KD, w=CH):
            return chunk[:, 0:kt * w].rearrange("p (k c) -> p k c", k=kt)

        def segment(cols):
            out = []
            for c in range(0, cols, CH):
                tiles = [(q, min(P, cols - c - q)) for q in range(0, min(CH, cols - c), P)]
                out += [("gate", tiles), ("up", tiles)]
            return out + [("down", [(q, min(P, cols - c - q)) for q in range(0, min(CH, cols - c), P)])
                          for c in range(0, cols, CH)]

        def per_segment(side):
            return {"A": 12 + 2 * BESIDE * side, "V": 12, "chunk": 12 + BESIDE * side, "split": 12}

        def sides(cols, side):
            return (beside(cols) if side else []) + [0] * 12

        def pe_side_rows(pe):
            w = by_k(stream.next(pe))
            j = pe.take("A")
            pe.wait_ge(freed["A"][j % 4], pe.opens(j))
            for k in range(KD):
                g = slice(32 * (k % 4), 32 * (k % 4) + 32)
                ins = stream.mm(pe, banks["A"][j % 4][g, 0:CH], cT[:, k, :], w[:, k, :], k < 4, k >= 4)
            ins.then_inc(full["A"][j % 4], 1)
            return j

        def pe_side_sums(pe, rows, i):
            pe.wait_ge(freed["A"][rows % 4], pe.frees(rows))
            j = pe.take("A")
            pe.wait_ge(freed["A"][j % 4], pe.opens(j))
            for t in range(2):
                ins = stream.mm(pe, banks["A"][j % 4][:, 2 * t:2 * t + 2], side_rows[:, i % 2, t * P:(t + 1) * P],
                                cat["sel"], True, True)
            ins.then_inc(full["A"][j % 4], 1)

        def pe_ffn(pe, n, f, side=False):
            pe.stage()

            h_tiles = [pe.next(h_made) for _ in range(KD)]

            def products(out, w, wc, rhs, start, stop, first):
                hi, lo = w
                a, b = rhs
                pairs = ((lo, a), (hi, b), (hi, a))
                for q, (l, r) in enumerate(pairs):
                    ins = pe.eng.matmul(out, l[wc], r, start=start and q == 0, stop=stop and q == 2)
                    if first and q == 0:
                        ins.then_inc(split_used, 1)
                    if first and q == 1 and stream.held is not None:
                        stream.let_go()
                        ins.then_inc(used[stream.pending], 1)
                        stream.pending = None
                return ins

            def run(cols):
                hidden_at = 0
                jobs = None
                chunks = segment(cols)
                waiting, turned = [], 0
                for i, (kind, tiles) in enumerate(chunks):
                    for rows in waiting:
                        pe_side_sums(pe, rows, turned)
                        turned += 1
                    waiting = [pe_side_rows(pe) for _ in range(sides(cols, side)[i])]
                    c, b = pe.job["chunk"], pe.job["split"] % 2
                    pe.job["chunk"] += 1
                    pe.job["split"] += 1
                    if kind == "down":
                        if jobs is None:
                            jobs = []
                            for p in "AAAAVVVV":
                                j = pe.take(p)
                                pe.wait_ge(freed[p][j % 4], pe.opens(j, p))
                                jobs.append((p, j))
                            hidden_at = 0
                        pe.wait_ge(v_pe, pe.next(v_pe))
                    pe.wait_ge(used[c % WEIGHT_SLOTS], pe.splits(c))
                    if kind == "down":
                        w = [m[:, b, :].rearrange("p (r c) -> p r c", r=2) for m in (w_hi, w_lo)]
                        for q, (_, rows) in enumerate(tiles):
                            r = slice(0, rows)
                            rhs = [m[r, hidden_at, 0:n] for m in (hid_hi, hid_lo)]
                            last = i == len(chunks) - 1 and q == len(tiles) - 1
                            for t, (p, j) in enumerate(jobs):
                                ins = products(banks[p][j % 4][:, 0:n], w, (r, q, slice(t * P, t * P + P)), rhs,
                                               hidden_at == 0, last, q == 0 and t == 0)
                                if last:
                                    ins.then_inc(full[p][j % 4], 1)
                            hidden_at += 1
                        continue
                    w = [m[:, b, :].rearrange("p (k c) -> p k c", k=KD) for m in (w_hi, w_lo)]
                    p = "A" if kind == "gate" else "V"
                    for q, (col, width) in enumerate(tiles):
                        j = pe.take(p)
                        pe.wait_ge(freed[p][j % 4], pe.opens(j, p))
                        for k in range(KD):
                            if i == 0 and q == 0:
                                pe.wait_ge(h_made, h_tiles[k])
                            ins = products(banks[p][j % 4][0:width, 0:n], w, (slice(0, P), k, slice(col, col + width)),
                                           [m[:, k, 0:n] for m in (h_hi, h_lo)], k == 0, k == KD - 1, q == 0 and k == 0)
                        ins.then_inc(full[p][j % 4], 1)

            with pe.repeat(SEG_TURNS, per_segment(side), {v_pe: 4}):
                run(SEG)
            run(f - SEG_TURNS * SEG)

        def act_ffn(act, n, f, side=False):
            act.stage()

            def run(cols, end):
                at, chunks = 0, segment(cols)
                b = sides(cols, side)
                rows, turned = 0, 0
                for i, (kind, tiles) in enumerate(chunks):
                    for _ in range(b[i - 1] if i else 0):
                        j = act.take("A")
                        act.wait_ge(full["A"][j % 4], act.fills(j))
                        at_ = 4 * (MOD_FIRST * MOD_CH + turned)
                        dst = side_mods[:, at_ + 4 * BESIDE * SEG_TURNS:at_ + 4 * BESIDE * SEG_TURNS + 4] if act.turn is None else \
                            side_mods[:, bass.ds(act.turn * (4 * BESIDE) + at_, 4)]
                        act.eng.activation(dst, banks["A"][j % 4][:, 0:4], ACT.Copy).then_inc(freed["A"][j % 4], 1)
                        turned += 1
                    for _ in range(b[i]):
                        j = act.take("A")
                        act.wait_ge(full["A"][j % 4], act.fills(j))
                        act.eng.activation(side_rows[:, rows % 2, :], banks["A"][j % 4][:, 0:CH], ACT.Copy).then_inc(freed["A"][j % 4], 1)
                        rows += 1
                    act.job["chunk"] += b[i]
                    if not end or i < len(chunks) - 1:
                        act_hi(act, 1 + (b[i + 1] if i < len(chunks) - 1 else b[0]), 1)
                    act.job["chunk"] += 1
                    act.job["split"] += 1
                    if kind == "gate":
                        for _, w in tiles:
                            j = act.take("A")
                            act.wait_ge(full["A"][j % 4], act.fills(j))
                            act.eng.activation(silb[0:w, j % 4, 0:n], banks["A"][j % 4][0:w, 0:n],
                                               ACT.Silu).then_inc(freed["A"][j % 4], 1)
                    if kind == "up":
                        for q, (_, w) in enumerate(tiles):
                            act.wait_ge(v_a, act.next(v_a))
                            act.eng.activation(hid_hi[0:w, at, 0:n], hid32[0:w, q, 0:n], ACT.Copy).then_inc(a_v, 1)
                            at += 1
                act.job["A"] += 4

            with act.repeat(SEG_TURNS, per_segment(side), {v_a: 8}):
                run(SEG, False)
            run(f - SEG_TURNS * SEG, True)

        def vec_ffn(v, n, f, m, side=False):
            v.stage()

            def run(cols, end):
                at, chunks = 0, segment(cols)
                b = sides(cols, side)
                for i, (kind, tiles) in enumerate(chunks):
                    v.job["chunk"] += b[i]
                    v.job["A"] += b[i] + (b[i - 1] if i else 0)
                    if not end or i < len(chunks) - 1:
                        vec_lo(v, 1 + (b[i + 1] if i < len(chunks) - 1 else b[0]), 1)
                    v.job["chunk"] += 1
                    v.job["split"] += 1
                    if kind == "gate":
                        gates = [v.take("A") for _ in tiles]
                    if kind != "up":
                        continue
                    for q, (_, w) in enumerate(tiles):
                        jv, ja = v.take("V"), gates[q]
                        v.wait_ge(freed["A"][ja % 4], v.frees(ja))
                        v.wait_ge(full["V"][jv % 4], v.fills(jv, "V"))
                        v.eng.tensor_tensor(hid32[0:w, q, 0:n], silb[0:w, ja % 4, 0:n], banks["V"][jv % 4][0:w, 0:n],
                                            ALU.mult).then_inc(freed["V"][jv % 4], 1)
                        v.wait_ge(freed["V"][jv % 4], v.frees(jv, "V"))
                        v.eng.sem_inc(v_a, 1)
                    for q, (_, w) in enumerate(tiles):
                        v.wait_ge(a_v, v.next(a_v))
                        v.eng.tensor_tensor(hid_lo[0:w, at, 0:n], hid32[0:w, q, 0:n], hid_hi[0:w, at, 0:n].bitcast(F32),
                                            ALU.subtract).then_inc(v_self, 1)
                        v.wait_ge(v_self, v.next(v_self))
                        at += 1
                    v.eng.sem_inc(v_pe, 1)
                add_to_x(v, [("A", v.take("A")) for _ in range(4)] + [("V", v.take("V")) for _ in range(4)], n, m, end)

            with v.repeat(SEG_TURNS, per_segment(side), {hi_made: 12, a_v: 8, v_self: 8}):
                run(SEG, False)
            run(f - SEG_TURNS * SEG, True)

        def add_to_x(v, jobs, n, m, last):
            for c, (p, j) in enumerate(jobs):
                v.wait_ge(full[p][j % 4], v.fills(j, p))
                bank = banks[p][j % 4]
                for g, o in groups(n):
                    s = 0.5 if m is None else 1.0 if m == "one" else mods[:, 8 * m + c, g:g + 1]
                    ins = v.eng.scalar_tensor_tensor(xT[:, c, o:o + T], bank[:, o:o + T], s, xT[:, c, o:o + T],
                                                     ALU.mult, ALU.add)
                ins.then_inc(freed[p][j % 4], 1)
                v.wait_ge(freed[p][j % 4], v.frees(j, p))
                if last and c % 2:
                    v.eng.sem_inc(x_made, 1)

        def pe_tiles(pe, chunk, kt, tiles, rhs_of, first=False):
            for q, (c, w, n) in enumerate(tiles):
                j = pe.take("A")
                pe.wait_ge(freed["A"][j % 4], pe.opens(j))
                bank = banks["A"][j % 4]
                for k in range(kt):
                    if first and q == 0:
                        pe.wait_ge(h_made, pe.next(h_made))
                    ins = stream.mm(pe, bank[0:w, 0:n], chunk[:, k, c:c + w], rhs_of(k, n), k == 0, k == kt - 1)
                ins.then_inc(full["A"][j % 4], 1)

        def pe_rows(pe, chunk, kt, c, w, n, lhs_of):
            for tt in range(n // P):
                j = pe.take("A")
                pe.wait_ge(freed["A"][j % 4], pe.opens(j))
                bank = banks["A"][j % 4]
                for k in range(kt):
                    ins = stream.mm(pe, bank[:, 0:w], lhs_of(k, tt), chunk[:, k, c:c + w], k == 0, k == kt - 1)
                ins.then_inc(full["A"][j % 4], 1)

        def act_out(act, dst, rows=slice(0, P), width=None, func=ACT.Copy, bias=None, scale=1.0, skip=0):
            j = act.take("A")
            act.wait_ge(full["A"][j % 4], act.fills(j))
            bank = banks["A"][j % 4]
            src = bank[rows, skip:width]
            if len(dst.shape) == 3:
                src = src.rearrange("p (a b) -> p a b", a=dst.shape[1])
            if bias is None:
                ins = act.eng.activation(dst, src, func, scale=scale)
            else:
                ins = act.eng.activation(dst, src, func, bias=bias, scale=scale)
            ins.then_inc(freed["A"][j % 4], 1)
            return j

        def pe_heads(pe, items, sq):
            pe.stage()
            for i in range(len(items) + 1):
                pe_heads_step(pe, items, sq, i)
            pe.wait_ge(v_pe, pe.next(v_pe))

        def pe_heads_step(pe, items, sq, i):
            if i < len(items):
                it = items[i]
                if it["size"]:
                    j = pe.take("V")
                    pe.wait_ge(freed["V"][j % 4], pe.opens(j))
                    bank = banks["V"][j % 4]
                    pe.wait_ge(a_pe, pe.next(a_pe))
                    for q in range(len(it["tiles"])):
                        ins = pe.eng.matmul(bank[:, 0:it["n"]], ones[it["size"]], sq[i % 2][:, q * it["n"]:(q + 1) * it["n"]],
                                            start=q == 0, stop=q == len(it["tiles"]) - 1)
                    ins.then_inc(full["V"][j % 4], 1)
            if i and items[i - 1]["rot"]:
                it = items[i - 1]
                for tile in it["tiles"]:
                    j = pe.take("V")
                    pe.wait_ge(freed["V"][j % 4], pe.opens(j))
                    bank = banks["V"][j % 4]
                    pe.wait_ge(v_pe, pe.next(v_pe))
                    pe.eng.matmul(bank[:, 0:it["n"]], cat[it["rot"][0]], tile, start=True, stop=True).then_inc(full["V"][j % 4], 1)

        def heads_jobs(items, base):
            norm, rot = {}, {}
            for i in range(len(items) + 1):
                if i < len(items) and items[i]["size"]:
                    norm[i] = base
                    base += 1
                if i and items[i - 1]["rot"]:
                    rot[i - 1] = [base + q for q in range(len(items[i - 1]["tiles"]))]
                    base += len(items[i - 1]["tiles"])
            return norm, rot, base

        def act_heads(act, items, sq, rt):
            act.stage()
            norm, _, _ = heads_jobs(items, act.job["V"])
            for i in range(len(items) + 1):
                act_heads_step(act, items, sq, rt, norm, i)
            act.wait_ge(v_a, act.next(v_a, min(2, len(norm))))

        def act_heads_step(act, items, sq, rt, norm, i):
            if i in norm:
                n = items[i]["n"]
                if i - 2 in norm:
                    act.wait_ge(full["V"][(norm[i - 2]) % 4], act.fills(norm[i - 2]))
                for q, tile in enumerate(items[i]["tiles"]):
                    ins = act.eng.activation(sq[i % 2][:, q * n:(q + 1) * n], tile, ACT.Square)
                ins.then_inc(a_self, 1)
                act.wait_ge(a_self, act.next(a_self))
                act.eng.sem_inc(a_pe, 1)
            if i - 1 in norm:
                it = items[i - 1]
                if i - 3 in norm:
                    act.wait_ge(v_a, act.next(v_a))
                act_root(act, norm[i - 1], rt[(i - 1) % 2][:, 0:it["n"]], it["over"], par("eps"))

        def vec_heads(v, items, rt, inv_t, rot_t):
            v.stage()
            norm, rot, end = heads_jobs(items, v.job["V"])

            def scale(i):
                it = items[i]
                n = it["n"]
                if it["size"]:
                    v.wait_ge(freed["V"][norm[i] % 4], v.frees(norm[i]))
                    v.eng.reciprocal(inv_t[:, 0:n], rt[i % 2][:, 0:n]).then_inc(v_self, 1)
                    v.wait_ge(v_self, v.next(v_self))
                    v.eng.sem_inc(v_a, 1)
                    for q, tile in enumerate(it["tiles"]):
                        ins = v.eng.scalar_tensor_tensor(tile, tile, it["gains"][q], inv_t[:, 0:n], ALU.mult, ALU.mult)
                        if it["rot"]:
                            ins.then_inc(v_self, 1)
                            v.wait_ge(v_self, v.next(v_self))
                            v.eng.sem_inc(v_pe, 1)
                        elif q == len(it["tiles"]) - 1:
                            ins.then_inc(v_self, 1)
                            v.wait_ge(v_self, v.next(v_self))
                elif it["rot"]:
                    for _ in it["tiles"]:
                        v.eng.sem_inc(v_pe, 1)

            def rotate(i):
                it = items[i]
                n = it["n"]
                for q, tile in enumerate(it["tiles"]):
                    v.wait_ge(full["V"][rot[i][q] % 4], v.fills(rot[i][q]))
                    bank = banks["V"][rot[i][q] % 4]
                    _, cos, sin = it["rot"]
                    v.eng.tensor_tensor(rot_t[:, 0:n], bank[:, 0:n], cat[sin][:, 0:n], ALU.mult).then_inc(freed["V"][rot[i][q] % 4], 1)
                    v.wait_ge(freed["V"][rot[i][q] % 4], v.frees(rot[i][q]))
                    v.eng.tensor_tensor(tile, tile, cat[cos][:, 0:n], ALU.mult).then_inc(v_self, 1)
                    v.wait_ge(v_self, v.next(v_self))
                    v.eng.tensor_tensor(tile, tile, rot_t[:, 0:n], ALU.add).then_inc(v_self, 1)
                    v.wait_ge(v_self, v.next(v_self))

            for i in range(len(items) + 1):
                if i < len(items):
                    scale(i)
                if i and items[i - 1]["rot"]:
                    rotate(i - 1)
            v.eng.sem_inc(v_pe, 1)
            v.job["V"] = end

        def item(tiles, n, size, over=None, gains=None, rot=None):
            return {"tiles": tiles, "n": n, "size": size, "over": over or size, "gains": gains, "rot": rot}

        def att_steps(gs, side):
            us = flat(gs)

            def chunk_at(i):
                c = i - i // 4
                return c if i % 4 < 3 and c < side else None

            steps = []
            for i in range(len(us) + LAG + 1):
                done = i - LAG - 1
                steps.append({"front": i if i < len(us) else None,
                              "turned": i - LAG if 0 <= i - LAG < len(us) else None,
                              "group": us[done][0] if done >= 0 and us[done][1] == len(gs[us[done][0]]["units"]) - 1 else None,
                              "rows": chunk_at(i), "sums": chunk_at(i - 1) if i else None})
            assert not side or sum(st["sums"] is not None for st in steps) == side
            return steps

        def att_jobs(gs, base, side):
            jobs = {}
            for i, st in enumerate(att_steps(gs, side)):
                for kind in ("rows", "turned", "group", "sums"):
                    if st[kind] is not None:
                        jobs[kind, st[kind]] = base
                        base += 1
            return jobs, base

        def flat(gs):
            return [(g, qi, un) for g, grp in enumerate(gs) for qi, un in enumerate(grp["units"])]

        def pe_att(pe, gs, W, side=0):
            pe.stage()
            us = flat(gs)
            for st in att_steps(gs, side):
                u = st["front"]
                if u is not None:
                    for parts in us[u][2]["maps"]:
                        j = pe.take("V")
                        pe.wait_ge(freed["V"][j % 4], pe.opens(j))
                        bank = banks["V"][j % 4]
                        for i, (q, k) in enumerate(parts):
                            ins = pe.eng.matmul(bank[:, 0:us[u][2]["nk"]], q, k, start=i == 0, stop=i == len(parts) - 1)
                        ins.then_inc(full["V"][j % 4], 1)
                if st["rows"] is not None:
                    jr = pe_side_rows(pe)
                if st["turned"] is not None:
                    u = st["turned"]
                    un = us[u][2]
                    j = pe.take("A")
                    pe.wait_ge(freed["A"][j % 4], pe.opens(j))
                    bank = banks["A"][j % 4]
                    pe.wait_ge(v_pe, pe.next(v_pe))
                    for c in range(un["nk"] // P):
                        ins = pe.eng.transpose(bank[:, c * P:(c + 1) * P], W["pn"][:, u % DEEP, c * P:(c + 1) * P], cat["ident"])
                    ins.then_inc(full["A"][j % 4], 1)
                if st["group"] is not None:
                    g = st["group"]
                    pe.wait_ge(freed["A"][turned % 4], pe.frees(turned))
                    jo = pe.take("A")
                    pe.wait_ge(freed["A"][jo % 4], pe.opens(jo))
                    bank = banks["A"][jo % 4]
                    n = P * len(gs[g]["units"])
                    r = gs[g]["rows"]
                    for c, val in enumerate(gs[g]["vals"]):
                        ins = pe.eng.matmul(bank[r, 0:n], val, W["pT"][:, g % 2, c, 0:n], start=c == 0,
                                            stop=c == len(gs[g]["vals"]) - 1)
                    ins.then_inc(full["A"][jo % 4], 1)
                if st["turned"] is not None:
                    turned = j
                if st["sums"] is not None:
                    pe_side_sums(pe, rows, st["sums"])
                if st["rows"] is not None:
                    rows = jr

        def act_att(act, gs, W, side=0):
            act.stage()
            us = flat(gs)
            jobs, end = att_jobs(gs, act.job["A"], side)
            scores = act.job["V"]
            for st in att_steps(gs, side):
                u = st["front"]
                if st["rows"] is not None:
                    c, j = st["rows"], jobs["rows", st["rows"]]
                    act.job["chunk"] += 1
                    act.wait_ge(full["A"][j % 4], act.fills(j))
                    act.eng.activation(side_rows[:, c % 2, :], banks["A"][j % 4][:, 0:CH], ACT.Copy).then_inc(freed["A"][j % 4], 1)
                if u is not None:
                    un = us[u][2]
                    for m in range(len(un["maps"])):
                        act.wait_ge(v_a, act.next(v_a))
                        s = W["s"][:, u % DEEP, m, 0:un["nk"]]
                        nm = W["st"][:, u % DEEP, m:m + 1]
                        if un["sink"] is not None:
                            act.eng.activation(W["st"][:, u % DEEP, 4:5], un["sink"], ACT.Exp, bias=nm)
                        total = W["st"][:, u % DEEP, 2 + m:3 + m]
                        if un["mask"] is None:
                            act.eng.activation(s, banks["V"][scores % 4][:, 0:un["nk"]], ACT.Exp, bias=nm, scale=un["scale"],
                                               accum_out=total).then_inc(freed["V"][scores % 4], 1)
                            act.wait_ge(freed["V"][scores % 4], act.frees(scores))
                        else:
                            act.eng.activation(s, s, ACT.Exp, bias=nm, accum_out=total).then_inc(a_self, 1)
                            act.wait_ge(a_self, act.next(a_self))
                        act.eng.sem_inc(a_v, 1)
                        scores += 1
                if st["turned"] is not None:
                    u = st["turned"]
                    g, qi, un = us[u]
                    nc_ = un["nk"] // P
                    j = jobs["turned", u]
                    act.wait_ge(full["A"][j % 4], act.fills(j))
                    act.eng.activation(W["pT"][:, g % 2, 0:nc_, qi * P:(qi + 1) * P],
                                       banks["A"][j % 4][:, 0:nc_ * P].rearrange("p (c q) -> p c q", c=nc_),
                                       ACT.Copy).then_inc(freed["A"][j % 4], 1)
                if st["group"] is not None:
                    g = st["group"]
                    j = jobs["group", g]
                    act.wait_ge(full["A"][j % 4], act.fills(j))
                    act.eng.activation(gs[g]["dst"], banks["A"][j % 4][gs[g]["rows"], 0:P * len(gs[g]["units"])],
                                       ACT.Copy).then_inc(freed["A"][j % 4], 1)
                if st["sums"] is not None:
                    c, j = st["sums"], jobs["sums", st["sums"]]
                    act.wait_ge(full["A"][j % 4], act.fills(j))
                    act.eng.activation(side_mods[:, 4 * c:4 * c + 4], banks["A"][j % 4][:, 0:4], ACT.Copy).then_inc(freed["A"][j % 4], 1)
            act.job["A"] = end

        def vec_att(v, gs, W, side=0):
            v.stage()
            us = flat(gs)
            jobs, end = att_jobs(gs, v.job["A"], side)
            v.job["chunk"] += side
            for u in range(len(us) + DEEP - 1):
                if u < len(us):
                    un = us[u][2]
                    nk = un["nk"]
                    for m in range(len(un["maps"])):
                        j = v.take("V")
                        v.wait_ge(full["V"][j % 4], v.fills(j))
                        bank = banks["V"][j % 4]
                        s = W["s"][:, u % DEEP, m, :]
                        nm = W["st"][:, u % DEEP, m:m + 1]
                        if un["mask"] is not None:
                            if nk > T:
                                v.eng.tensor_scalar(s[:, T:nk], bank[:, T:nk], un["scale"], None, ALU.mult)
                            v.eng.scalar_tensor_tensor(s[:, 0:T], bank[:, 0:T], un["scale"], un["mask"], ALU.mult,
                                                       ALU.add).then_inc(freed["V"][j % 4], 1)
                            v.wait_ge(freed["V"][j % 4], v.frees(j))
                            v.eng.tensor_reduce(nm, s[:, 0:nk], AX.X, ALU.max, negate=True).then_inc(v_self, 1)
                        else:
                            v.eng.tensor_reduce(nm, bank[:, 0:nk], AX.X, ALU.max, negate=True).then_inc(v_self, 1)
                            v.wait_ge(v_self, v.next(v_self))
                            v.eng.tensor_scalar(nm, nm, un["scale"], None, ALU.mult).then_inc(v_self, 1)
                        v.wait_ge(v_self, v.next(v_self))
                        if un["sink"] is not None:
                            v.eng.scalar_tensor_tensor(nm, un["sink"], -1.0, nm, ALU.mult, ALU.min).then_inc(v_self, 1)
                            v.wait_ge(v_self, v.next(v_self))
                        v.eng.sem_inc(v_a, 1)
                done = u - DEEP + 1
                if done >= 0:
                    g, qi, un = us[done]
                    b = done % DEEP
                    nk = un["nk"]
                    nm_ = len(un["maps"])
                    v.wait_ge(a_v, v.next(a_v, nm_))
                    st = W["st"]
                    if un["sink"] is not None:
                        v.eng.tensor_tensor(st[:, b, 2:3], st[:, b, 2:3], st[:, b, 4:5], ALU.add).then_inc(v_self, 1)
                        v.wait_ge(v_self, v.next(v_self))
                    v.eng.reciprocal(st[:, b, 5:5 + nm_], st[:, b, 2:2 + nm_]).then_inc(v_self, 1)
                    v.wait_ge(v_self, v.next(v_self))
                    if done >= DEEP:
                        j = jobs["turned", done - DEEP]
                        v.wait_ge(full["A"][j % 4], v.fills(j))
                    pn = W["pn"][:, b, 0:nk]
                    if nm_ == 1:
                        v.eng.tensor_scalar(pn, W["s"][:, b, 0, 0:nk], st[:, b, 5:6], None, ALU.mult).then_inc(v_self, 1)
                        v.wait_ge(v_self, v.next(v_self))
                        v.eng.sem_inc(v_pe, 1)
                    else:
                        v.eng.tensor_scalar(pn, W["s"][:, b, 0, 0:nk], st[:, b, 5:6], None, ALU.mult)
                        v.eng.tensor_tensor(st[:, b, 6:7], st[:, b, 6:7], small[:, 1:2], ALU.mult).then_inc(v_self, 1)
                        v.wait_ge(v_self, v.next(v_self))
                        v.eng.scalar_tensor_tensor(pn, W["s"][:, b, 1, 0:nk], st[:, b, 6:7], pn, ALU.mult, ALU.add).then_inc(v_self, 1)
                        v.wait_ge(v_self, v.next(v_self))
                        v.eng.sem_inc(v_pe, 1)
            v.job["A"] = end

        fm0, e0 = room(0, 13, TC)
        vt0, e0 = room(e0, 4, 640)
        sq0a, e1 = room(e0, TC)
        sq0b, e1 = room(e1, TC)
        rt0, e1 = room(e1, 2, TC)
        in0, e1 = room(e1, TC)
        ro0, e1 = room(e1, TC)
        W0 = {}
        W0["s"], e1 = room(e0, DEEP, 2, TC)
        W0["pn"], e1 = room(e1, DEEP, TC)
        W0["pT"], e1 = room(e1, 2, 4 * T)
        W0["pT"] = W0["pT"].rearrange("p g (c q) -> p g c q", c=4)
        W0["st"], e1 = room(e1, DEEP, 8)
        sqy, e2 = room(e0, 2, TC)
        rty, e2 = room(e2, 2, TC)
        iny, e2 = room(e2, TC)
        yT = hT

        def rope_items0():
            rope = ("rot16", "cosh", "sinh")
            its = []
            for t in range(13):
                g = "a_q" if t < BQ else "b_q" if t < AK else "a_k" if t < BK else "b_k"
                its.append(item([fm0[:, t, :]], TC, 64, gains=[par(g)], rot=rope))
            return its

        def att0():
            gs = []
            for side in range(2):
                nk, k0 = (TC, 0) if side == 0 else (T, T)
                kts = range(4) if side == 0 else range(2, 4)
                for h in range(8):
                    r = slice(64 * (h // 4), 64 * (h // 4) + 64)
                    units = []
                    for qt in range(2):
                        q0 = T * side + P * qt
                        units.append({"maps": [[(fm0[r, AQ + h % 4, q0:q0 + P], fm0[r, AK, k0:k0 + nk])]], "nk": nk,
                                      "scale": 0.125, "sink": par("sink", h),
                                      "mask": cat["amask"][:, qt * T:(qt + 1) * T] if side == 0 else None})
                    o = slice(64 * (h % 2), 64 * (h % 2) + 64)
                    gs.append({"units": units, "rows": o, "dst": yT[o, h // 2, T * side:T * side + T],
                               "vals": [vt0[:, kt, 64 * (h // 4):64 * (h // 4) + 64] for kt in kts]})
                for h in range(4):
                    units = []
                    for qt in range(2):
                        q0 = T * side + P * qt
                        maps = [[(fm0[64 * m:64 * m + 64, BQ + h, q0:q0 + P], fm0[64 * m:64 * m + 64, BK + h, k0:k0 + nk])]
                                for m in range(2)]
                        units.append({"maps": maps, "nk": nk, "scale": 0.125, "sink": None, "mask": None})
                    gs.append({"units": units, "rows": slice(0, P), "dst": yT[:, 4 + h, T * side:T * side + T],
                               "vals": [vt0[:, kt, 128 + 128 * h:256 + 128 * h] for kt in kts]})
            return gs

        def sub_items():
            return [item([yT[:, 4 + h, :]], TC, 128, gains=[small[:, 4:5]]) for h in range(4)]

        fm1, f0 = room(0, 17, TC)
        vt1, f0 = room(f0, 4, 512)
        bias1, _ = room(16000, 16, T)
        sq1, f1_ = room(f0, 2, 3 * TC)
        rt1, f1_ = room(f1_, 2, TC)
        in1, f1_ = room(f1_, TC)
        ro1, f1_ = room(f1_, TC)
        W1 = {}
        W1["s"], g0 = room(f0, DEEP, TC)
        W1["s"] = W1["s"].rearrange("p u (m k) -> p u m k", m=1)
        W1["pn"], g0 = room(g0, DEEP, TC)
        W1["pT"], g0 = room(g0, 2, 4 * T)
        W1["pT"] = W1["pT"].rearrange("p g (c q) -> p g c q", c=4)
        W1["st"], g0 = room(g0, DEEP, 8)

        qn1 = hT[:, 0:2, :].rearrange("p a (b t) -> p (a b) t", b=2)
        qr1 = hT[:, 2, :].rearrange("p (b t) -> p b t", b=2)
        kn1 = hT[:, 3:7, :]
        vm1 = fm1[:, CQ:CQ + 4, :]
        ym1 = xT[:, :, T:TC]

        def items1a():
            its = [item([fm1[:, CQ + t, 0:T] for t in range(6)], T, 128, 768, [par("c_qa", t) for t in range(6)])]
            its += [item([fm1[:, DQ + t, 0:T]], T, 64, gains=[par("d_q")]) for t in range(4)]
            its += [item([fm1[:, CKV + t, :] for t in range(2)], TC, 128, 256, [par("c_kva", t) for t in range(2)]),
                    item([fm1[:, KR, :]], TC, 32, gains=[par("c_kr")], rot=("rot8", "cosm", "sinm"))]
            its += [item([fm1[:, DK + t, :]], TC, 64, gains=[par("d_k")]) for t in range(4)]
            return its

        READY1 = [5, 6, 7, 8, 9, 11, 12, 13, 14, 15, 16]

        def items1b():
            its = [item([qn1[:, t, :]], T, 64, gains=[par("c_qn")]) for t in range(4)]
            its += [item([qr1[:, t, :]], T, 32, gains=[par("c_qr")], rot=("rot8", "cosm", "sinm")) for t in range(2)]
            its += [item([kn1[:, t, :]], TC, 64, gains=[par("c_kn")]) for t in range(4)]
            return its

        def att1(which):
            gs = []
            for h in range(8):
                o = slice(64 * (h % 2), 64 * (h % 2) + 64)
                units = []
                for qt in range(2):
                    q = slice(P * qt, P * qt + P)
                    if which == 0:
                        ro = slice(32 * (h % 4), 32 * (h % 4) + 32)
                        units.append({"maps": [[(qn1[o, h // 2, q], kn1[o, h // 2, :]), (qr1[ro, h // 4, q], fm1[ro, KR, :])]],
                                      "nk": TC, "scale": 96 ** -0.5, "sink": None, "mask": None})
                    else:
                        units.append({"maps": [[(fm1[o, DQ + h // 2, q], fm1[o, DK + h // 2, :])]], "nk": TC,
                                      "scale": 0.125, "sink": None, "mask": bias1[:, 2 * h + qt, :]})
                vals = [(vm1 if which == 0 else vt1)[:, kt, 64 * h:64 * h + 64] for kt in range(4)]
                gs.append({"units": units, "rows": o, "dst": ym1[o, 4 * which + h // 2, :], "vals": vals})
            return gs

        fs, s0 = room(0, 26, T)
        vtr, s0 = room(s0, 2, T)
        iw, s0 = room(s0, 2, 8)
        diff, _d = room(s0, 11, T)
        AR, s1 = room(s0, 3, 4 * P)
        AR = AR.rearrange("p a (b c t) -> p a b c t", b=2, c=2)
        Bf, s1 = room(s1, 3, T)
        Kf, s1 = room(s1, 3, T)
        gate, s1 = room(s1, 3, T)
        yr, s1 = room(s1, 3, T)
        ec, s1 = room(s1, 3, T)
        lo, s2 = room(s1, T)
        sgw, s2 = room(s2, 3, T)
        sa, s2 = room(s2, 3, T)
        sv, s2 = room(s2, 3, T)
        kk, s2 = room(s2, 3, T)
        w1, s2 = room(s2, 3, T)
        w2, s2 = room(s2, 3, T)
        SPLIT2 = [{"name": f"split{2 + l}", "h_lo": h_hi[:, :, T:TC], "hi": over(f"mix{2 + l}_w_hi", arena_at + 4 * s2, [P, 2, CHUNK]),
                   "lo": [over(f"mix{2 + l}_w_lo0", arena_at + 4 * (ARENA - CHUNK), [P, CHUNK]),
                          over(f"mix{2 + l}_w_lo1", arena_at + 4 * (s2 + 2 * CHUNK), [P, CHUNK])]} for l in range(2)]
        assert s2 + 4 * CHUNK <= ARENA
        tok, s3 = room(s1, 6, 384)
        prod, s3 = room(s3, 12, 512)
        NM, s3 = room(s3, 12, P)
        Y, s3 = room(s3, 12, P)
        U, _ = room(s3 - 2 * 12 * P, 384)
        SA, _ = room(s3 - 2 * 12 * P + 384, 384)
        S, _ = room(s3 - 2 * 12 * P + 768, 2, 192)
        acc, i0 = room(s3, 2, T)
        relu, i0 = room(i0, 2, T)
        top8, i0 = room(i0, 8)
        Xh, XTh = xT[:, 0:6, T:TC], hT[:, 0:6, T:TC]

        def at(m, i, r=slice(0, P), c=slice(0, P)):
            return m[r, i // 2, 128 * (i % 2) + c.start:128 * (i % 2) + c.stop]

        ctok, d0 = room(s0, 2, P)
        qlat, d0 = room(d0, 6, T)
        olat, d0 = room(d0, 6, T)
        W2 = {}
        sS, d0 = room(d0, DEEP, T)
        W2["s"] = sS.rearrange("p u (m k) -> p u m k", m=1)
        W2["pn"], d0 = room(d0, DEEP, T)
        W2["pT"], d0 = room(d0, 2, 2 * T)
        W2["pT"] = W2["pT"].rearrange("p g (c q) -> p g c q", c=2)
        W2["st"], d0 = room(d0, DEEP, 8)
        sT, r0 = room(d0, 4, 384)
        sg, r0 = room(r0, 2, T)
        sqr, r0 = room(r0, 2, T)
        rtr, r0 = room(r0, 2, T)
        inr, r0 = room(r0, T)
        ror, r0 = room(r0, T)

        def two(t):
            return t[:, 0, :], t[:, 1, :]

        def half(h):
            return slice(64 * (h % 2), 64 * (h % 2) + 64)

        def pe_mod(pe):
            pe.stage()
            stream.let_go()
            pe.wait_ge(a_pe, pe.next(a_pe))
            jm = pe.take("V")
            pe.wait_ge(freed["V"][jm % 4], pe.opens(jm))
            if stream.pending is not None:
                stream.mm(pe, banks["V"][jm % 4][0:32, 0:32], cT[:, 0, :], cT[:, 0, :], True, True)
            with pe.repeat(MOD_FIRST, {"A": 4, "chunk": 4}) as i:
                jobs = []
                for c in range(4):
                    w = by_k(stream.next(pe))
                    j = pe.take("A")
                    pe.wait_ge(freed["A"][j % 4], pe.opens(j))
                    for k in range(KD):
                        g = slice(32 * (k % 4), 32 * (k % 4) + 32)
                        ins = stream.mm(pe, banks["A"][j % 4][g, 0:CH], cT[:, k, :], w[:, k, :], k < 4, k >= 4)
                    ins.then_inc(full["A"][j % 4], 1)
                    jobs.append(j)
                stream.let_go()
                for c, j in enumerate(jobs):
                    pe.wait_ge(freed["A"][j % 4], pe.frees(j))
                    for t in range(2):
                        ins = stream.mm(pe, banks["V"][jm % 4][:, bass.ds(i * 16 + 4 * c + 2 * t, 2)],
                                        cond_rows[:, c, t * P:(t + 1) * P], cat["sel"], True, True)
                ins.then_inc(mod_turn, 1)
            pe.eng.sem_inc(full["V"][jm % 4], 1)

        def act_mod(act):
            act.stage()
            with act.repeat(MOD_FIRST, {"A": 4, "chunk": 4}):
                for c in range(4):
                    j = act.take("A")
                    act.job["chunk"] += 1
                    act.wait_ge(full["A"][j % 4], act.fills(j))
                    act.eng.activation(cond_rows[:, c, :], banks["A"][j % 4][:, 0:CH], ACT.Copy).then_inc(freed["A"][j % 4], 1)

        def vec_mod(v):
            v.stage()
            j = v.take("V")
            v.wait_ge(mod_turn, v.next(mod_turn, MOD_FIRST))
            vec_mods(v, 0, banks["V"][j % 4], 0, MOD_FIRST)
            v.eng.sem_inc(freed["V"][j % 4], 1)

        def vec_mods(v, l, src, first, end):
            m2 = mods[:, :, :].rearrange("p a b -> p (a b)")
            r = slice(16 * first, 16 * end)
            v.eng.tensor_tensor(m2[:, r], src[:, r], bmod[:, l, r], ALU.add).then_inc(v_self, 1)
            v.wait_ge(v_self, v.next(v_self))
            for m, add, mul in ((1, 1.0, 1.0), (4, 1.0, 1.0), (7, 1.0, 1.0), (2, 0.0, 0.5), (8, 0.0, 0.5)):
                if first <= m < end:
                    seg = m2[:, 16 * m:16 * m + 16]
                    ins = v.eng.tensor_scalar(seg, seg, add, mul, ALU.add, ALU.mult)
            ins.then_inc(v_self, 1)
            v.wait_ge(v_self, v.next(v_self))

        def pe_out(pe, n, rhs_of):
            pe.stage()
            for c in range(KD):
                if c % 2 == 0:
                    w = by_k(stream.next(pe))
                p = "A" if c < 4 else "V"
                j = pe.take(p)
                pe.wait_ge(freed[p][j % 4], pe.opens(j))
                bank = banks[p][j % 4]
                for k in range(KD):
                    ins = stream.mm(pe, bank[:, 0:n], w[:, k, (c % 2) * P:(c % 2 + 1) * P], rhs_of(k), k == 0, k == KD - 1)
                ins.then_inc(full[p][j % 4], 1)

        def vec_out(v, n, m):
            v.stage()
            add_to_x(v, [("A", v.take("A")) for _ in range(4)] + [("V", v.take("V")) for _ in range(4)], n, m, True)

        def pe_mix0(pe):
            pe.stage()
            items = rope_items0()
            for t in range(13):
                if t % 2 == 0:
                    w = pe_split_next(pe, SPLIT0)
                pe_split_tile(pe, SPLIT0, w, P * (t % 2), P, TC, t == 0)
                if t:
                    pe_heads_step(pe, items, (sq0a, sq0b), t - 1)
            pe_split_rows(pe, SPLIT0, w, 0, CH, TC)
            pe_heads_step(pe, items, (sq0a, sq0b), 12)
            for c in range(2):
                pe_split_rows(pe, SPLIT0, pe_split_next(pe, SPLIT0), 0, CH, TC)
                if c == 0:
                    pe_heads_step(pe, items, (sq0a, sq0b), 13)
            pe.wait_ge(v_pe, pe.next(v_pe))
            pe_att(pe, att0(), W0, 4 * N_MOD)
            pe.stage()
            for i in range(len(sub_items())):
                pe_heads_step(pe, sub_items(), two(sqy), i)
            pe.stage()
            w = [by_k(stream.next(pe))]
            before, slot = stream.pending, stream.held
            stream.held = None
            w.append(by_k(stream.next(pe)))
            stream.pending = before
            jobs = [pe.take("A") for _ in range(4)]
            for part in range(2):
                if part:
                    pe.wait_ge(v_pe, pe.next(v_pe))
                for c, j in enumerate(jobs):
                    if not part:
                        pe.wait_ge(freed["A"][j % 4], pe.opens(j))
                    if part and c == 2:
                        stream.pending = slot
                    for k in range(4 * part, 4 * part + 4):
                        ins = stream.mm(pe, banks["A"][j % 4][:, 0:TC], w[c // 2][:, k, (c % 2) * P:(c % 2 + 1) * P],
                                        yT[:, k, :], k == 0, k == KD - 1)
                    if part:
                        ins.then_inc(full["A"][j % 4], 1)
            for c in range(4, KD):
                if c % 2 == 0:
                    w = by_k(stream.next(pe))
                j = pe.take("V")
                pe.wait_ge(freed["V"][j % 4], pe.opens(j))
                for k in range(KD):
                    ins = stream.mm(pe, banks["V"][j % 4][:, 0:TC], w[:, k, (c % 2) * P:(c % 2 + 1) * P], yT[:, k, :],
                                    k == 0, k == KD - 1)
                ins.then_inc(full["V"][j % 4], 1)

        def act_mix0(act):
            act.stage()
            items = rope_items0()
            norm, _, _ = heads_jobs(items, act.job["V"])
            for t in range(13):
                if t:
                    act.wait_ge(freed["A"][j % 4], act.frees(j))
                    act_heads_step(act, items, (sq0a, sq0b), two(rt0), norm, t - 1)
                if t % 2 == 0:
                    act_first(act, SPLIT0, t // 2 + 1)
                j = act_out(act, fm0[:, t, :], width=TC)
            act.wait_ge(freed["A"][j % 4], act.frees(j))
            act_heads_step(act, items, (sq0a, sq0b), two(rt0), norm, 12)
            for tt in range(4):
                act_out(act, vt0[:, tt, 0:P], width=CH, skip=P)
            for c in range(2):
                if c == 0:
                    act_first(act, SPLIT0, 8)
                    act_heads_step(act, items, (sq0a, sq0b), two(rt0), norm, 13)
                for tt in range(4):
                    j = act_out(act, vt0[:, tt, P + CH * c:P + CH * c + CH], width=CH)
            act.wait_ge(v_a, act.next(v_a, 2))
            act_att(act, att0(), W0, 4 * N_MOD)
            act.wait_ge(freed["A"][(act.job["A"] - 1) % 4], act.frees(act.job["A"] - 1))
            act_heads(act, sub_items(), two(sqy), two(rty))

        def vec_mix0(v):
            vec_heads(v, rope_items0(), two(rt0), in0, ro0)
            vec_att(v, att0(), W0, 4 * N_MOD)
            vec_heads(v, sub_items(), two(rty), iny, None)
            vec_out(v, TC, 5)

        def pe_mix1(pe):
            def h_lhs(k, tt):
                return hT[:, k, tt * P:(tt + 1) * P]

            pe.stage()
            items = items1a()
            for t in range(17):
                if t % 2 == 0:
                    w = by_k(stream.next(pe))
                pe_tiles(pe, w, KD, [(P * (t % 2), P, T if t < CKV else TC)], lambda k, n: hT[:, k, 0:n], t == 0)
                if t - 1 in READY1:
                    pe_heads_step(pe, items, two(sq1), READY1.index(t - 1))
            for c in range(2):
                pe_rows(pe, by_k(stream.next(pe)), KD, 0, CH, TC, h_lhs)
                pe_heads_step(pe, items, two(sq1), len(items) - 1 + c)
            pe.wait_ge(v_pe, pe.next(v_pe))
            pe.stage()
            items = items1b()
            for t in range(6):
                if t % 2 == 0:
                    w = by_k(stream.next(pe), 6)
                pe_tiles(pe, w, 6, [(P * (t % 2), P, T)], lambda k, n: fm1[:, CQ + k, 0:n])
                if t:
                    pe_heads_step(pe, items, two(sq1), t - 1)
            w = by_k(stream.next(pe), 2, D)
            for t in range(4):
                pe_tiles(pe, w, 2, [(P * t, P, TC)], lambda k, n: fm1[:, CKV + k, 0:n])
                pe_heads_step(pe, items, two(sq1), t + 5)
            for tt in range(4):
                pe_rows(pe, w, 2, 512, 512, P, lambda k, _: fm1[:, CKV + k, tt * P:(tt + 1) * P])
                if tt < 2:
                    pe_heads_step(pe, items, two(sq1), tt + 9)
            pe.wait_ge(v_pe, pe.next(v_pe))
            pe_att(pe, att1(0), W1)
            pe_att(pe, att1(1), W1)
            pe.wait_ge(freed["A"][(pe.job["A"] - 1) % 4], pe.frees(pe.job["A"] - 1))
            pe_out(pe, T, lambda k: ym1[:, k, :])

        def act_mix1(act):
            act.stage()
            items = items1a()
            norm, _, _ = heads_jobs(items, act.job["V"])
            for t in range(17):
                if t - 1 in READY1:
                    act.wait_ge(freed["A"][j % 4], act.frees(j))
                    act_heads_step(act, items, two(sq1), two(rt1), norm, READY1.index(t - 1))
                n = T if t < CKV else TC
                j = act_out(act, fm1[:, t, 0:n], width=n)
            act.wait_ge(freed["A"][j % 4], act.frees(j))
            for c in range(2):
                act_heads_step(act, items, two(sq1), two(rt1), norm, len(items) - 1 + c)
                for tt in range(4):
                    act_out(act, vt1[:, tt, CH * c:CH * c + CH], width=CH)
            act.wait_ge(v_a, act.next(v_a, 2))
            act.stage()
            items = items1b()
            norm, _, _ = heads_jobs(items, act.job["V"])
            for t in range(10):
                if t:
                    act.wait_ge(freed["A"][j % 4], act.frees(j))
                    act_heads_step(act, items, two(sq1), two(rt1), norm, t - 1)
                if t < 4:
                    j = act_out(act, qn1[:, t, :], width=T)
                elif t < 6:
                    j = act_out(act, qr1[:, t - 4, :], width=T)
                else:
                    j = act_out(act, kn1[:, t - 6, :], width=TC)
            act.wait_ge(freed["A"][j % 4], act.frees(j))
            for tt in range(4):
                if tt < 2:
                    act_heads_step(act, items, two(sq1), two(rt1), norm, tt + 9)
                act_out(act, vm1[:, tt, :], width=TC)
            act.wait_ge(v_a, act.next(v_a, 2))
            act_att(act, att1(0), W1)
            act_att(act, att1(1), W1)

        def vec_mix1(v):
            vec_heads(v, items1a(), two(rt1), in1, ro1)
            vec_heads(v, items1b(), two(rt1), in1, ro1)
            vec_att(v, att1(0), W1)
            v.eng.wait_ge(s_bias, 16)
            vec_att(v, att1(1), W1)
            vec_out(v, T, 5)

        def c_items(l):
            return [item([fs[:, SC, :]], T, 128, gains=[par(f"kv_{l}")])] + \
                [item([fs[:, t, :]], T, 0, rot=("rot32", "cosr", "sinr")) for t in (TQ, TQ + 1, TK, TK + 1)]

        def ret_norms():
            return [item([yT[:, 6 + t, 0:T]], T, 64, gains=[par("one")]) for t in range(2)]

        def att2():
            gs = []
            for h in range(6):
                units = [{"maps": [[(qlat[:, h, P * qt:P * qt + P], fs[:, SC, :])]], "nk": T, "scale": 1.0, "sink": None,
                          "mask": acc[:, qt, :]} for qt in range(2)]
                gs.append({"units": units, "rows": slice(0, P), "dst": olat[:, h, :], "vals": [ctok[:, kt, :] for kt in range(2)]})
            return gs

        EARLY = 7
        INDEX_AT = [range(16 * lev // LEVELS, 16 * (lev + 1) // LEVELS) for lev in range(LEVELS)]
        SIXES = [(h, tt) for h in range(HEADS_R) for tt in range(2)]

        def pe_sums(pe, src):
            for t in range(3):
                j = pe.take("V")
                pe.wait_ge(freed["V"][j % 4], pe.opens(j))
                bank = banks["V"][j % 4]
                pe.eng.matmul(bank[:, 0:T], ones[64], src[:, t, :], start=True, stop=True).then_inc(full["V"][j % 4], 1)

        def pe_mix2(pe, l):
            S2 = SPLIT2[l]

            def tiles(chunks, width=P):
                for _ in range(chunks):
                    w = pe_split_next(pe, S2)
                    pe_split_tile(pe, S2, w, 0, P, T, width < P)
                    pe_split_tile(pe, S2, w, P, width, T)
                return w

            w = tiles(1, 24)
            pe_split_rows(pe, S2, w, P + 16, 8, T)
            tiles(EARLY)
            pe.wait_ge(a_pe, pe.next(a_pe))
            lora = par(f"lora_{l}", 0, 384)
            for r in (slice(0, 32), slice(32, 64), slice(64, P)):
                for t in range(3):
                    j = pe.take("A")
                    pe.wait_ge(freed["A"][j % 4], pe.opens(j))
                    bank = banks["A"][j % 4]
                    pe.eng.matmul(bank[:, 0:T], lora[r, t * P:(t + 1) * P], lo[r, :], start=True, stop=True).then_inc(full["A"][j % 4], 1)
            if l:
                for t in range(3):
                    j = pe.take("A")
                    pe.wait_ge(freed["A"][j % 4], pe.opens(j))
                    bank = banks["A"][j % 4]
                    pe.eng.matmul(bank[:, 0:T], par(f"v2_{l}", 0, 384)[0:16, t * P:(t + 1) * P], fs[0:16, MV, :],
                                          start=True, stop=True).then_inc(full["A"][j % 4], 1)
            pe.wait_ge(v_pe, pe.next(v_pe))
            pe_sums(pe, w1)
            tiles(12 - EARLY)
            pe_split_rows(pe, S2, pe_split_next(pe, S2), 0, CH, T)
            pe.wait_ge(v_pe, pe.next(v_pe))
            pe_sums(pe, w1)
            for h, tt in SIXES:
                j = pe.take("V")
                pe.wait_ge(freed["V"][j % 4], pe.opens(j))
                bank = banks["V"][j % 4]
                ts = slice(P * tt, P * tt + P)
                rhs = AR[half(h), h // 2, tt, :, :].rearrange("p c t -> p (c t)")
                pe.eng.matmul(bank[:, 0:T], Bf[half(h), h // 2, ts], rhs, start=True, stop=True)
                pe.eng.matmul(bank[:, T:TC], Kf[half(h), h // 2, ts], rhs, start=True, stop=True).then_inc(full["V"][j % 4], 1)
            for src in (Bf, Kf, fs[:, RV:RV + 3, :]):
                for tt in range(2):
                    j = pe.take("A")
                    pe.wait_ge(freed["A"][j % 4], pe.opens(j))
                    bank = banks["A"][j % 4]
                    for t in range(3):
                        ins = pe.eng.transpose(bank[:, t * P:(t + 1) * P], src[:, t, P * tt:P * tt + P], cat["ident"])
                    ins.then_inc(full["A"][j % 4], 1)
            pe.wait_ge(v_pe, pe.next(v_pe))
            plan[f"index{l}"] = []
            for lev in range(LEVELS):
                pe.wait_ge(g_pe, pe.next(g_pe))
                if lev:
                    pe.wait_ge(v_pe, pe.next(v_pe))
                for q in range(3):
                    j = pe.take("A")
                    pe.wait_ge(freed["A"][j % 4], pe.opens(j))
                    bank = banks["A"][j % 4]
                    for i in range(4 * q, 4 * q + 4):
                        ins = pe.eng.matmul(bank[:, (i % 4) * P:(i % 4 + 1) * P], NM[:, i, :], at(Xh, i), start=True, stop=True)
                    ins.then_inc(full["A"][j % 4], 1)
                for i in INDEX_AT[lev]:
                    tt, h = divmod(i, 8)
                    jj = pe.take("V")
                    plan[f"index{l}"].append(jj)
                    pe.wait_ge(freed["V"][jj % 4], pe.opens(jj))
                    pe.eng.matmul(banks["V"][jj % 4][:, 0:T], fs[half(h), SIQ + h // 2, P * tt:P * tt + P], fs[half(h), SIK, :],
                                  start=True, stop=True).then_inc(full["V"][jj % 4], 1)
                pe.wait_ge(freed["A"][j % 4], pe.frees(j))
                if lev:
                    pe.wait_ge(v_pe, pe.next(v_pe))
                if lev < LEVELS - 1:
                    for q in range(3):
                        j = pe.take("V")
                        pe.wait_ge(freed["V"][j % 4], pe.opens(j))
                        bank = banks["V"][j % 4]
                        for i in range(4 * q, 4 * q + 4):
                            ins = pe.eng.matmul(bank[:, (i % 4) * P:(i % 4 + 1) * P], at(XTh, i), Y[:, i, :], start=True, stop=True)
                        ins.then_inc(full["V"][j % 4], 1)
                for q in range(3):
                    j = pe.take("V")
                    pe.wait_ge(freed["V"][j % 4], pe.opens(j))
                    bank = banks["V"][j % 4]
                    for i in range(4 * q, 4 * q + 4):
                        ins = pe.eng.matmul(bank[:, (i % 4) * P:(i % 4 + 1) * P], Y[:, i, :], at(XTh, i), start=True, stop=True)
                    ins.then_inc(full["V"][j % 4], 1)
            pe.wait_ge(v_pe, pe.next(v_pe))
            for ci in range(T // RC):
                tt, o = ci // 2, slice(64 * (ci % 2), 64 * (ci % 2) + 64)
                S0 = S[:, ci % 2, :]
                same = [h for h in range(HEADS_R) if half(h) == o]
                other = [h for h in range(HEADS_R) if half(h) != o]

                def col(h):
                    return slice(64 * h, 64 * h + 64)

                def duo(h):
                    return slice(64 * (h // 2), 64 * (h // 2) + 64)

                jU = pe.take("V")
                pe.wait_ge(freed["V"][jU % 4], pe.opens(jU))
                bank = banks["V"][jU % 4]
                for h in other + same:
                    pe.eng.matmul(bank[o, col(h)], prod[o, 2 * h + tt, T + o.start:T + o.stop], tok[o, 4 + tt, col(h)],
                                  start=h == other[0], stop=False)
                    if ci and h == other[-1]:
                        pe.wait_ge(v_pe, pe.next(v_pe))
                    if h in same:
                        ins = pe.eng.matmul(bank[o, col(h)], AR[half(h), h // 2, tt, 0, o], S0[half(h), duo(h)],
                                            start=False, stop=False)
                ins.then_inc(pe_self, 1)
                pe.wait_ge(pe_self, pe.next(pe_self))
                for h in other:
                    ins = pe.eng.matmul(bank[o, col(h)], AR[half(h), h // 2, tt, 0, o], S0[half(h), duo(h)],
                                        start=False, stop=h == other[-1])
                ins.then_inc(full["V"][jU % 4], 1)
                jSA = pe.take("V")
                pe.wait_ge(freed["V"][jSA % 4], pe.opens(jSA))
                bank = banks["V"][jSA % 4]
                pe.wait_ge(freed["V"][jU % 4], pe.frees(jU))
                for h in range(HEADS_R):
                    c = slice(64 * h, 64 * h + 64)
                    ins = pe.eng.matmul(bank[o, c], at(XTh, 2 * h + tt, o, o), U[o, c], start=True, stop=True)
                ins.then_inc(full["V"][jSA % 4], 1)
                pe.wait_ge(freed["V"][jSA % 4], pe.frees(jSA))
                if ci < T // RC - 1:
                    j = pe.take("V")
                    pe.wait_ge(freed["V"][j % 4], pe.opens(j))
                    bank = banks["V"][j % 4]
                    for h in range(HEADS_R):
                        c, hs = slice(64 * h, 64 * h + 64), slice(64 * (h // 2), 64 * (h // 2) + 64)
                        pe.eng.matmul(bank[half(h), hs], tok[o, tt, c], SA[o, c], start=True, stop=False)
                        ins = pe.eng.matmul(bank[half(h), hs], tok[o, 2 + tt, c], tok[o, 4 + tt, c], start=False, stop=True)
                    ins.then_inc(full["V"][j % 4], 1)
                j = pe.take("A")
                pe.wait_ge(freed["A"][j % 4], pe.opens(j))
                bank = banks["A"][j % 4]
                for h in other + same:
                    i, out = 2 * h + tt, bank[half(h), duo(h)]
                    pe.eng.matmul(out, SA[o, col(h)], prod[o, i, P + o.start:P + o.stop], start=h in (other[0], same[0]), stop=False)
                    ins = pe.eng.matmul(out, tok[o, 4 + tt, col(h)], prod[o, i, 384 + o.start:384 + o.stop],
                                        start=False, stop=False)
                    if h in same:
                        ins = pe.eng.matmul(out, S0[half(h), duo(h)], AR[half(h), h // 2, tt, 1, o], start=False, stop=h == same[-1])
                ins.then_inc(pe_self, 1)
                pe.wait_ge(pe_self, pe.next(pe_self))
                for h in other:
                    ins = pe.eng.matmul(bank[half(h), duo(h)], S0[half(h), duo(h)], AR[half(h), h // 2, tt, 1, o],
                                        start=False, stop=h == other[-1])
                ins.then_inc(full["A"][j % 4], 1)
            pe.wait_ge(freed["A"][j % 4], pe.frees(j))
            pe_sums(pe, yr)
            pe.wait_ge(v_pe, pe.next(v_pe))
            plan[f"variance{l}"] = pe.job["V"]
            pe_sums(pe, Kf)
            pe_heads(pe, c_items(l), two(sqr))
            j = pe.take("A")
            pe.wait_ge(freed["A"][j % 4], pe.opens(j))
            bank = banks["A"][j % 4]
            for tt in range(2):
                ins = pe.eng.transpose(bank[:, P * tt:P * tt + P], fs[:, SC, P * tt:P * tt + P], cat["ident"])
            ins.then_inc(full["A"][j % 4], 1)
            uk, uv = par(f"uk_{l}", 0, 384), par(f"uv_{l}", 0, 384)
            for h in range(6):
                j = pe.take("A")
                pe.wait_ge(freed["A"][j % 4], pe.opens(j))
                bank = banks["A"][j % 4]
                pe.eng.matmul(bank[:, 0:T], uk[half(h), P * (h // 2):P * (h // 2) + P], fs[half(h), SQ + h // 2, :],
                                      start=True, stop=True).then_inc(full["A"][j % 4], 1)
            pe.wait_ge(freed["A"][j % 4], pe.frees(j))
            pe_att(pe, att2(), W2)
            pe.wait_ge(freed["A"][(pe.job["A"] - 1) % 4], pe.frees(pe.job["A"] - 1))
            for t in range(3):
                j = pe.take("A")
                pe.wait_ge(freed["A"][j % 4], pe.opens(j))
                bank = banks["A"][j % 4]
                for h in (2 * t, 2 * t + 1):
                    ins = pe.eng.matmul(bank[half(h), 0:T], uv[:, 64 * h:64 * h + 64], olat[:, h, :], start=True, stop=True)
                ins.then_inc(full["A"][j % 4], 1)
            for h in range(4):
                j = pe.take("V")
                pe.wait_ge(freed["V"][j % 4], pe.opens(j))
                bank = banks["V"][j % 4]
                q, k = fs[half(h), TQ + h // 2, :], fs[half(h), TK + h // 2, :]
                pe.eng.matmul(bank[:, 0:T], k[:, 0:P], q, start=True, stop=True)
                pe.eng.matmul(bank[:, T:T + P], k[:, P:T], q[:, P:T], start=True, stop=True).then_inc(full["V"][j % 4], 1)
            pe.wait_ge(freed["V"][j % 4], pe.frees(j))
            for t in range(2):
                j = pe.take("A")
                pe.wait_ge(freed["A"][j % 4], pe.opens(j))
                bank = banks["A"][j % 4]
                for h in (2 * t, 2 * t + 1):
                    c = slice(64 * h, 64 * h + 64)
                    pe.eng.matmul(bank[half(h), 0:P], vtr[:, 0, c], sT[:, h, 0:P], start=True, stop=True)
                    pe.eng.matmul(bank[half(h), P:T], vtr[:, 0, c], sT[:, h, P:T], start=True, stop=False)
                    ins = pe.eng.matmul(bank[half(h), P:T], vtr[:, 1, c], sT[:, h, T:T + P], start=False, stop=True)
                ins.then_inc(full["A"][j % 4], 1)
            pe_heads(pe, ret_norms(), two(sqr))
            pe.wait_ge(v_pe, pe.next(v_pe))
            pe_out(pe, T, lambda k: yT[:, k, 0:T])

        def act_mix2(act, l):
            def tiles(first, n):
                for t in range(first, first + n):
                    r = slice(0, 24 if t == MV else P)
                    if t % 2 == 0:
                        act_first(act, SPLIT2[l], 1 if t == MV - 1 else t // 2 + 2)
                    act_out(act, fs[r, t, :], rows=r, width=T)

            act.wait_ge(h_made, plan[f"split{2 + l}"]["h"])
            tiles(MV - 1, 2)
            for tt in range(2):
                act_out(act, iw[:, tt, :], width=8, scale=8 ** -0.5 * 0.125)
            tiles(0, 2 * EARLY)
            act.wait_ge(v_a, act.next(v_a))
            act.eng.activation(lo[0:32, :], fs[0:32, LORA, :], ACT.Tanh)
            act.eng.activation(lo[32:64, :], fs[32:64, LORA, :], ACT.Copy)
            act.eng.activation(lo[64:P, :], fs[64:P, LORA, :], ACT.Sigmoid).then_inc(a_self, 1)
            act.wait_ge(a_self, act.next(a_self))
            act.eng.sem_inc(a_pe, 1)
            for dst, name in ((sgw, "w0_"), (sa, "a0_"), (gate, None), (sv, "v0_")):
                if dst is sv and not l:
                    continue
                for t in range(3):
                    if name:
                        act_out(act, dst[:, t, :], width=T, func=ACT.Sigmoid, bias=par(f"{name}{l}", t))
                    else:
                        act_out(act, dst[:, t, :], width=T)
            act.wait_ge(v_a, act.next(v_a))
            act.eng.activation(w2[:, :, :], w2[:, :, :], ACT.Sqrt).then_inc(a_self, 1)
            act.wait_ge(a_self, act.next(a_self))
            act.eng.sem_inc(a_v, 1)
            tiles(2 * EARLY, 4)
            act.wait_ge(v_a, act.next(v_a))
            act.eng.activation(ec[:, :, :], w1[:, :, :], ACT.Exp)
            act.wait_ge(v_a, act.next(v_a))
            act.eng.activation(sgw[:, :, :], w1[:, :, :], ACT.Exp, scale=-1.0)
            act.eng.activation(sv[:, :, :], w2[:, :, :], ACT.Exp).then_inc(a_self, 1)
            act.wait_ge(a_self, act.next(a_self))
            act.eng.sem_inc(a_v, 1)
            tiles(2 * EARLY + 4, 24 - 2 * EARLY - 4)
            for tt in range(2):
                act_out(act, vtr[:, tt, :], width=T)
            for q in range(6):
                act_out(act, tok[:, q, :], width=384)
            for lev in range(LEVELS):
                for q in range(3):
                    act_out(act, Y[:, 4 * q:4 * q + 4, :], width=TC)
                for i in INDEX_AT[lev]:
                    j = plan[f"index{l}"][i]
                    act.wait_ge(full["V"][j % 4], act.fills(j))
                    if i >= 2:
                        act.wait_ge(head_summed, act.next(head_summed))
                    act.eng.activation(relu[:, i % 2, :], banks["V"][j % 4][:, 0:T], ACT.Relu).then_inc(freed["V"][j % 4], 1)
            act.wait_ge(head_summed, act.next(head_summed, 2))
            for ci in range(T // RC):
                act_out(act, yr[:, :, RC * ci:RC * ci + RC], width=192)
            for t in range(3):
                act_root(act, plan[f"variance{l}"] + t, Bf[:, t, :], 64, par("gn_eps"))
            act.wait_ge(v_a, act.next(v_a))
            act_heads(act, c_items(l), two(sqr), two(rtr))
            act_out(act, ctok[:, :, :], width=T)
            for h in range(6):
                act_out(act, qlat[:, h, :], width=T, scale=0.125)
            act_att(act, att2(), W2)
            for t in range(3):
                act_out(act, yT[:, 3 + t, 0:T], width=T)
            for t in range(2):
                j = act_out(act, yT[:, 6 + t, 0:T], width=T)
            act.wait_ge(freed["A"][j % 4], act.frees(j))
            act_heads(act, ret_norms(), two(sqr), two(rtr))
            act.eng.activation(sg[:, :, :], fs[:, TG:TG + 2, :], ACT.Silu).then_inc(a_self, 1)
            act.wait_ge(a_self, act.next(a_self))
            act.eng.sem_inc(a_v, 1)

        def vec_pick(v, first, n):
            for i in range(first, min(first + n, 2 * PICKS)):
                tt, step = divmod(i, PICKS)
                w = acc[:, tt, :]
                if step < PICKS - 1:
                    v.eng.max(top8[:, :], w).then_inc(v_self, 1)
                    v.wait_ge(v_self, v.next(v_self))
                    v.eng.match_replace(w, top8[:, :], w, TAKEN).then_inc(v_self, 1)
                    v.wait_ge(v_self, v.next(v_self))
                else:
                    v.eng.tensor_scalar(w, w, TAKEN / 2, NEG, ALU.is_gt, ALU.mult).then_inc(v_self, 1)
                    v.wait_ge(v_self, v.next(v_self))
                    v.eng.tensor_tensor(w, w, cat["causal"][:, tt * T:(tt + 1) * T], ALU.add).then_inc(v_self, 1)
                    v.wait_ge(v_self, v.next(v_self))
            return min(first + n, 2 * PICKS)

        def vec_mix2(v, l):
            E = v.eng
            a0 = v.job["A"]
            first = a0 + 4 + LORA
            v.wait_ge(freed["A"][first % 4], v.frees(first))
            v.job["A"] += 4 + 2 * EARLY
            spans = [(0, 10, "mu_")] + ([(MV, 1, "vmu_")] if l else [])
            for t0, nt, _ in spans:
                d = diff[:, min(t0, 10):min(t0, 10) + nt, :]
                E.tensor_tensor(d[:, :, 1:T], fs[:, t0:t0 + nt, 0:T - 1], fs[:, t0:t0 + nt, 1:T], ALU.subtract) if t0 == 0 else \
                    E.tensor_tensor(d[0:16, :, 1:T], fs[0:16, t0:t0 + nt, 0:T - 1], fs[0:16, t0:t0 + nt, 1:T], ALU.subtract)
                r = slice(0, P if t0 == 0 else 16)
                E.tensor_scalar(d[r, :, 0:1], fs[r, t0:t0 + nt, 0:1], -1.0, None, ALU.mult).then_inc(v_self, 1)
                v.wait_ge(v_self, v.next(v_self))
            for t0, nt, name in spans:
                r = slice(0, P if t0 == 0 else 16)
                for t in range(nt):
                    x_ = fs[r, t0 + t, :]
                    ins = E.scalar_tensor_tensor(x_, diff[r, min(t0, 10) + t, :], par(f"{name}{l}", t, rows=r), x_, ALU.mult, ALU.add)
            ins.then_inc(v_self, 1)
            v.wait_ge(v_self, v.next(v_self))
            E.sem_inc(v_a, 1)
            k_, r_, v_ = fs[:, RK:RK + 3, :], fs[:, RR:RR + 3, :], fs[:, RV:RV + 3, :]
            for t in range(3):
                ins = E.tensor_scalar(kk[:, t, :], k_[:, t, :], par(f"kk_{l}", t), None, ALU.mult)
            ins.then_inc(v_self, 1)
            v.wait_ge(v_self, v.next(v_self))
            E.tensor_tensor(w1[:, :, :], kk[:, :, :], kk[:, :, :], ALU.mult).then_inc(v_self, 1)
            v.wait_ge(v_self, v.next(v_self))
            v.eng.sem_inc(v_pe, 1)
            for t in range(3):
                j = v.take("V")
                v.wait_ge(full["V"][j % 4], v.fills(j))
                bank = banks["V"][j % 4]
                E.tensor_scalar(w2[:, t, :], bank[:, 0:T], 1e-24, None, ALU.max).then_inc(freed["V"][j % 4], 1)
                v.wait_ge(freed["V"][j % 4], v.frees(j))
            E.sem_inc(v_a, 1)
            v.wait_ge(a_v, v.next(a_v))
            E.reciprocal(w2[:, :, :], w2[:, :, :]).then_inc(v_self, 1)
            v.wait_ge(v_self, v.next(v_self))
            E.tensor_tensor(kk[:, :, :], kk[:, :, :], w2[:, :, :], ALU.mult).then_inc(v_self, 1)
            v.wait_ge(v_self, v.next(v_self))
            n_lo = 12 if l else 9
            v.wait_ge(freed["A"][(v.job["A"] + n_lo - 1) % 4], v.frees(v.job["A"] + n_lo - 1))
            v.job["A"] += n_lo + 24 - 2 * EARLY + 2
            for t in range(3):
                ins = E.tensor_scalar(w1[:, t, :], sa[:, t, :], 1.0, par(f"ka_{l}", t), ALU.subtract, ALU.mult)
            ins.then_inc(v_self, 1)
            v.wait_ge(v_self, v.next(v_self))
            E.scalar_tensor_tensor(k_, w1[:, :, :], 1.0, k_, ALU.add, ALU.mult).then_inc(v_self, 1)
            v.wait_ge(v_self, v.next(v_self))
            if l:
                E.tensor_tensor(w2[:, :, :], vfirst[:, :, :], v_, ALU.subtract).then_inc(v_self, 1)
                v.wait_ge(v_self, v.next(v_self))
                E.tensor_tensor(w2[:, :, :], w2[:, :, :], sv[:, :, :], ALU.mult).then_inc(v_self, 1)
                v.wait_ge(v_self, v.next(v_self))
                E.tensor_tensor(v_, v_, w2[:, :, :], ALU.add).then_inc(v_self, 1)
                v.wait_ge(v_self, v.next(v_self))
            else:
                E.tensor_copy(vfirst[:, :, :], v_).then_inc(v_self, 1)
                v.wait_ge(v_self, v.next(v_self))
            E.tensor_scalar(w2[:, :, :], sgw[:, :, :], -DECAY, None, ALU.mult).then_inc(v_self, 1)
            v.wait_ge(v_self, v.next(v_self))
            f2 = "p a b -> p (a b)"
            E.tensor_tensor_scan(w1[:, :, :].rearrange(f2), cat["scanm"], w2[:, :, :].rearrange(f2), 0.0, ALU.mult, ALU.add).then_inc(v_self, 1)
            v.wait_ge(v_self, v.next(v_self))
            E.sem_inc(v_a, 1)
            E.tensor_tensor(w2[:, :, :], w1[:, :, :], w2[:, :, :], ALU.subtract).then_inc(v_self, 1)
            v.wait_ge(v_self, v.next(v_self))
            E.sem_inc(v_a, 1)
            E.tensor_tensor(Bf[:, :, :], kk[:, :, :], sa[:, :, :], ALU.mult).then_inc(v_self, 1)
            v.wait_ge(v_self, v.next(v_self))
            v.wait_ge(a_v, v.next(a_v))
            E.tensor_tensor(Bf[:, :, :], Bf[:, :, :], sgw[:, :, :], ALU.mult)
            E.tensor_tensor(Kf[:, :, :], k_, sgw[:, :, :], ALU.mult)
            by2 = "p (b t) -> p b t"
            for t in range(3):
                E.scalar_tensor_tensor(AR[:, t, :, 0, :], kk[:, t, :].rearrange(by2, b=2), -1.0, sv[:, t, :].rearrange(by2, b=2),
                                       ALU.mult, ALU.mult)
                E.tensor_tensor(AR[:, t, :, 1, :], r_[:, t, :].rearrange(by2, b=2), ec[:, t, :].rearrange(by2, b=2), ALU.mult)
            for t in range(3):
                ins = E.scalar_tensor_tensor(w1[:, t, :], r_[:, t, :], par(f"rk_{l}", t), k_[:, t, :], ALU.mult, ALU.mult)
            ins.then_inc(v_self, 1)
            v.wait_ge(v_self, v.next(v_self))
            v.eng.sem_inc(v_pe, 1)
            for t in range(3):
                j = v.take("V")
                v.wait_ge(full["V"][j % 4], v.fills(j))
                bank = banks["V"][j % 4]
                E.tensor_tensor(k_[:, t, :], bank[:, 0:T], v_[:, t, :], ALU.mult).then_inc(freed["V"][j % 4], 1)
                v.wait_ge(freed["V"][j % 4], v.frees(j))
            for i in range(12):
                j = v.take("V")
                v.wait_ge(full["V"][j % 4], v.fills(j))
                bank = banks["V"][j % 4]
                E.tensor_tensor(prod[:, i, :], bank[:, :], cat["prodm"], ALU.mult).then_inc(freed["V"][j % 4], 1)
                v.wait_ge(freed["V"][j % 4], v.frees(j))
            v.wait_ge(freed["V"][j % 4], v.frees(j))
            E.sem_inc(v_g, 1)
            for m in (Xh, XTh):
                for i in range(12):
                    ins = E.tensor_copy(at(m, i), cat["ident"])
            ins.then_inc(v_self, 1)
            v.wait_ge(v_self, v.next(v_self))
            v.eng.sem_inc(v_pe, 1)
            v.job["A"] += 6 + 3 * LEVELS
            for lev in range(LEVELS):
                for i in INDEX_AT[lev]:
                    tt, h = divmod(i, 8)
                    j = v.take("V")
                    v.wait_ge(freed["V"][j % 4], v.frees(j))
                    if h:
                        E.scalar_tensor_tensor(acc[:, tt, :], relu[:, i % 2, :], iw[:, tt, h:h + 1], acc[:, tt, :],
                                               ALU.mult, ALU.add).then_inc(head_summed, 1)
                    else:
                        causal = cat["causal"][:, tt * T:(tt + 1) * T]
                        E.scalar_tensor_tensor(acc[:, tt, :], relu[:, i % 2, :], iw[:, tt, h:h + 1], causal,
                                               ALU.mult, ALU.add).then_inc(head_summed, 1)
                    v.wait_ge(head_summed, v.next(head_summed))
                for m in ([Xh, XTh] if lev < LEVELS - 1 else [XTh]):
                    for q in range(3):
                        j = v.take("V")
                        v.wait_ge(full["V"][j % 4], v.fills(j))
                        bank = banks["V"][j % 4]
                        dst = m[:, 2 * q:2 * q + 2, :]
                        E.tensor_tensor(dst, dst, bank[:, :].rearrange("p (a b) -> p a b", a=2), ALU.add).then_inc(freed["V"][j % 4], 1)
                        v.wait_ge(freed["V"][j % 4], v.frees(j))
                    if lev < LEVELS - 1:
                        v.wait_ge(freed["V"][j % 4], v.frees(j))
                        E.sem_inc(v_pe, 1)
            v.wait_ge(freed["V"][j % 4], v.frees(j))
            E.memset(S[:, 0, :], 0.0).then_inc(v_self, 1)
            v.wait_ge(v_self, v.next(v_self))
            v.eng.sem_inc(v_pe, 1)
            picks = 0
            for ci in range(T // RC):
                o = slice(64 * (ci % 2), 64 * (ci % 2) + 64)
                for dst in (U, SA):
                    j = v.take("V")
                    v.wait_ge(full["V"][j % 4], v.fills(j))
                    bank = banks["V"][j % 4]
                    E.tensor_copy(dst[o, :], bank[o, 0:384]).then_inc(freed["V"][j % 4], 1)
                    v.wait_ge(freed["V"][j % 4], v.frees(j))
                    picks = vec_pick(v, picks, 2)
                if ci < T // RC - 1:
                    j = v.take("V")
                    v.wait_ge(full["V"][j % 4], v.fills(j))
                    bank = banks["V"][j % 4]
                    S1 = S[:, (ci + 1) % 2, :]
                    if ci:
                        v.wait_ge(full["A"][(v.job["A"] + ci - 1) % 4], v.fills(v.job["A"] + ci - 1))
                    E.tensor_tensor(S1, bank[:, 0:192], S[:, ci % 2, :], ALU.add).then_inc(freed["V"][j % 4], 1)
                    v.wait_ge(freed["V"][j % 4], v.frees(j))
                    for t in range(3):
                        e = RC * ci + RC - 1
                        ins = E.tensor_scalar(S1[:, 64 * t:64 * t + 64], S1[:, 64 * t:64 * t + 64], ec[:, t, e:e + 1], None, ALU.mult)
                    ins.then_inc(v_self, 1)
                    v.wait_ge(v_self, v.next(v_self))
                    v.eng.sem_inc(v_pe, 1)
                picks = vec_pick(v, picks, 1)
            vec_pick(v, picks, 2 * PICKS - picks)
            v.job["A"] += 4
            for t in range(3):
                j = v.take("V")
                v.wait_ge(full["V"][j % 4], v.fills(j))
                bank = banks["V"][j % 4]
                E.scalar_tensor_tensor(yr[:, t, :], bank[:, 0:T], -1.0 / 64, yr[:, t, :], ALU.mult, ALU.add).then_inc(freed["V"][j % 4], 1)
                v.wait_ge(freed["V"][j % 4], v.frees(j))
            E.tensor_tensor(Kf[:, :, :], yr[:, :, :], yr[:, :, :], ALU.mult).then_inc(v_self, 1)
            v.wait_ge(v_self, v.next(v_self))
            v.eng.sem_inc(v_pe, 1)
            for t in range(3):
                j = v.take("V")
                v.wait_ge(freed["V"][j % 4], v.frees(j))
            E.reciprocal(Bf[:, :, :], Bf[:, :, :]).then_inc(v_self, 1)
            v.wait_ge(v_self, v.next(v_self))
            E.tensor_tensor(yr[:, :, :], yr[:, :, :], Bf[:, :, :], ALU.mult).then_inc(v_self, 1)
            v.wait_ge(v_self, v.next(v_self))
            for t in range(3):
                ins = E.tensor_scalar(yr[:, t, :], yr[:, t, :], par(f"lnw_{l}", t), par(f"lnb_{l}", t), ALU.mult, ALU.add)
            ins.then_inc(v_self, 1)
            v.wait_ge(v_self, v.next(v_self))
            E.tensor_tensor(yr[:, :, :], yr[:, :, :], k_, ALU.add).then_inc(v_self, 1)
            v.wait_ge(v_self, v.next(v_self))
            E.tensor_tensor(yT[:, 0:3, 0:T], yr[:, :, :], gate[:, :, :], ALU.mult).then_inc(v_self, 1)
            v.wait_ge(v_self, v.next(v_self))
            E.sem_inc(v_a, 1)
            vec_heads(v, c_items(l), two(rtr), inr, ror)
            v.job["A"] += 7
            vec_att(v, att2(), W2)
            v.job["A"] += 3
            for h in range(4):
                j = v.take("V")
                v.wait_ge(full["V"][j % 4], v.fills(j))
                bank = banks["V"][j % 4]
                E.tensor_tensor(sT[:, h, :], bank[:, 0:384], cat["retm"][:, 384 * h:384 * h + 384], ALU.mult).then_inc(freed["V"][j % 4], 1)
                v.wait_ge(freed["V"][j % 4], v.frees(j))
            v.job["A"] += 2
            vec_heads(v, ret_norms(), two(rtr), inr, ror)
            v.wait_ge(a_v, v.next(a_v))
            E.tensor_tensor(yT[:, 6:8, 0:T], yT[:, 6:8, 0:T], sg[:, :, :], ALU.mult).then_inc(v_self, 1)
            v.wait_ge(v_self, v.next(v_self))
            v.eng.sem_inc(v_pe, 1)
            vec_out(v, T, "one")

        block = ctx.enter_context(nc.Block())

        @block.tensor
        def _(eng):
            pe = Hand(eng, plan)
            plan["writer"] = pe
            for p in "AV":
                for b in range(4):
                    eng.sem_inc(freed[p][b], 1)
            eng.wait_ge(s_par, 16 * 4)
            pe.wait_ge(v_pe, pe.next(v_pe))
            j = pe.take("V")
            pe.wait_ge(freed["V"][j % 4], pe.opens(j))
            bank = banks["V"][j % 4]
            eng.matmul(bank[:, 0:2], ones[128], small[:, 2:4], start=True, stop=True).then_inc(full["V"][j % 4], 1)

            def splits_from(pe, name):
                plan[name] = {"chunk": pe.job["chunk"], "split": pe.job["split"], "h": pe.seen[h_made] + KD}

            def ffn(n, f, side=False):
                pe_norm(pe, n)
                pe_ffn(pe, n, f, side)

            pe_mod(pe)
            ffn(TC, F1, True)
            eng.wait_ge(s_tab, 16)
            splits_from(pe, "split0")
            pe_norm(pe, TC)
            pe_mix0(pe)
            ffn(TC, F1)
            ffn(TC, F1)
            pe_norm(pe, TC)
            pe_mix1(pe)
            ffn(T, F1)
            for l in range(2):
                ffn(T, F2)
                splits_from(pe, f"split{2 + l}")
                pe_norm(pe, T)
                plan[f"mix{2 + l}"] = pe.job["A"]
                pe_mix2(pe, l)
                ffn(T, F2)
            pe_norm(pe, T)

        @block.scalar
        def _(eng):
            act = Hand(eng, plan)
            for dst, src in ((pk, "pack"), (const, "const"), (bmod, "bmod"), (cT, "cT")):
                eng.dma_start(dst[:], A[src]).then_inc(s_par, 16)
            eng.dma_start(xT[:], A["xT"]).then_inc(s_x, 16)
            eng.dma_start(shared[:, 0:sum(w for _, w in SHARED)], A["tab1"]).then_inc(s_tab, 16)
            eng.wait_ge(s_par, 16 * 4)
            act.wait_ge(v_a, act.next(v_a))
            eng.activation(small[:, 5:7], small[:, 5:7], ACT.Exp).then_inc(a_v, 1)
            eng.activation(cT[:], cT[:], ACT.Silu).then_inc(a_self, 1)
            act.wait_ge(a_self, act.next(a_self))
            eng.sem_inc(a_pe, 1)
            act_mod(act)

            def ffn(n, f, m, side=False):
                act_norm(act, n, m, split=FFN_SIDE if side else FFN)
                act_ffn(act, n, f, side)

            eng.wait_ge(s_x, 16)
            ffn(TC, F1, 1, True)
            act_norm(act, TC, 4, SPLIT0)
            act_mix0(act)
            act.stage()
            ffn(TC, F1, 7)
            ffn(TC, F1, 1)
            act_norm(act, TC, 4)
            act_mix1(act)
            act.stage()
            ffn(T, F1, 7)
            for l in range(2):
                ffn(T, F2, None)
                act_norm(act, T, None, SPLIT2[l])
                act_mix2(act, l)
                act.stage()
                ffn(T, F2, None)
            act_norm(act, T, None)

        @block.vector
        def _(eng):
            v = Hand(eng, plan)
            eng.wait_ge(s_par, 16 * 4)
            lam = par("lam", 0, 4)
            eng.tensor_tensor(small[:, 2:3], lam[:, 0:1], lam[:, 1:2], ALU.mult)
            v.eng.tensor_tensor(small[:, 3:4], lam[:, 2:3], lam[:, 3:4], ALU.mult).then_inc(v_pe, 1)
            eng.tensor_scalar(small[:, 4:5], par("sub"), 1.0 - LAM_INIT, None, ALU.mult)
            j = v.take("V")
            v.wait_ge(full["V"][j % 4], v.fills(j))
            bank = banks["V"][j % 4]
            eng.tensor_copy(small[:, 5:7], bank[:, 0:2]).then_inc(freed["V"][j % 4], 1)
            v.wait_ge(freed["V"][j % 4], v.frees(j))
            eng.sem_inc(v_a, 1)
            v.wait_ge(a_v, v.next(a_v))
            eng.tensor_tensor(small[:, 7:8], small[:, 5:6], small[:, 6:7], ALU.subtract).then_inc(v_self, 1)
            v.wait_ge(v_self, v.next(v_self))
            eng.tensor_scalar(small[:, 1:2], small[:, 7:8], LAM_INIT, -1.0, ALU.add, ALU.mult).then_inc(v_self, 1)
            v.wait_ge(v_self, v.next(v_self))
            eng.wait_ge(s_x, 16)

            def ffn(n, f, affine, gain, m, side=False):
                vec_norm(v, n, affine, gain, split=FFN_SIDE if side else FFN)
                vec_ffn(v, n, f, m, side)

            vec_mod(v)
            eng.sem_inc(x_made, KD // 2)
            ffn(TC, F1, 1, None, 2, True)
            eng.wait_ge(s_tab, 16)
            j = v.job["A"] - 5
            v.wait_ge(freed["A"][j % 4], v.frees(j))
            vec_mods(v, 0, side_mods, MOD_FIRST, N_MOD)
            eng.sem_inc(side_read, 1)
            vec_norm(v, TC, 4, split=SPLIT0)
            vec_mix0(v)
            ffn(TC, F1, 7, None, 8)
            vec_mods(v, 1, side_mods, 0, N_MOD)
            ffn(TC, F1, 1, None, 2)
            vec_norm(v, TC, 4)
            eng.sem_inc(s_biasroom, 1)
            vec_mix1(v)
            eng.sem_inc(s_room, 1)
            ffn(T, F1, 7, None, 8)
            eng.wait_ge(s_tab2, 16)
            for l in range(2):
                ffn(T, F2, None, f"n1_{l}", None)
                vec_norm(v, T, None, f"nm_{l}", SPLIT2[l])
                vec_mix2(v, l)
                ffn(T, F2, None, f"n2_{l}", None)
            vec_norm(v, T, None, "final")

        @block.gpsimd
        def _(eng):
            g = Hand(eng, plan)
            g.wait_ge(side_read, 1)
            pool_rest(g, SPLIT0, 9)
            eng.wait_ge(s_biasroom, 1)
            eng.dma_start(bias1, A["bias"]).then_inc(s_bias, 16)
            eng.wait_ge(s_room, 1)
            eng.dma_start(shared[:], A["tab2"]).then_inc(s_tab2, 16)
            for l in range(2):
                pool_rest(g, SPLIT2[l], 14)
                first = plan[f"mix{2 + l}"] + 30 + (12 if l else 9) + 6
                g.wait_ge(v_g, g.next(v_g))
                for lev in range(LEVELS):
                    if lev:
                        g.wait_ge(full["A"][(first + 3 * lev - 1) % 4], g.fills(first + 3 * lev - 1))
                    mask = cat["levelm"][:, lev * P:(lev + 1) * P]
                    for i in range(12):
                        ins = eng.tensor_tensor(NM[:, i, :], prod[:, i, 0:P], mask, ALU.mult)
                    ins.then_inc(g_pe, 1)

        @block.sync
        def _(eng):
            for s in range(WEIGHT_SLOTS):
                eng.sem_inc(used[s], 1)
            whole = n_chunks // WEIGHT_SLOTS
            with eng.Fori(0, whole) as i:
                for s in range(WEIGHT_SLOTS):
                    eng.wait_ge(used[s], i + 1)
                    eng.dma_start(ring[:, s, :], A["stream"][bass.ds(i * WEIGHT_SLOTS + s, 1), :, :].rearrange("a p f -> (a p) f"))\
                       .then_inc(landed[s], 16)
            for s in range(n_chunks - whole * WEIGHT_SLOTS):
                eng.wait_ge(used[s], whole + 1)
                eng.dma_start(ring[:, s, :], A["stream"][whole * WEIGHT_SLOTS + s, :, :]).then_inc(landed[s], 16)
            eng.wait_ge(s_vdone, 1)
            eng.dma_start(A["out"], hT[:, :, 0:T]).then_inc(s_out, 16)
            eng.wait_ge(s_out, 16)

        assert plan["writer"].job["chunk"] == n_chunks


def _feature_major(a):
    a = np.asarray(a).reshape(-1, a.shape[-1])
    c = a.shape[-1]
    out = np.zeros((a.shape[0], -(-c // P) * P), np.float32)
    out[:, :c] = a
    return np.ascontiguousarray(out.reshape(a.shape[0], -1, P).transpose(2, 1, 0))


def _twice(g):
    return np.concatenate([g] * (P // g.shape[0]))[:, None]


def _columns(chunks, w, width=CH):
    kt = w.shape[0] // P
    for c in range(0, w.shape[1], width):
        part = w[:, c:c + width]
        out = np.zeros((P, kt, width), np.float32)
        out[:, :, :part.shape[1]] = part.reshape(kt, P, -1).transpose(1, 0, 2)
        flat = np.zeros((P, CHUNK), np.float32)
        flat[:, :kt * width] = out.reshape(P, -1)
        chunks.append(flat)


def _rows(chunks, w):
    for r in range(0, w.shape[0], CH):
        out = np.zeros((2, P, D), np.float32)
        part = w[r:r + CH]
        out.reshape(-1, D)[:part.shape[0]] = part
        chunks.append(out.transpose(1, 0, 2).reshape(P, -1))


def _ffn(chunks, g, u, d, side=None):
    for s in range(0, g.shape[1], SEG):
        n = min(SEG, g.shape[1] - s)
        before = beside(n) if side else []
        for q, c in enumerate(range(s, s + n, CH)):
            for i, w in enumerate((g, u)):
                for _ in range(before[2 * q + i] if side else 0):
                    chunks.append(side.pop(0))
                _columns(chunks, w[:, c:c + CH])
        _rows(chunks, d[s:s + SEG])


def _stream(I):
    ch = []
    heads = np.arange(512).reshape(8, 64)
    for l in range(2):
        if l == 0:
            _columns(ch, I["w_mod"][0])
            side = ch[MOD_FIRST * MOD_CH:]
            del ch[MOD_FIRST * MOD_CH:]
        _ffn(ch, I["ffn1_w_gate"][l], I["ffn1_w_up"][l], I["ffn1_w_down"][l], None if l else side)
        if l == 0:
            w = I["ab_w_in"][0]
            aq, bq, ak, av, bk, bv = np.split(w, np.cumsum([512, 512, 128, 128, 512]), axis=1)
            pairs = np.concatenate([np.concatenate([heads[h], heads[h + 4]]) for h in range(4)])
            _columns(ch, np.concatenate([aq[:, pairs], bq, ak, bk, av, bv], axis=1))
            _columns(ch, I["w_mod"][1])
            _columns(ch, I["ab_w_out"][0])
        else:
            w = I["cd_w_in"][0]
            cq, dq, ckv, kr, dk, dv = np.split(w, np.cumsum([768, 512, 256, 32, 512]), axis=1)
            _columns(ch, np.concatenate([cq, dq, ckv, kr, kr, kr, kr, dk], axis=1))
            _columns(ch, dv)
            uq = I["c_w_uq"][0].reshape(768, 8, 96)
            _columns(ch, np.concatenate([uq[:, :, :64].reshape(768, 512), uq[:, :, 64:].reshape(768, 256)], axis=1))
            ukv = I["c_w_ukv"][0].reshape(256, 8, 128)
            _columns(ch, np.concatenate([ukv[:, :, :64].reshape(256, 512), ukv[:, :, 64:].reshape(256, 512)], axis=1), D)
            _columns(ch, I["cd_w_out"][0])
        _ffn(ch, I["ffn2_w_gate"][l], I["ffn2_w_up"][l], I["ffn2_w_down"][l])
    for l in range(2):
        _ffn(ch, I["ffn1_w_gate_2"][l], I["ffn1_w_up_2"][l], I["ffn1_w_down_2"][l])
        w = I["w_in_2"][l]
        rwkv, q, c, iq, ik, iw, rq, rk, rv, rg = np.split(w, np.cumsum([1280, 384, 128, 512, 64, 8, 256, 256, 256]), axis=1)
        mv = I["rwkv_vres_w_in_2"][0] if l else np.zeros((D, 16), np.float32)
        last = np.concatenate([mv, iw, np.zeros((D, P - 24), np.float32)], axis=1)
        w = np.concatenate([rwkv, q, c, iq, ik, ik, rq, rk, rg, last], axis=1)
        _columns(ch, w[:, P * (MV - 1):])
        _columns(ch, w[:, :P * (MV - 1)])
        _columns(ch, rv)
        _columns(ch, I["w_out_2"][l])
        _ffn(ch, I["ffn2_w_gate_2"][l], I["ffn2_w_up_2"][l], I["ffn2_w_down_2"][l])
    return np.stack(ch)


def _pack(I):
    PK, PW = param_layout()
    out = np.zeros((P, PW), np.float32)

    def put(name, a):
        at, w = PK[name]
        assert a.shape[1] == w, (name, a.shape, w)
        out[:a.shape[0], at:at + w] = a

    for n, key in (("a_q", "a_q_norm"), ("a_k", "a_k_norm"), ("b_q", "b_q_norm"), ("b_k", "b_k_norm"), ("sub", "b_sub_norm"),
                   ("c_qn", "c_q_nope_norm"), ("c_qr", "c_q_rope_norm"), ("c_kn", "c_k_nope_norm"), ("c_kr", "c_k_rope_norm"),
                   ("d_q", "d_q_norm"), ("d_k", "d_k_norm")):
        put(n, _twice(I[key][0]))
    put("sink", np.broadcast_to(I["a_sink"], (P, 8)))
    put("lam", np.stack([I[f"b_lambda_{n}"][0] for n in ("q1", "k1", "q2", "k2")], axis=1))
    put("c_qa", _feature_major(I["c_q_a_norm"])[:, :, 0])
    put("c_kva", _feature_major(I["c_kv_a_norm"])[:, :, 0])
    put("final", _feature_major(I["final_norm_2"][None])[:, :, 0])
    for n, value in (("one", 1.0), ("eps", EPS), ("gn_eps", GN_EPS)):
        put(n, np.full((P, 1), value, np.float32))
    for l in range(2):
        for n, key in (("n1_", "ffn1_norm_2"), ("nm_", "mix_norm_2"), ("n2_", "ffn2_norm_2"), ("mu_", "rwkv_mu_2"),
                       ("w0_", "rwkv_w0_2"), ("a0_", "rwkv_a0_2"), ("kk_", "rwkv_k_k_2"), ("ka_", "rwkv_k_a_2"),
                       ("lnw_", "rwkv_ln_w_2"), ("lnb_", "rwkv_ln_b_2"), ("kv_", "dsa_kv_norm_2")):
            put(f"{n}{l}", _feature_major(I[key][l][None])[:, :, 0])
        put(f"rk_{l}", _feature_major(I["rwkv_r_k_2"][l].reshape(1, -1))[:, :, 0])
        put(f"lora_{l}", np.concatenate([I["rwkv_w2_2"][l], I["rwkv_a2_2"][l], I["rwkv_g2_2"][l]]))
        put(f"uk_{l}", I["dsa_w_uk_2"][l].reshape(3, P, P).transpose(1, 0, 2).reshape(P, 384))
        put(f"uv_{l}", I["dsa_w_uv_2"][l].transpose(1, 0, 2).reshape(P, 384))
        if l:
            put(f"vmu_{l}", _feature_major(I["rwkv_vres_mu_2"][0][None])[:, :, 0])
            put(f"v0_{l}", _feature_major(I["rwkv_v0_2"][0][None])[:, :, 0])
            put(f"v2_{l}", I["rwkv_v2_2"][0])
    return out


def _constants():
    p = np.arange(P)
    parts = {"sel": (p[:, None] % 32 == np.arange(2)[None]) * 1.0, "ident": np.eye(P), "ones128": np.ones((P, P))}
    for g in (64, 32):
        parts[f"ones{g}"] = (p[:, None] // g == p[None] // g) * 1.0
    for h in (32, 16, 8):
        R = np.zeros((P, P))
        for i in p:
            if i % (2 * h) < h:
                R[i, i + h] = -1
            else:
                R[i, i - h] = 1
        parts[f"rot{h}"] = R.T
    return np.concatenate([parts[n] for n, _ in CONST], axis=1).astype(np.float32)


def _axial(nf):
    f32 = np.float32
    i = np.arange(P) % (4 * nf)
    inv = (f32(10000.0) ** (-np.arange(nf, dtype=f32) / f32(nf)))[i % nf]
    t = np.arange(T)
    pos = np.where((i // (2 * nf) == 0)[:, None], (t // 64)[None], (t % 64)[None]).astype(f32)
    ang = pos * inv[:, None]
    cos, sin = np.ones((P, TC), f32), np.zeros((P, TC), f32)
    cos[:, :T], sin[:, :T] = np.cos(ang), np.sin(ang)
    return cos, sin


def _tables():
    f32 = np.float32
    q, k = np.arange(T)[:, None], np.arange(T)[None]
    am = np.where(np.abs(q - k) <= 128, 0.0, NEG).reshape(2, P, T).transpose(1, 0, 2).reshape(P, -1)
    first = np.concatenate([am, *_axial(16), *_axial(8)], axis=1).astype(f32)
    i = np.arange(P) % 32
    theta = f32(10000.0) ** (-np.linspace(0.0, 1.0, 32, dtype=f32))
    ang = theta[i][:, None] * np.arange(T, dtype=f32)[None]
    gamma = np.log(1.0 - 2.0 ** (-5.0 - np.arange(4)))
    d = np.arange(T)[None] - np.arange(P)[:, None]
    one = [np.where(d >= 0, np.exp(np.maximum(d, 0) * g), 0.0) * 0.125 for g in gamma]
    retm = np.concatenate([np.concatenate([m, m[:, :P]], axis=1) for m in one], axis=1)
    s, t = np.arange(P)[:, None], np.arange(P)[None]
    same = s // RC == t // RC
    prodm = np.concatenate([same & (s < t), same & (s <= t)] * 2, axis=1) * 1.0
    levels = []
    for j in range(LEVELS):
        b = 2 << j
        levels.append((s // b == t // b) & (s % b < b // 2) & (t % b >= b // 2))
    scan = np.broadcast_to((np.arange(768) % RC != 0) * 1.0, (P, 768))
    causal = np.where(k <= q, 0.0, NEG).reshape(2, P, T).transpose(1, 0, 2).reshape(P, -1)
    second = np.concatenate([np.cos(ang), np.sin(ang), retm, prodm, np.concatenate(levels, axis=1) * 1.0, scan, causal],
                            axis=1).astype(f32)
    return first, second


def _bias(rpb):
    q, k = np.arange(T)[:, None], np.arange(T)[None]
    start = np.clip(q % 64 - 8, 0, 48)
    inside = (k % 64 >= start) & (k % 64 < start + 16)
    dr = k // 64 - q // 64 + 7
    dc = np.clip(k % 64 - q % 64, -15, 15) + 15
    out = np.full((8, T, T), NEG, np.float32)
    out[:, inside] = rpb[:, dr[inside], dc[inside]]
    return np.ascontiguousarray(out.reshape(8, 2, P, T).transpose(2, 0, 1, 3).reshape(P, 16, T))


def layout(inputs):
    I = {n: np.asarray(a) for n, a in inputs.items()}
    first, second = _tables()
    xt = np.concatenate([I["x"][0], I["ctx"][0]])
    b = [_feature_major(I["b_mod"][l][None])[:, :, 0] for l in range(2)]
    return {
        "stream": _stream(I), "pack": _pack(I), "const": _constants(), "tab1": first, "tab2": second,
        "bias": _bias(I["d_rpb"][0]), "xT": _feature_major(xt), "cT": np.pad(_feature_major(np.stack([I["c"][0], I["c_ctx"]])), ((0, 0), (0, 0), (0, 30))),
        "bmod": np.ascontiguousarray(np.repeat(np.stack(b, axis=1), 2, axis=2)),
    }


def kernel(**inputs):
    import concourse.bacc as bacc
    from concourse.bass_utils import run_bass_kernel_spmd as run

    nc = bacc.Bacc("TRN2", target_bir_lowering=False, num_devices=1)
    arrays = layout(inputs)
    A = {n: nc.dram_tensor(f"in_{n}", a.shape, F32, kind="ExternalInput").ap() for n, a in arrays.items()}
    A["out"] = nc.dram_tensor("out_0", [P, KD, T], F32, kind="ExternalOutput").ap()
    build(nc, A)
    r = run(nc, [{f"in_{n}": a for n, a in arrays.items()}], core_ids=[0])
    out = r.results[0]["out_0"]
    return np.ascontiguousarray(out.transpose(2, 1, 0).reshape(1, T, D))
```
